# Optimizing a Trainium2 kernel written in Bass

```python
import jax
import jax.numpy as jnp
from jax import lax
import numpy as np

D_MODEL = 1024
BATCH = 1
SEQ = 1024
DEPTH = 2

GRID_W = 64
CTX_LEN = 256
HEAD_DIM = 64
NA_HEADS = 6
NA_WIN_ROWS = 8
NA_WIN_COLS = 16
GQA_HEADS = 6
GQA_KV_HEADS = 2
Q_BLOCK = 128
ROPE_THETA = 10000.0
HG_HEADS = 4
HG_CHUNK = 64
LB_FLOOR = 1e-30
WA = NA_HEADS * HEAD_DIM
WB = GQA_HEADS * HEAD_DIM
WKV = GQA_KV_HEADS * HEAD_DIM
WC = HG_HEADS * HEAD_DIM
MIX_WIDTH = WA + WB + WC
COL_LAYOUT = (('a_k', WA), ('a_v', WA), ('b_k', WKV), ('b_v', WKV), ('c_f', WC), ('c_b', WC), ('c_i', WC),
              ('a_q', WA), ('b_q', WB), ('c_q', WC), ('c_g', WC))
KEY_SIDE_COLS = 2 * WA + 2 * WKV + 3 * WC
IN_COLS = KEY_SIDE_COLS + WA + WB + 2 * WC
D_FF = 2816
CONV_W = 3
N_MOD = 6
DEEPNORM_ALPHA = (2.0 * DEPTH) ** 0.25
DEEPNORM_BETA = (8.0 * DEPTH) ** -0.25
LN_EPS = 1e-6
RMS_EPS = 1e-6

kernel_name = 'hybrid_natten_gqa_hgrn2_dit_block'

def layer_norm(x, g=None, b=None):
    xf = x.astype(jnp.float32)
    mu = jnp.mean(xf, -1, keepdims=True)
    var = jnp.mean(jnp.square(xf - mu), -1, keepdims=True)
    y = (xf - mu) * lax.rsqrt(var + LN_EPS)
    if g is not None:
        y = y * g.astype(jnp.float32) + b.astype(jnp.float32)
    return y.astype(x.dtype)

def rms_norm(x, g):
    xf = x.astype(jnp.float32)
    y = xf * lax.rsqrt(jnp.mean(jnp.square(xf), -1, keepdims=True) + RMS_EPS)
    return (y * g.astype(jnp.float32)).astype(x.dtype)

def modulate(x, shift, scale):
    return layer_norm(x) * (1 + scale) + shift

def split_heads(t):
    return t.reshape(t.shape[0], t.shape[1], -1, HEAD_DIM)

def split_projection(y):
    parts, off = {}, 0
    for name, width in COL_LAYOUT:
        if off + width > y.shape[-1]:
            break
        parts[name] = split_heads(y[..., off:off + width])
        off += width
    return parts

def axial_rope_tables(n):
    t = jnp.arange(n)
    pos = jnp.stack([t // GRID_W, t % GRID_W]).astype(jnp.float32)
    n_freq = HEAD_DIM // 4
    inv_freq = ROPE_THETA ** (-jnp.arange(n_freq, dtype=jnp.float32) / n_freq)
    ang = pos[:, :, None] * inv_freq
    return jnp.cos(ang), jnp.sin(ang)

def apply_axial_rope(x, cos, sin):
    B, T, H, d = x.shape
    xs = x.reshape(B, T, H, 2, 2, d // 4)
    cos = jnp.swapaxes(cos, 0, 1)[:, None].astype(x.dtype)
    sin = jnp.swapaxes(sin, 0, 1)[:, None].astype(x.dtype)
    x1, x2 = xs[..., 0, :], xs[..., 1, :]
    out = jnp.stack([x1 * cos - x2 * sin, x2 * cos + x1 * sin], axis=-2)
    return out.reshape(B, T, H, d)

def block_attention(q, k, v):
    B, T, Hq, d = q.shape
    Hkv = k.shape[2]
    G = Hq // Hkv
    scale = d ** -0.5
    qb = q.reshape(B, T // Q_BLOCK, Q_BLOCK, Hkv, G, d).transpose(1, 0, 2, 3, 4, 5)

    def one_block(q_blk):
        s = jnp.einsum('bqkgd,bskd->bkgqs', q_blk, k).astype(jnp.float32) * scale
        p = jax.nn.softmax(s, axis=-1).astype(v.dtype)
        return jnp.einsum('bkgqs,bskd->bqkgd', p, v)

    o = lax.map(one_block, qb)
    return o.transpose(1, 0, 2, 3, 4, 5).reshape(B, T, Hq * d)

def neighbourhood_attention(q, k, v, k_ctx, v_ctx, rpb):
    B, N, H, d = q.shape
    rows = N // GRID_W
    kr = min(NA_WIN_ROWS, rows)
    kc = NA_WIN_COLS
    n_loc = kr * kc
    scale = d ** -0.5
    cols = np.arange(GRID_W)
    col_start = np.clip(cols - kc // 2, 0, GRID_W - kc)
    col_idx = (col_start[:, None] + np.arange(kc)[None, :]).astype(np.int32)
    dc_idx = (col_idx - cols[:, None] + (NA_WIN_COLS - 1)).astype(np.int32)
    kg = k.reshape(B, rows, GRID_W, H, d)
    vg = v.reshape(B, rows, GRID_W, H, d)
    qg = q.reshape(B, rows, GRID_W, H, d).transpose(1, 0, 2, 3, 4)

    def one_row(args):
        r, q_row = args
        r_start = jnp.clip(r - kr // 2, 0, rows - kr)
        k_nb = lax.dynamic_slice_in_dim(kg, r_start, kr, axis=1)[:, :, col_idx]
        v_nb = lax.dynamic_slice_in_dim(vg, r_start, kr, axis=1)[:, :, col_idx]
        dr_idx = r_start + jnp.arange(kr) - r + (NA_WIN_ROWS - 1)
        bias = rpb[:, dr_idx[:, None, None], dc_idx[None]]
        s_loc = (jnp.einsum('bwhd,brwjhd->bhwrj', q_row, k_nb).astype(jnp.float32) * scale
                 + bias.transpose(0, 2, 1, 3).astype(jnp.float32))
        s_ctx = jnp.einsum('bwhd,blhd->bhwl', q_row, k_ctx).astype(jnp.float32) * scale
        s = jnp.concatenate([s_loc.reshape(B, H, GRID_W, n_loc), s_ctx], axis=-1)
        p = jax.nn.softmax(s, axis=-1).astype(v.dtype)
        p_loc = p[..., :n_loc].reshape(B, H, GRID_W, kr, kc)
        return (jnp.einsum('bhwrj,brwjhd->bwhd', p_loc, v_nb)
                + jnp.einsum('bhwl,blhd->bwhd', p[..., n_loc:], v_ctx))

    o = lax.map(one_row, (jnp.arange(rows), qg))
    return o.transpose(1, 0, 2, 3, 4).reshape(B, N, H * d)

def forget_log(z, lb):
    lb = lb.astype(jnp.float32)
    return jnp.logaddexp(jnp.log(jnp.maximum(lb, LB_FLOOR)),
                         jnp.log1p(-lb) + jax.nn.log_sigmoid(z.astype(jnp.float32)))

def gla_chunkwise(q, k, v, logf, s0):
    B, T, H, dk = q.shape
    C = HG_CHUNK
    n = T // C

    def to_chunks(a):
        return a.reshape(B, n, C, H, a.shape[-1]).transpose(1, 0, 3, 2, 4)

    causal = jnp.tril(jnp.ones((C, C), bool))[:, :, None]

    def step(S, inp):
        qc, kc, vc, gc = inp
        b = jnp.cumsum(gc, axis=-2)
        diff = b[..., :, None, :] - b[..., None, :, :]
        decay = jnp.where(causal, jnp.exp(jnp.where(causal, diff, 0.0)), 0.0)
        att = jnp.einsum('bhtk,bhsk,bhtsk->bhts', qc, kc, decay)
        o = jnp.einsum('bhts,bhsv->bhtv', att, vc) + jnp.einsum('bhtk,bhkv->bhtv', qc * jnp.exp(b), S)
        b_last = b[..., -1:, :]
        S = S * jnp.exp(b_last[..., 0, :])[..., None] + jnp.einsum('bhsk,bhsv->bhkv', kc * jnp.exp(b_last - b), vc)
        return S, o

    S, o = lax.scan(step, s0, (to_chunks(q), to_chunks(k), to_chunks(v), to_chunks(logf)))
    o = o.transpose(1, 0, 3, 2, 4).reshape(B, T, H, v.shape[-1])
    return o.astype(v.dtype), S

def hgrn2_scan(q, v, logf, s0, reverse):
    k = -jnp.expm1(logf)
    if reverse:
        q, k, v, logf = (jnp.flip(a, axis=1) for a in (q, k, v, logf))
    o, s = gla_chunkwise(q, k, v, logf, s0)
    if reverse:
        o = jnp.flip(o, axis=1)
    return o, s

def hgrn2_final_state(v, logf, reverse):
    k = -jnp.expm1(logf)
    if reverse:
        k, v, logf = (jnp.flip(a, axis=1) for a in (k, v, logf))
    suffix = lax.cumsum(logf, axis=1, reverse=True) - logf
    return jnp.einsum('bthk,bthv->bhkv', k * jnp.exp(suffix), v)

def hgrn2_readout(o, g, gn_g):
    y = rms_norm(o, gn_g) * jax.nn.silu(g)
    return y.reshape(y.shape[0], y.shape[1], WC)

def token_mixer(h, hc, w_in, w_out, rpb, q_g, k_g, lb, gn_g, rope_cos, rope_sin, with_ctx_out):
    lat = split_projection(h @ w_in)
    ctx = split_projection(hc @ (w_in if with_ctx_out else w_in[:, :KEY_SIDE_COLS]))
    o_a = neighbourhood_attention(lat['a_q'], lat['a_k'], lat['a_v'], ctx['a_k'], ctx['a_v'], rpb)
    kc_b = rms_norm(ctx['b_k'], k_g)
    q_b = apply_axial_rope(rms_norm(lat['b_q'], q_g), rope_cos, rope_sin)
    k_b = jnp.concatenate([kc_b, apply_axial_rope(rms_norm(lat['b_k'], k_g), rope_cos, rope_sin)], axis=1)
    v_b = jnp.concatenate([ctx['b_v'], lat['b_v']], axis=1)
    o_b = block_attention(q_b, k_b, v_b)
    lb_f = lb[0].reshape(HG_HEADS, HEAD_DIM)
    lb_b = lb[1].reshape(HG_HEADS, HEAD_DIM)
    q_scale = HEAD_DIM ** -0.5
    logf_cf = forget_log(ctx['c_f'], lb_f)
    logf_cb = forget_log(ctx['c_b'], lb_b)
    if with_ctx_out:
        zero = jnp.zeros((hc.shape[0], HG_HEADS, HEAD_DIM, HEAD_DIM), jnp.float32)
        qc_c = ctx['c_q'] * q_scale
        oc_f, s_f = hgrn2_scan(qc_c, ctx['c_i'], logf_cf, zero, False)
        oc_bw, s_b = hgrn2_scan(qc_c, ctx['c_i'], logf_cb, zero, True)
    else:
        s_f = hgrn2_final_state(ctx['c_i'], logf_cf, False)
        s_b = hgrn2_final_state(ctx['c_i'], logf_cb, True)
    q_c = lat['c_q'] * q_scale
    o_f, _ = hgrn2_scan(q_c, lat['c_i'], forget_log(lat['c_f'], lb_f), s_f, False)
    o_bw, _ = hgrn2_scan(q_c, lat['c_i'], forget_log(lat['c_b'], lb_b), s_b, True)
    o_c = hgrn2_readout(o_f + o_bw, lat['c_g'], gn_g)
    y = jnp.concatenate([o_a, o_b, o_c], axis=-1) @ w_out
    if not with_ctx_out:
        return y, None
    oc_a = block_attention(ctx['a_q'], ctx['a_k'], ctx['a_v'])
    oc_b = block_attention(rms_norm(ctx['b_q'], q_g), kc_b, ctx['b_v'])
    oc_c = hgrn2_readout(oc_f + oc_bw, ctx['c_g'], gn_g)
    yc = jnp.concatenate([oc_a, oc_b, oc_c], axis=-1) @ w_out
    return y, yc

def conv_ffn(h, w_up, conv_w, conv_b, w_down):
    T = h.shape[1]
    u = h @ w_up
    up = jnp.pad(u, ((0, 0), (CONV_W // 2, CONV_W // 2), (0, 0)))
    u = sum(up[:, j:j + T] * conv_w[j] for j in range(CONV_W)) + conv_b
    gate, val = jnp.split(u, 2, axis=-1)
    return (jax.nn.silu(gate) * val) @ w_down

def setup_inputs(seed: int = 0) -> dict:
    key = jax.random.key(seed)
    ks = jax.random.split(key, 21)

    def nrm(k, shape, scale):
        return jax.random.normal(k, shape, jnp.float32) * scale

    D = D_MODEL
    return {
        'x': nrm(ks[0], (BATCH, SEQ, D), 1.0),
        'c': nrm(ks[1], (BATCH, D), 1.0),
        'ctx': nrm(ks[2], (BATCH, CTX_LEN, D), 1.0),
        'c_ctx': nrm(ks[3], (D,), 1.0),
        'w_ada': nrm(ks[4], (DEPTH, D, N_MOD * D), 0.5 * D ** -0.5),
        'b_ada': nrm(ks[5], (DEPTH, N_MOD * D), 0.02),
        'w_in': nrm(ks[6], (DEPTH, D, IN_COLS), D ** -0.5),
        'w_out': nrm(ks[7], (DEPTH, MIX_WIDTH, D), DEEPNORM_BETA * MIX_WIDTH ** -0.5),
        'na_rpb': nrm(ks[8], (DEPTH, NA_HEADS, 2 * NA_WIN_ROWS - 1, 2 * NA_WIN_COLS - 1), 0.1),
        'q_norm': 1.0 + nrm(ks[9], (DEPTH, HEAD_DIM), 0.02),
        'k_norm': 1.0 + nrm(ks[10], (DEPTH, HEAD_DIM), 0.02),
        'hg_lower_bound': 1.0 + nrm(ks[11], (DEPTH, 2, WC), 0.1),
        'hg_norm': 1.0 + nrm(ks[12], (DEPTH, HEAD_DIM), 0.02),
        'ln1_g': 1.0 + nrm(ks[13], (DEPTH, D), 0.02),
        'ln1_b': nrm(ks[14], (DEPTH, D), 0.02),
        'w_up': nrm(ks[15], (DEPTH, D, 2 * D_FF), D ** -0.5),
        'conv_w': nrm(ks[16], (DEPTH, CONV_W, 2 * D_FF), CONV_W ** -0.5),
        'conv_b': nrm(ks[17], (DEPTH, 2 * D_FF), 0.02),
        'w_down': nrm(ks[18], (DEPTH, D_FF, D), DEEPNORM_BETA * D_FF ** -0.5),
        'ln2_g': 1.0 + nrm(ks[19], (DEPTH, D), 0.02),
        'ln2_b': nrm(ks[20], (DEPTH, D), 0.02),
    }

def reference(x, c, ctx, c_ctx, w_ada, b_ada, w_in, w_out, na_rpb, q_norm, k_norm, hg_lower_bound, hg_norm,
              ln1_g, ln1_b, w_up, conv_w, conv_b, w_down, ln2_g, ln2_b):
    s_c = jax.nn.silu(c)
    s_cc = jax.nn.silu(c_ctx)
    lb = jax.nn.softmax(hg_lower_bound.astype(jnp.float32), axis=0)
    lb = jnp.cumsum(lb, axis=0) - lb[0]
    rope_cos, rope_sin = axial_rope_tables(x.shape[1])
    xc = ctx
    for l in range(DEPTH):
        last = l == DEPTH - 1
        mod = jnp.split((s_c @ w_ada[l] + b_ada[l])[:, None, :], N_MOD, axis=-1)
        n_ctx_mod = 2 if last else N_MOD
        mod_c = jnp.split(s_cc @ w_ada[l, :, :n_ctx_mod * D_MODEL] + b_ada[l, :n_ctx_mod * D_MODEL],
                          n_ctx_mod, axis=-1)
        h = modulate(x, mod[0], mod[1])
        hc = modulate(xc, mod_c[0], mod_c[1])
        y, yc = token_mixer(h, hc, w_in[l], w_out[l], na_rpb[l], q_norm[l], k_norm[l], lb[l], hg_norm[l],
                            rope_cos, rope_sin, not last)
        x = layer_norm(DEEPNORM_ALPHA * x + mod[2] * y, ln1_g[l], ln1_b[l])
        f = conv_ffn(modulate(x, mod[3], mod[4]), w_up[l], conv_w[l], conv_b[l], w_down[l])
        x = layer_norm(DEEPNORM_ALPHA * x + mod[5] * f, ln2_g[l], ln2_b[l])
        if not last:
            xc = layer_norm(DEEPNORM_ALPHA * xc + mod_c[2] * yc, ln1_g[l], ln1_b[l])
            fc = conv_ffn(modulate(xc, mod_c[3], mod_c[4]), w_up[l], conv_w[l], conv_b[l], w_down[l])
            xc = layer_norm(DEEPNORM_ALPHA * xc + mod_c[5] * fc, ln2_g[l], ln2_b[l])
    return x


_drawn_inputs = setup_inputs


def setup_inputs(seed=0):
    import zlib

    import numpy as np

    out = dict(_drawn_inputs(seed))
    spreads = {}
    factors = {'ctx': 6.899,
     'c_ctx': 3.063,
     'b_ada': 5.545,
     'na_rpb': 64.0,
     'q_norm': 23.527,
     'k_norm': 21.982,
     'hg_lower_bound': 8.0,
     'hg_norm': 51.434,
     'conv_b': 8.0}
    for name, (base, spread) in spreads.items():
        noise = np.random.default_rng([zlib.crc32(name.encode()), seed]).standard_normal(out[name].shape)
        drawn = base * np.exp(spread * noise) if base else spread * noise
        out[name] = jnp.asarray(drawn.astype(out[name].dtype))
    for name, factor in factors.items():
        out[name] = (out[name] * factor).astype(out[name].dtype)
    return out
```

```python
from contextlib import ExitStack

import concourse.bass as bass
from concourse import mybir

P = 128
D = 1024
KT = D // P
LAT, CTX = 1024, 256
T = LAT + CTX
NT, NTL = T // P, LAT // P
DEPTH = 2
GRID_W, ROWS = 64, LAT // 64
WIN_R, WIN_C = 8, 16
HD = 64
HG_COLS = 256
D_FF = 2816
FT = D_FF // P
NPAIR = FT // 2
N_MOD = 6
MODS = N_MOD * KT
ALPHA = (2.0 * DEPTH) ** 0.25
EPS = 1e-6
LB_FLOOR = 1e-30
QSCALE = HD ** -0.5
LN_SHIFT = 40
LN2 = 0.6931471805599453
COL = dict(a_k=0, a_v=384, b_k=768, b_v=896, c_f=1024, c_b=1280, c_i=1536, a_q=1792, b_q=2176, c_q=2560, c_g=2816)
GROUPS = [(0, 512), (512, 512), (1024, 256)]
LEVELS = [1, 2, 4, 8, 16, 32, 64]
PAD_W = 128
N_RPB = 15
RPB_ROWS = 6 * N_RPB
ROW_PAIRS = []
for _p in range(ROWS // 2):
    _s = [min(max(r - WIN_R // 2, 0), ROWS - WIN_R) for r in (2 * _p, 2 * _p + 1)]
    _n = _s[1] + WIN_R - _s[0]
    ROW_PAIRS.append((_s[0], _n, 14 if _n > WIN_R else _s[0] - 2 * _p + 6))
BIAS_BLOCKS = 14 + 9
B_PARTS = [("k", COL["b_k"]), ("v", COL["b_v"])] + [(f"q{j}", COL["b_q"] + P * j) for j in range(3)]
B_NORMED = ["k", "q0", "q1", "q2"]
C_PARTS = [(f"{x}{j}", COL["c_" + x] + P * j) for x in "igfbq" for j in range(2)]
C_TURNED = ("i0", "i1", "g0", "g1")
ADA_CHUNKS = N_MOD * D // 512
N_CONSTS = 6 + DEPTH
N_ROWS = 4 * DEPTH + 7
ARENA = 206 * 1024
CHUNK_GROUPS = [(0, 4), (4, 4), (8, 2)]


def q_tiles(l):
    return NT if l < DEPTH - 1 else NTL


def next_h(l, which):
    if which == 0:
        return ("h2", l)
    return ("h", l + 1) if l < DEPTH - 1 else None

F32 = mybir.dt.float32
F32R = mybir.dt.float32r
U8 = mybir.dt.uint8
ALU = mybir.AluOpType
ACT = mybir.ActivationFunctionType
AX = mybir.AxisListType.X
LN_EXP_SET = "natural_log_exp_and_others"


class Signal:

    def __init__(self, sem):
        self.sem, self.n = sem, 0

    def on(self, instruction, by=1):
        instruction.then_inc(self.sem, by)
        self.n += by
        return self.sem, self.n


class Plan:

    def __init__(self):
        self.use, self.tile, self.tiles, self.tile_last = {}, {}, [], []
        for i in range(NT):
            self.slot("h", 0, i)
        for l in range(DEPTH):
            nq = q_tiles(l)
            for r in range(3):
                for name in "qkv":
                    self.gemm(("in", l, COL["a_" + name] + P * r), ("A", l, r, name))
                self.slot("A", l, r, "vt")
                for hh in range(2):
                    self.slot("A", l, r, "bias", hh)
                for u in range(2 * nq):
                    self.slot("A", l, r, u)
            for name, col in B_PARTS:
                self.gemm(("in", l, col), ("B", l, name))
            self.slot("B", l, "vt")
            for name in B_NORMED:
                self.slot("B", l, name, "ms")
                self.slot("B", l, name, "rot")
            self.slot("B", l, "ks")
            for u in range(6 * nq):
                self.slot("B", l, u)
            for name, col in C_PARTS:
                self.gemm(("in", l, col), ("C", l, name))
                if name in C_TURNED:
                    self.slot("C", l, name, "t")
            for j in range(4):
                self.slot("C", l, "kd", j)
                self.slot("C", l, "D", j)
            for lev in range(len(LEVELS) + 1):
                for tile in range(2):
                    for q in range(len(CHUNK_GROUPS)):
                        self.slot("C", l, "att", lev, tile, q)
            for i in range(nq):
                self.slot("O", l, i)
            for m in range(KT):
                self.gemm(("out", l, m), ("W", l, m))
            self.post(l, 0, nq)
            for i in range(NPAIR + 1):
                if i < NPAIR:
                    for f in (2 * i, 2 * i + 1):
                        for half in range(2):
                            self.gemm(("up", l, f, half), ("F", l, f, half))
                if i:
                    for q in range(2):
                        self.gemm(("down", l, i - 1, q), *[("Y", l, i - 1, m) for m in range(4 * q, 4 * q + 4)])
            self.post(l, 1, nq)

    def post(self, l, which, n):
        for i in range(n + 2):
            if i < n:
                self.slot("y", l, which, i)
            if i >= 2 and next_h(l, which):
                self.slot(*next_h(l, which), i - 2)

    def slot(self, *key):
        assert key not in self.use, key
        self.use[key] = len(self.use)

    def gemm(self, tile, *uses):
        self.tile[tile] = len(self.tiles)
        self.tiles.append(tile)
        for key in uses:
            self.slot(*key)
        self.tile_last.append(uses[-1])

    def events(self):
        e = {k: [] for k in ("stat", "xh", "unit", "bn", "hg", "lev", "levx", "chunk", "osplit", "post", "conv", "ff")}
        for i in range(NT):
            e["stat"].append(("h", 0, i))
            e["xh"].append(("h", 0, i))
        for l in range(DEPTH):
            nq = q_tiles(l)
            e["unit"] += [("A", l, r, u) for r in range(3) for u in range(2 * nq)]
            e["unit"] += [("B", l, u) for u in range(6 * nq)]
            e["bn"] += [(l, name) for name in B_NORMED]
            e["hg"] += [(l, j) for j in range(4)]
            e["lev"] += [(l, lev, tile) for lev in range(len(LEVELS) + 1) for tile in range(2)]
            e["levx"] += [(l, lev, tile) for lev in range(len(LEVELS)) for tile in range(2)]
            e["chunk"] += [(l, i) for i in range(nq)]
            e["osplit"] += [(l, i) for i in range(nq)]
            e["conv"] += [(l, f, half) for f in range(FT) for half in range(2)]
            e["ff"] += [(l, f) for f in range(FT)]
            for which in range(2):
                after = next_h(l, which)
                for i in range(nq + 1):
                    if i < nq:
                        e["stat"].append(("y", l, which, i))
                        e["post"].append((l, which, i))
                    if i and after:
                        e["stat"].append((*after, i - 1))
                if after:
                    e["xh"] += [(*after, i) for i in range(nq)]
        return e


def spread(row):
    return bass.AP(tensor=row.tensor, offset=row.offset, ap=[[0, P], *row.ap])


def build(nc, x, c, ctx, c_ctx, w_ada, b_ada, w_in, w_out, na_rpb, q_norm, k_norm, hg_lower_bound, hg_norm,
          ln1_g, ln1_b, w_up, conv_w, conv_b, w_down, ln2_g, ln2_b,
          identity, reverse_columns, rotate_halves, swap_heads, head_means, level_masks, rope_cos, rope_sin, window_mask, out, dump=None):
    plan = Plan()
    events = plan.events()
    ordinal = {kind: {key: n + 1 for n, key in enumerate(keys)} for kind, keys in events.items()}
    XH = events["xh"]

    def nth(kind, *key):
        return ordinal[kind][key]

    with ExitStack() as stack:
        top_before = nc.sbuf_base
        arena = stack.enter_context(nc.sbuf_tensor("arena", [P, ARENA // 4], F32))
        ARENA_AT = nc.sbuf_base - ARENA
        psum = stack.enter_context(nc.psum_tensor("psum", [P, 8, 512], F32))
        top = [0]

        def place(name, shape, offset, dtype=F32):
            size = mybir.dt.size(dtype)
            for n in shape:
                size *= n
            assert offset + size <= ARENA, (name, offset + size)
            top[0] = max(top[0], offset + size)
            return nc.alloc_sbuf_tensor_at(name, [P, *shape], dtype, offset=ARENA_AT + offset)

        H, O, W = 0, 8 * KT * T, 12 * KT * T
        G = W + 6 * KT * P * 4
        C = G + 51200

        h_hi = place("h_hi", [KT, T], H, F32R)
        h_lo = place("h_lo", [KT, T], H + 4 * KT * T, F32R)
        o_tok = place("o_tok", [NT, D], O)
        y_chan = place("y_chan", [KT, T], O)
        w_raw = place("w_raw", [2, KT * P], W)
        w_hi = place("w_hi", [2, KT * P], W + 8 * KT * P, F32R)
        w_lo = place("w_lo", [2, KT * P], W + 16 * KT * P, F32R)

        at = [C]

        def keep(name, shape, dtype=F32):
            t = place(name, shape, at[0], dtype)
            size = mybir.dt.size(dtype)
            for n in shape:
                size *= n
            at[0] += (size + 31) // 32 * 32
            return t

        ident = keep("ident", [P])
        flip = keep("flip", [P])
        rot = keep("rot", [P])
        swap = keep("swap", [P])
        means = keep("means", [P])
        ones = keep("ones", [P])
        masks = keep("masks", [len(LEVELS) + 1, P], U8)
        vec = keep("vec", [2 * 224 + 8])
        mods = keep("mods", [DEPTH, MODS, 2])
        head_g = keep("head_g", [2, DEPTH])
        hgn = keep("hgn", [DEPTH, HD])
        cond = keep("cond", [KT, 2])
        lb = keep("lb", [4, 8])
        stats = keep("stats", [4, 64])
        bn = keep("bn", [NT, 12])
        mv = keep("mv", [2, NT, 2])
        rstd = keep("rstd", [2, NT])

        def g(name, shape, at_float, dtype=F32):
            return place(name, shape, G + 4 * at_float, dtype)

        rows = g("rows", [14, P], 0)
        pad_rows = g("pad_rows", [DEPTH, PAD_W], 14 * P)
        masks_in = g("masks_in", [len(LEVELS) + 1, P], (14 + 2) * P)
        ada = place("ada", [4, KT, 512], H)

        n_xt = g("n_xt", [2, D], 0)
        n_xh = g("n_xh", [2, D], 2 * D)
        n_t = g("n_t", [2, KT, P], 4 * D)
        n_r = g("n_r", [2, D], 6 * D)
        n_x1 = g("n_x1", [2, D], 8 * D)
        n_g = g("n_g", [D], 10 * D)
        n_b = g("n_b", [D], 11 * D)

        a_q = g("a_q", [T], 0)
        a_k = g("a_k", [T], T)
        a_v = g("a_v", [NT, P], 2 * T)
        a_bias = g("a_bias", [2, BIAS_BLOCKS * 64], 3 * T)
        a_mask = g("a_mask", [BIAS_BLOCKS * 64], 3 * T + 2 * BIAS_BLOCKS * 64)
        a_at = 3 * T + 3 * BIAS_BLOCKS * 64
        a_p = g("a_p", [2, 832], a_at)
        a_pt = g("a_pt", [2, 7, P], a_at + 2 * 832)
        a_vt = g("a_vt", [T], a_at + 2 * 832)

        b_q = g("b_q", [3, T], 0)
        b_k = g("b_k", [T], 3 * T)
        b_ks = g("b_ks", [T], 4 * T)
        b_v = g("b_v", [NT, P], 5 * T)
        b_cos = g("b_cos", [LAT], 6 * T)
        b_sin = g("b_sin", [LAT], 6 * T + LAT)
        b_tmp = g("b_tmp", [T], 6 * T + 2 * LAT)
        b_vt = g("b_vt", [T], 7 * T + 2 * LAT)
        b_p = g("b_p", [2, T], 6 * T)
        b_pt = g("b_pt", [2, NT, P], 8 * T)

        c_z = g("c_z", [4, T], 0)
        c_state = g("c_state", [4, NT, HD], 0)
        c_q = g("c_q", [2, T], 4 * T)
        c_v = g("c_v", [NT, 2 * P], 6 * T)
        c_g = g("c_g", [NT, 2 * P], 8 * T)
        c_b = place("c_b", [4, T], H)
        c_k = place("c_k", [4, T], H + 16 * T)
        c_lq = place("c_lq", [2, T], H + 32 * T)
        c_lk = place("c_lk", [2, T], H + 40 * T)
        c_w = place("c_w", [2, 4, T], H + 32 * T)
        c_att = place("c_att", [NT, 4, P], H + 48 * T)
        c_el = keep("c_el", [4, NT])
        c_o = g("c_o", [2, 2 * P], 2 * T)
        c_o2 = g("c_o2", [2, 2 * P], 2 * T + 4 * P)
        c_ms = keep("c_ms", [2, NT, 4])

        f_hi = g("f_hi", [2, 2, T], 0, F32R)
        f_lo = g("f_lo", [2, 2, T], 4 * T, F32R)
        f_t = g("f_t", [2, T], 8 * T)

        pads = nc.dram_tensor("pads", (DEPTH, RPB_ROWS, PAD_W), F32, kind="Internal").ap()
        x_mid = [[nc.dram_tensor(f"x_mid{l}{w}", (T, D), F32, kind="Internal").ap() for w in range(2)]
                 for l in range(DEPTH)]

        def sem(name):
            return stack.enter_context(nc.semaphore(name))

        s = {}
        for name in (
            "const_landed", "rows_landed", "pads_stored", "cond_ready", "rows_turned", "vec_ready",
            "ada_landed0", "ada_landed1", "ada_landed2", "ada_landed3", "ada_used", "lb_shifted", "lb_exps",
            "lb_args", "lb_logs", "phase_end",
            "w_landed0", "w_landed1", "w_hi_done", "w_ready",
            "full0", "full1", "freed0", "freed1",
            "x_landed0", "x_landed1", "ln_landed", "mean_ready", "rstd_ready", "xh_ready", "h_ready",
            "mean2_ready", "rstd2_ready", "x1_ready", "x1_stored0", "x1_stored1",
            "bias_landed", "scores_ready", "negmax_ready", "probs_ready", "out_ready", "out_freed",
            "sq_ready", "act_headrstd", "headnorm_ready", "rope_ready", "rope_landed",
            "gate_l", "gate_m", "gate_k", "b_ready", "el_args", "el_ready", "kd_ready", "states_ready",
            "lev_args", "lev_exps", "lev_ready", "att_done", "inter_exps", "inter_ready",
            "ms_ready", "hg_rstd", "c_out_ready", "c_out_freed", "silu_g", "o_hi_ready", "h_split",
            "conv_start", "conv_done", "silu_done", "a_ready", "w_unused",
            "pe_step", "act_step", "dve_step", "pool_step", "sp_done",
        ):
            s[name] = sem(name)

        def full(*key):
            n = plan.use[key]
            return s[f"full{n % 2}"], n // 2 + 1

        def freed(*key):
            n = plan.use[key]
            return s[f"freed{n % 2}"], n // 2 + 1

        def slot(*key):
            n = plan.use[key] % 2
            return psum[:, 3 * n:3 * n + 3, :].rearrange("p b n -> p (b n)")

        def before(*key):
            n = plan.use[key]
            return (s[f"freed{n % 2}"], n // 2) if n >= 2 else None

        def groups(l):
            return GROUPS if q_tiles(l) == NT else GROUPS[:2]

        phases = []
        for l in range(DEPTH):
            phases += [("A", l, 0), ("A", l, 1), ("A", l, 2), ("B", l), ("C", l), ("O", l), ("post", l, 0), ("F", l),
                       ("post", l, 1)]
        phases = [("setup",), ("h0",)] + phases
        PHASE = {key: n for n, key in enumerate(phases)}

        def phase_entered(*key):
            return s["phase_end"], 3 * PHASE[key]

        def n_bias_loads(l, r):
            return 8 * (3 * l + r + 1) + l + 1

        def end_phase(eng, last, *key):
            eng.wait_ge(*last)
            eng.sem_inc(s["phase_end"], 1)
            eng.wait_ge(s["phase_end"], 3 * (PHASE[key] + 1))

        block = stack.enter_context(nc.Block())

        @block.sync
        def _(sp):
            consts = Signal(s["const_landed"])
            for dst, src in ((ident, identity), (flip, reverse_columns), (rot, rotate_halves), (swap, swap_heads), (means, head_means)):
                consts.on(sp.dma_start(dst[:], src), 16)
            consts.on(sp.dma_start(masks_in[:], level_masks), 16)
            for l in range(DEPTH):
                consts.on(sp.dma_start(hgn[:, l, :], spread(hg_norm[l])), 16)
            assert consts.n == 16 * N_CONSTS
            rows_in = Signal(s["rows_landed"])
            for l in range(DEPTH):
                rows_in.on(sp.dma_start(rows[0:MODS, 5 * l, :], b_ada[l].rearrange("(m p) -> m p", p=P)), 16)
                rows_in.on(sp.dma_start(rows[0:2 * FT, 5 * l + 1:5 * l + 4, :],
                                        conv_w[l].rearrange("j (m p) -> m j p", p=P)), 16)
                rows_in.on(sp.dma_start(rows[0:2 * FT, 5 * l + 4, :], conv_b[l].rearrange("(m p) -> m p", p=P)), 16)
            rows_in.on(sp.dma_start(rows[0:8, 10, :], hg_lower_bound.rearrange("l d (m p) -> (l d m) p", p=P)), 16)
            for a, vector in enumerate((c[0], c_ctx)):
                rows_in.on(sp.dma_start(rows[0:KT, 11 + a, :], vector.rearrange("(k p) -> k p", p=P)), 16)
            for n, gain in enumerate((q_norm, k_norm)):
                for half in range(2):
                    rows_in.on(sp.dma_start(rows[DEPTH * n:DEPTH * (n + 1), 13, HD * half:HD * (half + 1)], gain), 16)
            sp.wait_ge(s["pool_step"], 1)
            for l in range(DEPTH):
                rows_in.on(sp.dma_start(pad_rows[0:RPB_ROWS, l, 48:79], na_rpb[l].rearrange("h a b -> (h a) b")), 16)
            sp.wait_ge(s["rows_landed"], rows_in.n)
            assert rows_in.n == 16 * N_ROWS
            pads_out = Signal(s["pads_stored"])
            pads_out.on(sp.dma_start(pads.rearrange("l r n -> r l n"), pad_rows[0:RPB_ROWS]), 16)

            def load_weights(n):
                kind, l, a, *b = plan.tiles[n]
                if kind == "in":
                    src = w_in[l].rearrange("(k p) n -> p k n", p=P)[:, :, a:a + P]
                elif kind == "out":
                    src = w_out[l].rearrange("(k p) n -> p k n", p=P)[:, :, P * a:P * a + P]
                elif kind == "up":
                    at_col = P * a + D_FF * b[0]
                    src = w_up[l].rearrange("(k p) n -> p k n", p=P)[:, :, at_col:at_col + P]
                else:
                    src = w_down[l][2 * P * a:2 * P * (a + 1)].rearrange("(k p) n -> p k n", p=P)[
                        :, :, 512 * b[0]:512 * (b[0] + 1)]
                if n >= 2:
                    sp.wait_ge(s["w_ready"], n - 1)
                sp.dma_start(w_raw[:, n % 2].rearrange("p (k n) -> p k n", k=src.shape[1]), src)\
                  .then_inc(s[f"w_landed{n % 2}"], 16)

            sent = [0]

            def weights_up_to(*tile):
                end = plan.tile[tile] + 1
                for n in range(sent[0], end):
                    load_weights(n)
                sent[0] = max(sent[0], end)

            weights_up_to("in", 0, COL["a_k"])
            for n in range(DEPTH * ADA_CHUNKS):
                if n >= 4:
                    sp.wait_ge(s["ada_used"], n - 3)
                src = w_ada[n // ADA_CHUNKS].rearrange("(k p) n -> p k n", p=P)[
                    :, :, 512 * (n % ADA_CHUNKS):512 * (n % ADA_CHUNKS + 1)]
                sp.dma_start(ada[:, n % 4], src).then_inc(s[f"ada_landed{n % 4}"], 16)

            x_in = [Signal(s["x_landed0"]), Signal(s["x_landed1"])]
            n_in = [0]

            def load_x(src, i):
                x_in[n_in[0] % 2].on(sp.dma_start(n_xt[:, n_in[0] % 2, :], src), 16)
                n_in[0] += 1

            def source(l, which, i):
                if (l, which) == (0, 0):
                    return x[0, P * i:P * i + P, :] if i < NTL else ctx[0, P * (i - NTL):P * (i - NTL) + P, :]
                before_ = x_mid[l][0] if which else x_mid[l - 1][1]
                return before_[P * i:P * i + P, :]

            sp.wait_ge(*phase_entered("h0"))
            for i in range(NT):
                if i >= 2:
                    sp.wait_ge(s["xh_ready"], i - 1)
                load_x(source(0, 0, i), i)

            bias_in = Signal(s["bias_landed"])
            ln_in = Signal(s["ln_landed"])
            rope_in = Signal(s["rope_landed"])
            x_out = [Signal(s["x1_stored0"]), Signal(s["x1_stored1"])]
            n_post = 0
            for l in range(DEPTH):
                for r in range(3):
                    weights_up_to("in", l, COL["a_v"] + P * r)
                    sp.wait_ge(*phase_entered("A", l, r))
                    if r == 0:
                        bias_in.on(sp.dma_start(a_mask[:], window_mask), 16)
                        if l == 0:
                            sp.wait_ge(s["pads_stored"], pads_out.n)
                    for hh in range(2):
                        row = (l * 6 + 2 * r + hh) * N_RPB
                        table = a_bias[:, hh].rearrange("p (b n) -> p b n", n=64)
                        for half, first, blocks, at_block in ((0, 1, 14, 0), (1, 0, 14, 0), (0, 3, 9, 14), (1, 2, 9, 14)):
                            src = bass.AP(tensor=pads.tensor, offset=(row + first) * PAD_W,
                                          ap=[[1, 64], [PAD_W, blocks], [1, 64]])
                            bias_in.on(sp.dma_start(table[64 * half:64 * half + 64, at_block:at_block + blocks, :],
                                                    src), 16)
                weights_up_to("in", l, B_PARTS[-1][1])
                sp.wait_ge(*phase_entered("B", l))
                rope_in.on(sp.dma_start(b_cos[:], rope_cos), 16)
                rope_in.on(sp.dma_start(b_sin[:], rope_sin), 16)
                weights_up_to("in", l, C_PARTS[-1][1])
                weights_up_to("out", l, KT - 1)
                for which in range(2):
                    if which:
                        weights_up_to("down", l, NPAIR - 1, 1)
                    sp.wait_ge(*phase_entered("post", l, which))
                    gain, shift = (ln2_g, ln2_b) if which else (ln1_g, ln1_b)
                    ln_in.on(sp.dma_start(n_g[:], spread(gain[l])), 16)
                    ln_in.on(sp.dma_start(n_b[:], spread(shift[l])), 16)
                    last = next_h(l, which) is None
                    dst = out[0] if last else x_mid[l][which]
                    nq = q_tiles(l)
                    for i in range(nq + 1):
                        if i < nq:
                            if i >= 2:
                                sp.wait_ge(*freed("y", l, which, i - 2))
                            if not (l == 0 and which == 0) and i == 0:
                                for k in range(2):
                                    sp.wait_ge(x_out[k].sem, x_out[k].n)
                            load_x(source(l, which, i), i)
                        if i >= 1:
                            sp.wait_ge(s["x1_ready"], n_post + 1)
                            x_out[n_post % 2].on(sp.dma_start(dst[P * (i - 1):P * i, :], n_x1[:, n_post % 2, :]), 16)
                            n_post += 1
            for k in range(2):
                sp.wait_ge(x_out[k].sem, x_out[k].n)

        @block.gpsimd
        def _(pool):
            pool.memset(pad_rows[:], 0.0).then_inc(s["pool_step"], 1)
            for n in range(len(plan.tiles)):
                pool.wait_ge(s[f"w_landed{n % 2}"], 16 * (n // 2 + 1))
                if n >= 2:
                    pool.wait_ge(*full(*plan.tile_last[n - 2]))
                pool.tensor_copy(w_hi[:, n % 2], w_raw[:, n % 2]).then_inc(s["w_hi_done"], 1)
                pool.wait_ge(s["w_hi_done"], n + 1)
                pool.tensor_tensor(w_lo[:, n % 2], w_raw[:, n % 2], w_hi[:, n % 2].bitcast(F32), ALU.subtract)\
                    .then_inc(s["w_ready"], 1)

        @block.tensor
        def _(pe):
            def wait(token):
                if token is not None and token[1] > 0:
                    pe.wait_ge(*token)

            def fill(ins, *key):
                ins.then_inc(s[f"full{plan.use[key] % 2}"], 1)
                return full(*key)

            def turn(out_ap, in_ap, rows_=P):
                return pe.transpose(out_ap, in_ap, ident[0:rows_, 0:rows_])

            def gemm(tile, key, parts, kt=KT, col=0, x_hi=h_hi, x_lo=h_lo):
                n = plan.tile[tile]
                wait((s["w_ready"], n + 1))
                wait(before(*key))
                acc = slot(*key)
                halves = ((w_hi, x_hi), (w_hi, x_lo), (w_lo, x_hi))
                for k in range(kt):
                    for j, (w, a) in enumerate(halves):
                        weight = w[:, n % 2].rearrange("p (k n) -> p k n", k=kt)[:, k, col:col + P]
                        for t0, tn in parts:
                            last = pe.matmul(acc[:, t0:t0 + tn], weight, a[:, k, t0:t0 + tn],
                                             start=(k == 0 and j == 0), stop=(k == kt - 1 and j == 2))
                return fill(last, *key)

            wait((s["const_landed"], 16 * N_CONSTS))
            wait((s["rows_landed"], 16 * N_ROWS))
            for l in range(DEPTH):
                turn(psum[:, 6, 224 * l:224 * l + MODS], rows[0:MODS, 5 * l, :], MODS)
                for j in range(4):
                    at_col = 224 * l + MODS + 2 * FT * j
                    turn(psum[:, 6, at_col:at_col + 2 * FT], rows[0:2 * FT, 5 * l + 1 + j, :], 2 * FT)
            turn(psum[:, 6, 448:456], rows[0:8, 10, :], 8)
            for a in range(2):
                turn(psum[:, 6, 456 + KT * a:456 + KT * (a + 1)], rows[0:KT, 11 + a, :], KT)
            turn(psum[:, 6, 472:476], rows[0:2 * DEPTH, 13, :], 2 * DEPTH).then_inc(s["rows_turned"], 1)
            wait((s["cond_ready"], 1))
            for n in range(DEPTH * ADA_CHUNKS):
                wait((s[f"ada_landed{n % 4}"], 16 * (n // 4 + 1)))
                for m in range(4):
                    at_col = 8 * n + 2 * m
                    for k in range(KT):
                        last = pe.matmul(psum[:, 7, at_col:at_col + 2], ada[:, n % 4, k, P * m:P * m + P],
                                         cond[:, k, :], start=(k == 0), stop=(k == KT - 1))
                last.then_inc(s["ada_used"], 1)
            end_phase(pe, (s["ada_used"], DEPTH * ADA_CHUNKS), "setup")

            def turn_normed(key):
                wait((s["xh_ready"], nth("xh", *key)))
                wait(before(*key))
                acc = slot(*key)
                for k in range(KT):
                    last = turn(acc[:, P * k:P * k + P], n_xh[:, nth("xh", *key) % 2, P * k:P * k + P])
                return fill(last, *key)

            for i in range(NT):
                last = turn_normed(("h", 0, i))
            end_phase(pe, last, "h0")

            def attend_pv(unit_key, blocks):
                u = nth("unit", *unit_key)
                wait(freed(*unit_key))
                if u > 2:
                    wait((s["out_freed"], u - 2))
                for n, (probs, values) in enumerate(blocks):
                    last = pe.matmul(psum[:, 6 + u % 2, 0:HD], probs, values, start=(n == 0),
                                     stop=(n == len(blocks) - 1))
                last.then_inc(s["out_ready"], 1)

            def phase_a(l, r):
                wait((s["h_ready"], nth("xh", "h", l, NT - 1)))
                for name in "qkv":
                    gemm(("in", l, COL["a_" + name] + P * r), ("A", l, r, name),
                         groups(l) if name == "q" else GROUPS)
                key = ("A", l, r, "vt")
                wait(freed("A", l, r, "v"))
                wait(before(*key))
                for i in range(NT):
                    last = turn(slot(*key)[:, P * i:P * i + P], a_vt[:, P * i:P * i + P])
                fill(last, *key)
                wait((s["bias_landed"], 16 * n_bias_loads(l, r)))
                for hh in range(2):
                    key = ("A", l, r, "bias", hh)
                    wait(before(*key))
                    for t0 in range(0, BIAS_BLOCKS * 64, 512):
                        t1 = min(t0 + 512, BIAS_BLOCKS * 64)
                        last = pe.matmul(slot(*key)[:, t0:t1], flip[:], a_bias[:, hh, t0:t1], start=True, stop=True)
                    fill(last, *key)
                nq = q_tiles(l)
                units = [(hh, p) for hh in range(2) for p in range(nq)]

                def scores(u):
                    hh, p = units[u]
                    rows_ = slice(HD * hh, HD * hh + HD)
                    key = ("A", l, r, u)
                    if u == 0:
                        for name in "qk":
                            wait(freed("A", l, r, name))
                    wait(before(*key))
                    acc = slot(*key)
                    q = a_q[rows_, P * p:P * p + P]
                    if p < NTL:
                        start, n, _ = ROW_PAIRS[p]
                        pe.matmul(acc[:, 0:512], q, a_k[rows_, 64 * start:64 * start + 512], start=True, stop=True)
                        if n > WIN_R:
                            pe.matmul(acc[:, 512:576], q, a_k[rows_, 64 * (start + 8):64 * (start + 9)],
                                      start=True, stop=True)
                    last = pe.matmul(acc[:, 576:832], q, a_k[rows_, LAT:T], start=True, stop=True)
                    last.then_inc(s["scores_ready"], 1)

                def turn_probs(u):
                    hh, p = units[u]
                    key = ("A", l, r, u)
                    n_unit = nth("unit", *key)
                    wait((s["probs_ready"], n_unit))
                    acc = slot(*key)
                    src = a_p[:, n_unit % 2]
                    last = None
                    if p < NTL:
                        for b in range(4):
                            turn(acc[:, P * b:P * b + P], src[:, P * b:P * b + P])
                    for b in range(2):
                        last = turn(acc[:, P * (4 + b):P * (5 + b)], src[:, 576 + P * b:576 + P * b + P])
                    if p < NTL and ROW_PAIRS[p][1] > WIN_R:
                        last = pe.transpose(acc[0:64, P * 6:P * 7], src[:, 512:576], ident[:])
                    fill(last, *key)

                def values(u):
                    hh, p = units[u]
                    key = ("A", l, r, u)
                    if u == 0:
                        wait(freed("A", l, r, "vt"))
                    pt = a_pt[:, nth("unit", *key) % 2]
                    cols = slice(HD * hh, HD * hh + HD)
                    blocks = [(pt[:, 4 + b, :], a_v[:, NTL + b, cols]) for b in range(2)]
                    if p < NTL:
                        start, n, _ = ROW_PAIRS[p]
                        blocks += [(pt[:, b, :], a_v[:, start // 2 + b, cols]) for b in range(4)]
                        if n > WIN_R:
                            blocks.append((pt[0:64, 6, :], a_v[0:64, start // 2 + 4, cols]))
                    attend_pv(key, blocks)

                scores(0)
                for u in range(len(units) + 1):
                    if u + 1 < len(units):
                        scores(u + 1)
                    if u < len(units):
                        turn_probs(u)
                    if u >= 1:
                        values(u - 1)
                return s["out_ready"], nth("unit", "A", l, r, len(units) - 1)

            def phase_b(l):
                for name, col in B_PARTS:
                    gemm(("in", l, col), ("B", l, name), groups(l) if name[0] == "q" else GROUPS)
                key = ("B", l, "vt")
                wait(freed("B", l, "v"))
                wait(before(*key))
                for i in range(NT):
                    last = turn(slot(*key)[:, P * i:P * i + P], b_vt[:, P * i:P * i + P])
                fill(last, *key)
                for name in B_NORMED:
                    key = ("B", l, name, "ms")
                    n = nth("bn", l, name)
                    wait((s["sq_ready"], n))
                    wait(before(*key))
                    for t0, tn in (GROUPS if name == "k" else groups(l)):
                        last = pe.matmul(slot(*key)[:, t0:t0 + tn], means[:], b_tmp[:, t0:t0 + tn],
                                         start=True, stop=True)
                    fill(last, *key)
                    key = ("B", l, name, "rot")
                    src = b_k[:] if name == "k" else b_q[:, int(name[1])]
                    wait((s["headnorm_ready"], n))
                    wait(before(*key))
                    for t0, tn in GROUPS[:2]:
                        last = pe.matmul(slot(*key)[:, t0:t0 + tn], rot[:], src[:, t0:t0 + tn], start=True, stop=True)
                    fill(last, *key)
                key = ("B", l, "ks")
                wait((s["rope_ready"], nth("bn", l, "k")))
                wait(before(*key))
                for t0, tn in GROUPS:
                    last = pe.matmul(slot(*key)[:, t0:t0 + tn], swap[:], b_k[:, t0:t0 + tn], start=True, stop=True)
                fill(last, *key)
                nq = q_tiles(l)
                units = [(h, i) for h in range(6) for i in range(nq)]

                def scores(u):
                    h, i = units[u]
                    kv, base = h // 3, HD * (h % 2)
                    key = ("B", l, u)
                    if u == 0:
                        wait((s["rope_ready"], nth("bn", l, "q2")))
                        wait(freed("B", l, "ks"))
                    wait(before(*key))
                    acc = slot(*key)
                    k = (b_k if kv == h % 2 else b_ks)
                    for t0, tn in (GROUPS if i < NTL else GROUPS[2:]):
                        last = pe.matmul(acc[:, t0:t0 + tn], b_q[base:base + HD, h // 2, P * i:P * i + P],
                                         k[base:base + HD, t0:t0 + tn], start=True, stop=True)
                    last.then_inc(s["scores_ready"], 1)

                def turn_probs(u):
                    h, i = units[u]
                    key = ("B", l, u)
                    n_unit = nth("unit", *key)
                    wait((s["probs_ready"], n_unit))
                    for b in range(0 if i < NTL else NTL, NT):
                        last = turn(slot(*key)[:, P * b:P * b + P], b_p[:, n_unit % 2, P * b:P * b + P])
                    fill(last, *key)

                def values(u):
                    h, i = units[u]
                    key = ("B", l, u)
                    pt = b_pt[:, nth("unit", *key) % 2]
                    cols = slice(HD * (h // 3), HD * (h // 3) + HD)
                    attend_pv(key, [(pt[:, b, :], b_v[:, b, cols]) for b in range(0 if i < NTL else NTL, NT)])

                scores(0)
                for u in range(len(units) + 1):
                    if u + 1 < len(units):
                        scores(u + 1)
                    if u < len(units):
                        turn_probs(u)
                    if u >= 1:
                        values(u - 1)
                return s["out_ready"], nth("unit", "B", l, len(units) - 1)

            def phase_c(l):
                def turn_part(name):
                    key = ("C", l, name, "t")
                    wait(freed("C", l, name))
                    wait(before(*key))
                    for i in range(NT):
                        last = turn(slot(*key)[:, P * i:P * i + P], c_z[:, 2 + int(name[1]), P * i:P * i + P])
                    fill(last, *key)

                for name, col in C_PARTS:
                    gemm(("in", l, col), ("C", l, name), GROUPS)
                    if name in C_TURNED:
                        turn_part(name)
                for j in range(4):
                    key = ("C", l, "kd", j)
                    wait((s["kd_ready"], nth("hg", l, j)))
                    wait(before(*key))
                    for i in range(NT):
                        last = turn(slot(*key)[:, P * i:P * i + P], c_w[:, j % 2, 0, P * i:P * i + P])
                    fill(last, *key)
                    wait(freed(*key))
                    key = ("C", l, "D", j)
                    wait(before(*key))
                    kd = c_w[:, j % 2, 1].rearrange("p (c k) -> p c k", k=P)
                    for i in range(NT):
                        for par in range(2):
                            at_col = P * (j % 2) + HD * par
                            last = pe.matmul(slot(*key)[HD * par:HD * par + HD, HD * i:HD * i + HD],
                                             kd[:, i, HD * par:HD * par + HD], c_v[:, i, at_col:at_col + HD],
                                             start=True, stop=True)
                    fill(last, *key)
                for lev in range(len(LEVELS) + 1):
                    diag = lev == len(LEVELS)
                    for tile in range(2):
                        wait((s["lev_ready"], nth("lev", l, lev, tile)))
                        for q, (c0, cn) in enumerate(CHUNK_GROUPS):
                            key = ("C", l, "att", lev, tile, q)
                            wait(before(*key))
                            acc = slot(*key)
                            for par in range(2):
                                rows_ = slice(HD * par, HD * par + HD)
                                for n in range(cn):
                                    t = slice(P * (c0 + n), P * (c0 + n) + P)
                                    qs = c_q[rows_, tile, t] if diag else c_lq[rows_, tile, t]
                                    last = pe.matmul(acc[:, 512 * par + P * n:512 * par + P * n + P],
                                                     c_lk[rows_, tile, t], qs, start=True, stop=True)
                            fill(last, *key)
                for n, i in enumerate(range(q_tiles(l))):
                    if n == 0:
                        wait(freed("C", l, "att", len(LEVELS), 1, len(CHUNK_GROUPS) - 1))
                        wait((s["inter_ready"], 4 * (l + 1)))
                        wait((s["states_ready"], 4 * (l + 1)))
                    done = nth("chunk", l, i)
                    if done > 1:
                        wait((s["c_out_freed"], done - 1))
                    for tile in range(2):
                        for par in range(2):
                            h = 2 * tile + par
                            dst = psum[:, 6 + par, HD * tile:HD * tile + HD]
                            rows_ = slice(HD * par, HD * par + HD)
                            pe.matmul(dst, c_att[:, i, h, :], c_v[:, i, HD * h:HD * h + HD], start=True, stop=False)
                            for way in range(2):
                                last = pe.matmul(dst, c_b[rows_, 2 * way + tile, P * i:P * i + P],
                                                 c_state[rows_, 2 * way + tile, i, :], start=False, stop=(way == 1))
                    last.then_inc(s["c_out_ready"], 1)
                return s["c_out_ready"], nth("chunk", l, q_tiles(l) - 1)

            def phase_o(l):
                for i in range(q_tiles(l)):
                    key = ("O", l, i)
                    wait(before(*key))
                    for k in range(KT):
                        last = turn(slot(*key)[:, P * k:P * k + P], o_tok[:, i, P * k:P * k + P])
                    fill(last, *key)
                for i in range(q_tiles(l) - 2, q_tiles(l)):
                    wait(freed("O", l, i))
                for m in range(KT):
                    last = gemm(("out", l, m), ("W", l, m), groups(l))
                return last

            def phase_post(l, which):
                nq = q_tiles(l)
                for i in range(nq + 2):
                    if i < nq:
                        key = ("y", l, which, i)
                        wait(before(*key))
                        for k in range(KT):
                            last = turn(slot(*key)[:, P * k:P * k + P], y_chan[:, k, P * i:P * i + P])
                        last = fill(last, *key)
                    if i >= 2 and next_h(l, which):
                        last = turn_normed((*next_h(l, which), i - 2))
                return last

            def phase_f(l):
                wait((s["h_ready"], nth("xh", "h2", l, q_tiles(l) - 1)))
                for i in range(NPAIR + 1):
                    if i < NPAIR:
                        for f in (2 * i, 2 * i + 1):
                            for half in range(2):
                                gemm(("up", l, f, half), ("F", l, f, half), groups(l))
                    if i:
                        wait((s["a_ready"], nth("ff", l, 2 * i - 1)))
                        for q in range(2):
                            for m in range(4 * q, 4 * q + 4):
                                last = gemm(("down", l, i - 1, q), ("Y", l, i - 1, m), groups(l), kt=2,
                                            col=P * (m % 4), x_hi=f_hi[:, (i - 1) % 2], x_lo=f_lo[:, (i - 1) % 2])
                return last

            for l in range(DEPTH):
                for r in range(3):
                    end_phase(pe, phase_a(l, r), "A", l, r)
                end_phase(pe, phase_b(l), "B", l)
                end_phase(pe, phase_c(l), "C", l)
                end_phase(pe, phase_o(l), "O", l)
                end_phase(pe, phase_post(l, 0), "post", l, 0)
                end_phase(pe, phase_f(l), "F", l)
                end_phase(pe, phase_post(l, 1), "post", l, 1)

        def blocks_of(ap, h):
            v = ap.rearrange("p (n a h) -> p n a h", a=2, h=h)
            return v[:, :, 0, :], v[:, :, 1, :]

        @block.vector
        def _(dve):
            own = Signal(s["dve_step"])

            def step(ins):
                token = own.on(ins)
                dve.wait_ge(*token)
                return token

            def also(ins):
                return own.on(ins)

            def release(ins, *key):
                ins.then_inc(s[f"freed{plan.use[key] % 2}"], 1)
                return freed(*key)

            def say(name, ins):
                ins.then_inc(s[name], 1)

            step(dve.memset(ones[:], 1.0))
            dve.wait_ge(s["const_landed"], 16 * N_CONSTS)
            also(dve.tensor_copy(masks[:], masks_in[:]))
            dve.wait_ge(s["cond_ready"], 1)
            also(dve.tensor_scalar(head_g[:, 0, :], psum[:, 6, 472:474], QSCALE, None, ALU.mult))
            also(dve.tensor_copy(head_g[:, 1, :], psum[:, 6, 474:476]))
            step(dve.tensor_copy(vec[:], psum[:, 6, 0:456]))
            top_ = stats[:, 0, 0:4]
            step(dve.tensor_tensor(top_, vec[:, 448:452], vec[:, 452:456], ALU.max))
            for l in range(2):
                ins = dve.tensor_tensor(lb[:, 0, 4 * l:4 * l + 4], vec[:, 448 + 4 * l:452 + 4 * l], top_, ALU.subtract)
                say("lb_shifted", ins)
            dve.wait_ge(s["lb_exps"], 1)
            step(dve.tensor_tensor(stats[:, 0, 4:8], lb[:, 0, 0:4], lb[:, 0, 4:8], ALU.add))
            step(dve.reciprocal(stats[:, 0, 8:12], stats[:, 0, 4:8]))
            for l in range(2):
                step(dve.tensor_tensor(lb[:, 0, 4 * l:4 * l + 4], lb[:, 0, 4 * l:4 * l + 4], stats[:, 0, 8:12], ALU.mult))
            step(dve.tensor_tensor(stats[:, 0, 12:16], lb[:, 0, 0:4], lb[:, 0, 4:8], ALU.add))
            step(dve.tensor_tensor(lb[:, 0, 4:8], stats[:, 0, 12:16], lb[:, 0, 0:4], ALU.subtract))
            step(dve.tensor_tensor(lb[:, 0, 0:4], lb[:, 0, 0:4], lb[:, 0, 0:4], ALU.subtract))
            step(dve.tensor_scalar(lb[:, 1], lb[:, 0], LB_FLOOR, None, ALU.max))
            step(dve.tensor_scalar(lb[:, 2], lb[:, 0], -1.0, 1.0, ALU.mult, ALU.add))
            say("lb_args", dve.tensor_scalar(lb[:, 2], lb[:, 2], 1e-19, None, ALU.max))
            dve.wait_ge(s["lb_logs"], 1)
            step(dve.tensor_scalar(lb[:, 1], lb[:, 1], -LN_SHIFT * LN2, None, ALU.add))
            step(dve.tensor_tensor(lb[:, 3], lb[:, 2], lb[:, 1], ALU.subtract))
            dve.wait_ge(s["ada_used"], DEPTH * ADA_CHUNKS)
            for l in range(DEPTH):
                step(dve.tensor_tensor(mods[:, l], psum[:, 7, 2 * MODS * l:2 * MODS * (l + 1)].rearrange(
                    "p (m a) -> p m a", a=2), vec[:, 224 * l:224 * l + MODS].unsqueeze(2).broadcast_to([P, MODS, 2]),
                    ALU.add))
                for i in (1, 4):
                    last = step(dve.tensor_scalar(mods[:, l, KT * i:KT * i + KT], mods[:, l, KT * i:KT * i + KT], 1.0,
                                                  None, ALU.add))
            end_phase(dve, last, "setup")

            def moments(x_ap, key):
                n = nth("stat", *key)
                i = (n - 1) % NT
                w = (n - 1) // NT % 2
                for half in range(2):
                    tok = also(dve.bn_stats(bn[:, i, 6 * half:6 * half + 6], x_ap[:, 512 * half:512 * half + 512]))
                dve.wait_ge(*tok)
                say("mean_ready", dve.bn_aggr(mv[:, w, i, :], bn[:, i, :]))

            def mean_of(key):
                n = nth("stat", *key)
                return mv[:, (n - 1) // NT % 2, (n - 1) % NT, 0:1], rstd[:, (n - 1) // NT % 2, (n - 1) % NT:(n - 1) % NT + 1]

            def normed(dst, src, key):
                mean, r = mean_of(key)
                dve.wait_ge(s["mean_ready"], nth("stat", *key))
                dve.wait_ge(s["rstd_ready"], nth("stat", *key))
                return dve.tensor_scalar(dst, src, mean, r, ALU.subtract, ALU.mult)

            def normed_for_pe(src, key):
                n = nth("xh", *key)
                if n > 2:
                    dve.wait_ge(*full(*XH[n - 3]))
                    dve.wait_ge(s["xh_ready"], n - 2)
                say("xh_ready", normed(n_xh[:, n % 2], src, key))

            def split(key):
                n = nth("xh", *key)
                i = key[-1]
                dve.wait_ge(*freed(*key))
                t = slice(P * i, P * i + P)
                step(dve.tensor_copy(h_hi[:, :, t], n_t[:, n % 2]))
                say("h_ready", dve.tensor_tensor(h_lo[:, :, t], n_t[:, n % 2], h_hi[:, :, t].bitcast(F32), ALU.subtract))

            for i in range(NT + 2):
                if i < NT:
                    dve.wait_ge(s[f"x_landed{i % 2}"], 16 * (i // 2 + 1))
                    moments(n_xt[:, i % 2], ("h", 0, i))
                if 1 <= i <= NT:
                    normed_for_pe(n_xt[:, (i - 1) % 2], ("h", 0, i - 1))
                if i >= 2:
                    split(("h", 0, i - 2))
            end_phase(dve, (s["h_ready"], nth("xh", "h", 0, NT - 1)), "h0")

            def attend(l, units, key_of, negmax, out_of):
                def reciprocal_of_sum(u):
                    n = nth("unit", *key_of(u))
                    dve.wait_ge(s["probs_ready"], n)
                    c_ = n % 64
                    step(dve.tensor_tensor(stats[:, 2, c_:c_ + 1], stats[:, 2, c_:c_ + 1], stats[:, 3, c_:c_ + 1], ALU.add))
                    return also(dve.reciprocal(stats[:, 2, c_:c_ + 1], stats[:, 2, c_:c_ + 1]))

                def output(u):
                    n = nth("unit", *key_of(u))
                    c_ = n % 64
                    dve.wait_ge(s["out_ready"], n)
                    dve.wait_ge(*sums[u])
                    say("out_freed", dve.tensor_scalar(out_of(u), psum[:, 6 + n % 2, 0:HD], stats[:, 2, c_:c_ + 1],
                                                       None, ALU.mult))
                sums = {}
                for u in range(len(units) + 2):
                    if u < len(units):
                        negmax(u)
                    if 1 <= u <= len(units):
                        sums[u - 1] = reciprocal_of_sum(u - 1)
                    if u >= 2:
                        output(u - 2)
                return s["out_freed"], nth("unit", *key_of(len(units) - 1))

            def phase_a(l, r):
                for hh in range(2):
                    key = ("A", l, r, "bias", hh)
                    dve.wait_ge(*full(*key))
                    dve.wait_ge(*release(dve.tensor_tensor(a_bias[:, hh], slot(*key)[:, 0:BIAS_BLOCKS * 64], a_mask[:],
                                                           ALU.add), *key))
                units = [(hh, p) for hh in range(2) for p in range(q_tiles(l))]

                def key_of(u):
                    return ("A", l, r, u)

                def negmax(u):
                    hh, p = units[u]
                    n = nth("unit", *key_of(u))
                    c_ = n % 64
                    acc = slot(*key_of(u))
                    dve.wait_ge(s["scores_ready"], n)
                    if p < NTL:
                        if u >= 2:
                            dve.wait_ge(*full(*key_of(u - 2)))
                        _, rows_, block_ = ROW_PAIRS[p]
                        w = 64 * rows_
                        also(dve.tensor_tensor_reduce(
                            out=a_p[:, n % 2, 0:w], in0=acc[:, 0:w], in1=a_bias[:, hh, 64 * block_:64 * block_ + w],
                            scale=1.0, scalar=-3e38, op0=ALU.add, op1=ALU.max, accum_out=stats[:, 0, c_:c_ + 1]))
                        step(dve.tensor_reduce(stats[:, 1, c_:c_ + 1], acc[:, 576:832], AX, ALU.max))
                        say("negmax_ready", dve.tensor_scalar(stats[:, 1, c_:c_ + 1], stats[:, 1, c_:c_ + 1],
                                                              stats[:, 0, c_:c_ + 1], -1.0, ALU.max, ALU.mult))
                    else:
                        say("negmax_ready", dve.tensor_reduce(stats[:, 1, c_:c_ + 1], acc[:, 576:832], AX, ALU.max,
                                                              negate=True))

                def out_of(u):
                    hh, p = units[u]
                    return o_tok[:, p, HD * (2 * r + hh):HD * (2 * r + hh) + HD]
                return attend(l, units, key_of, negmax, out_of)

            def phase_b(l):
                for name in B_NORMED:
                    src = b_k[:] if name == "k" else b_q[:, int(name[1])]
                    w = T if name == "k" or q_tiles(l) == NT else LAT
                    n = nth("bn", l, name)
                    dve.wait_ge(*freed("B", l, name))
                    dve.wait_ge(s["act_headrstd"], n)
                    gain = head_g[:, int(name == "k"), l:l + 1]
                    say("headnorm_ready", dve.scalar_tensor_tensor(out=src[:, 0:w], in0=src[:, 0:w], scalar=gain,
                                                                   in1=b_tmp[:, 0:w], op0=ALU.mult, op1=ALU.mult))
                    dve.wait_ge(s["headnorm_ready"], n)
                    if name == "k":
                        dve.wait_ge(s["rope_landed"], 32 * (l + 1))
                    step(dve.tensor_tensor(b_tmp[:, 0:LAT], src[:, 0:LAT], b_cos[:], ALU.mult))
                    dve.wait_ge(*full("B", l, name, "rot"))
                    dve.wait_ge(*release(dve.tensor_tensor(src[:, 0:LAT], slot("B", l, name, "rot")[:, 0:LAT], b_sin[:],
                                                           ALU.mult), "B", l, name, "rot"))
                    say("rope_ready", dve.tensor_tensor(src[:, 0:LAT], src[:, 0:LAT], b_tmp[:, 0:LAT], ALU.add))
                units = [(h, i) for h in range(6) for i in range(q_tiles(l))]

                def key_of(u):
                    return ("B", l, u)

                def negmax(u):
                    h, i = units[u]
                    n = nth("unit", *key_of(u))
                    c_ = n % 64
                    dve.wait_ge(s["scores_ready"], n)
                    if i < NTL:
                        keys = slot(*key_of(u))[:, 0:T]
                    else:
                        keys = slot(*key_of(u))[:, LAT:T]
                    say("negmax_ready", dve.tensor_reduce(stats[:, 1, c_:c_ + 1], keys, AX, ALU.max, negate=True))

                def out_of(u):
                    h, i = units[u]
                    return o_tok[:, i, HD * (6 + h):HD * (7 + h)]
                return attend(l, units, key_of, negmax, out_of)

            def phase_c(l):
                dve.wait_ge(*freed("C", l, "q1"))
                dve.wait_ge(*freed("C", l, "q0"))

                def gates_1(j):
                    dve.wait_ge(s["gate_l"], nth("hg", l, j))
                    w = c_w[:, j % 2]
                    also(dve.scalar_tensor_tensor(out=w[:, 1], in0=c_z[:, j], scalar=0.0, in1=w[:, 0], op0=ALU.min,
                                                  op1=ALU.subtract))
                    say("gate_m", dve.scalar_tensor_tensor(out=w[:, 2], in0=c_z[:, j], scalar=0.0, in1=w[:, 0],
                                                           op0=ALU.max, op1=ALU.add))

                def gates_2(j):
                    w = c_w[:, j % 2]
                    way = j // 2
                    dve.wait_ge(s["gate_k"], nth("hg", l, j))
                    step(dve.tensor_scalar(w[:, 1], w[:, 1], lb[:, 2, 4 * l + j:4 * l + j + 1],
                                           lb[:, 1, 4 * l + j:4 * l + j + 1], ALU.add, ALU.max))
                    step(dve.tensor_tensor(c_z[:, j], w[:, 1], w[:, 3], ALU.add))
                    for i in range(NT):
                        src, dst = c_z[:, j, P * i:P * i + P], c_b[:, j, P * i:P * i + P]
                        if way:
                            src, dst = src[:, ::-1], dst[:, ::-1]
                        ins = dve.tensor_tensor_scan(dst, ones[:], src, 0.0, ALU.mult, ALU.add)
                        also(ins) if i < NT - 1 else say("b_ready", ins)

                gates_1(0)
                for j in range(4):
                    if j < 3:
                        gates_1(j + 1)
                    gates_2(j)

                def chunks(ap):
                    return ap.rearrange("p (c t) -> p c t", t=P)

                def end_of(j):
                    return chunks(c_b[:, j])[:, :, P - 1:P] if j < 2 else chunks(c_b[:, j])[:, :, 0:1]

                def to_end(j):
                    dve.wait_ge(s["b_ready"], nth("hg", l, 3))
                    if j >= 2:
                        dve.wait_ge(*full("C", l, "kd", j - 2))
                    w = chunks(c_w[:, j % 2, 0])
                    say("el_args", dve.tensor_tensor(w, end_of(j).broadcast_to([P, NT, P]), chunks(c_b[:, j]),
                                                     ALU.subtract))
                    dve.wait_ge(s["el_ready"], nth("hg", l, j))
                    say("kd_ready", dve.tensor_tensor(c_w[:, j % 2, 0], c_w[:, j % 2, 0], c_k[:, j], ALU.mult))

                def states(j):
                    order = [8, 9] + list(range(8)) if j < 2 else list(range(9, -1, -1))
                    step(dve.memset(c_state[:, j, order[0], :], 0.0))
                    dve.wait_ge(*full("C", l, "D", j))
                    for now, then in zip(order[:-1], order[1:]):
                        ins = dve.scalar_tensor_tensor(
                            out=c_state[:, j, then, :], in0=c_state[:, j, now, :], scalar=c_el[:, j, now:now + 1],
                            in1=slot("C", l, "D", j)[:, HD * now:HD * now + HD], op0=ALU.mult, op1=ALU.add)
                        if then != order[-1]:
                            step(ins)
                        else:
                            token = release(ins, "C", l, "D", j)
                    dve.wait_ge(*token)
                    dve.sem_inc(s["states_ready"], 1)

                for j in range(5):
                    if j < 4:
                        to_end(j)
                    if j >= 1:
                        states(j - 1)

                levels = [(lev, tile) for lev in range(len(LEVELS) + 1) for tile in range(2)]

                def level_args(n):
                    lev, tile = levels[n]
                    if n >= 2:
                        dve.wait_ge(*full("C", l, "att", lev - 1, tile, len(CHUNK_GROUPS) - 1))
                    else:
                        for j in (2, 3):
                            dve.wait_ge(*full("C", l, "D", j))
                    if lev == len(LEVELS):
                        return
                    h = LEVELS[lev]
                    bf1, bf2 = blocks_of(c_b[:, tile], h)
                    bb1, bb2 = blocks_of(c_b[:, 2 + tile], h)
                    q1, q2 = blocks_of(c_lq[:, tile], h)
                    k1, k2 = blocks_of(c_lk[:, tile], h)
                    shape = [P, T // (2 * h), h]
                    mid_f = bf1[:, :, h - 1:h].broadcast_to(shape)
                    mid_b = bb2[:, :, 0:1].broadcast_to(shape)
                    also(dve.tensor_tensor(q2, bf2, mid_f, ALU.subtract))
                    also(dve.tensor_tensor(q1, bb1, mid_b, ALU.subtract))
                    also(dve.tensor_tensor(k1, mid_f, bf1, ALU.subtract))
                    say("lev_args", dve.tensor_tensor(k2, mid_b, bb2, ALU.subtract))

                def level_operands(n):
                    lev, tile = levels[n]
                    if lev == len(LEVELS):
                        say("lev_ready", dve.tensor_tensor(c_lk[:, tile], c_k[:, tile], c_k[:, 2 + tile], ALU.add))
                        return
                    h = LEVELS[lev]
                    dve.wait_ge(s["lev_exps"], nth("levx", l, lev, tile))
                    k1, k2 = blocks_of(c_lk[:, tile], h)
                    kf1, _ = blocks_of(c_k[:, tile], h)
                    _, kb2 = blocks_of(c_k[:, 2 + tile], h)
                    also(dve.tensor_tensor(k1, k1, kf1, ALU.mult))
                    also(dve.tensor_tensor(k2, k2, kb2, ALU.mult))
                    say("lev_ready", dve.tensor_tensor(c_lq[:, tile], c_lq[:, tile], c_q[:, tile], ALU.mult))

                def level_masked(n):
                    lev, tile = levels[n]
                    for q, (c0, cn) in enumerate(CHUNK_GROUPS):
                        key = ("C", l, "att", lev, tile, q)
                        dve.wait_ge(*full(*key))
                        if lev:
                            dve.wait_ge(*freed("C", l, "att", lev - 1, tile, q))
                        src = slot(*key)[:, 0:1024].rearrange("p (h c t) -> p h c t", h=2, t=P)[:, :, 0:cn, :]
                        dst = c_att[:, c0:c0 + cn, 2 * tile:2 * tile + 2, :].rearrange("p c h t -> p h c t")
                        mask = masks[:, lev, :].unsqueeze(1).unsqueeze(1).broadcast_to([P, 2, cn, P])
                        release(dve.copy_predicated(out=dst, mask=mask, data=src), *key)

                for n in range(len(levels) + 1):
                    if n < len(levels):
                        level_args(n)
                    if n >= 1:
                        level_masked(n - 1)
                    if n < len(levels):
                        level_operands(n)
                for j in range(4):
                    dve.wait_ge(s["inter_exps"], nth("hg", l, j))
                    say("inter_ready", dve.tensor_tensor(c_b[:, j], c_b[:, j], c_q[:, j % 2], ALU.mult))
                gated = step(dve.tensor_tensor(
                    c_g[:].rearrange("p c (h v) -> p (c h) v", v=HD), c_g[:].rearrange("p c (h v) -> p (c h) v", v=HD),
                    hgn[:, l, :].unsqueeze(1).broadcast_to([P, 4 * NT, HD]), ALU.mult))

                def read_out(i):
                    n = nth("chunk", l, i)
                    dve.wait_ge(s["c_out_ready"], n)
                    say("c_out_freed", dve.tensor_copy(
                        c_o[:, n % 2].rearrange("p (t a v) -> p a t v", a=2, v=HD),
                        psum[:, 6:8, 0:P].rearrange("p a (t v) -> p a t v", v=HD)))
                    dve.wait_ge(s["c_out_freed"], n)
                    step(dve.tensor_tensor(c_o2[:, n % 2], c_o[:, n % 2], c_o[:, n % 2], ALU.mult))
                    say("ms_ready", dve.tensor_reduce(c_ms[:, 0, i, :], c_o2[:, n % 2].rearrange(
                        "p (h v) -> p h v", v=HD), AX, ALU.add))
                    dve.wait_ge(s["ms_ready"], n)

                def gate_out(i):
                    n = nth("chunk", l, i)
                    dve.wait_ge(s["hg_rstd"], n)
                    step(dve.tensor_tensor(
                        c_o2[:, n % 2].rearrange("p (h v) -> p h v", v=HD), c_o[:, n % 2].rearrange(
                            "p (h v) -> p h v", v=HD),
                        c_ms[:, 1, i, :].unsqueeze(2).broadcast_to([P, 4, HD]), ALU.mult))
                    return also(dve.tensor_tensor(o_tok[:, i, D - 2 * P:D], c_o2[:, n % 2], c_g[:, i, :], ALU.mult))

                nq = q_tiles(l)
                for i in range(nq + 1):
                    if i < nq:
                        read_out(i)
                    if i >= 1:
                        last = gate_out(i - 1)
                        dve.wait_ge(*last)
                return last

            def phase_o(l):
                for i in range(q_tiles(l)):
                    dve.wait_ge(s["o_hi_ready"], nth("osplit", l, i))
                    t = slice(P * i, P * i + P)
                    last = release(dve.tensor_tensor(
                        h_lo[:, :, t], slot("O", l, i)[:, 0:D].rearrange("p (k n) -> p k n", n=P),
                        h_hi[:, :, t].bitcast(F32), ALU.subtract), "O", l, i)
                return last

            def phase_post(l, which):
                nq = q_tiles(l)
                after = next_h(l, which)
                last = None
                dve.wait_ge(s["ln_landed"], 32 * (2 * l + which + 1))

                def post(i):
                    return nth("post", l, which, i)

                for i in range(nq + 4):
                    if i < nq:
                        n = post(i)
                        key = ("y", l, which, i)
                        k = NT + n - 1
                        dve.wait_ge(s[f"x_landed{k % 2}"], 16 * (k // 2 + 1))
                        dve.wait_ge(*full(*key))
                        if i >= 2:
                            dve.wait_ge(s["x1_ready"], n - 2)
                        dve.wait_ge(*release(dve.scalar_tensor_tensor(
                            out=n_r[:, n % 2], in0=n_xt[:, k % 2], scalar=ALPHA, in1=slot(*key)[:, 0:D],
                            op0=ALU.mult, op1=ALU.add), *key))
                        moments(n_r[:, n % 2], key)
                    if 1 <= i <= nq:
                        n = post(i - 1)
                        r = n_r[:, n % 2]
                        step(normed(r, r, ("y", l, which, i - 1)))
                        step(dve.tensor_tensor(r, r, n_g[:], ALU.mult))
                        if n > 2:
                            dve.wait_ge(s[f"x1_stored{(n - 1) % 2}"], 16 * ((n - 1) // 2))
                        if after and i >= 3:
                            dve.wait_ge(s["xh_ready"], nth("xh", *after, i - 3))
                        say("x1_ready", dve.tensor_tensor(n_x1[:, (n - 1) % 2], r, n_b[:], ALU.add))
                        dve.wait_ge(s["x1_ready"], n)
                        if after:
                            moments(n_x1[:, (n - 1) % 2], (*after, i - 1))
                    if after and 2 <= i <= nq + 1:
                        n = post(i - 2)
                        normed_for_pe(n_x1[:, (n - 1) % 2], (*after, i - 2))
                    if after and i >= 4:
                        split((*after, i - 4))
                for k in range(2):
                    n = sum(1 for m in range(post(nq - 1)) if m % 2 == k)
                    dve.wait_ge(s[f"x1_stored{k}"], 16 * n)
                if after:
                    return s["h_ready"], nth("xh", *after, nq - 1)
                return s["x1_ready"], post(nq - 1)

            def phase_f(l):
                ctx_too = q_tiles(l) == NT

                def conv(f, half):
                    key = ("F", l, f, half)
                    w = f_t[:, half]
                    acc = slot(*key)
                    dve.wait_ge(s["conv_start"], nth("conv", l, f, half))
                    parts = [(0, LAT)] + [(LAT, T)] * ctx_too
                    for j in (0, 2):
                        at_col = 224 * l + MODS + 2 * FT * j + FT * half + f
                        for a, b in parts:
                            dst, src = (w[:, a + 1:b], acc[:, a:b - 1]) if j == 0 else (w[:, a:b - 1], acc[:, a + 1:b])
                            ins = dve.scalar_tensor_tensor(out=dst, in0=src, scalar=vec[:, at_col:at_col + 1], in1=dst,
                                                           op0=ALU.mult, op1=ALU.add)
                            if (j, b) == (2, parts[-1][1]):
                                dve.wait_ge(*release(ins, *key))
                            elif b == parts[-1][1]:
                                step(ins)
                            else:
                                also(ins)

                w = T if ctx_too else LAT
                for i in range(NPAIR + 1):
                    if i < NPAIR:
                        for f in (2 * i, 2 * i + 1):
                            conv(f, 0)
                            conv(f, 1)
                            dve.wait_ge(s["silu_done"], nth("ff", l, f))
                            step(dve.tensor_tensor(f_t[:, 0, 0:w], f_t[:, 0, 0:w], f_t[:, 1, 0:w], ALU.mult))
                            hi, lo = f_hi[:, i % 2, f % 2, 0:w], f_lo[:, i % 2, f % 2, 0:w]
                            if i >= 2:
                                dve.wait_ge(*full("Y", l, i - 2, KT - 1))
                            step(dve.tensor_copy(hi, f_t[:, 0, 0:w]))
                            say("a_ready", dve.tensor_tensor(lo, f_t[:, 0, 0:w], hi.bitcast(F32), ALU.subtract))
                    if i:
                        for m in range(KT):
                            key = ("Y", l, i - 1, m)
                            dve.wait_ge(*full(*key))
                            parts = [(0, LAT, 0)] + [(LAT, T, 1)] * ctx_too
                            if i > 1:
                                dve.wait_ge(*freed("Y", l, i - 2, m))
                            for a, b, who in parts:
                                gate = mods[:, l, KT * 5 + m, who:who + 1]
                                if i == 1:
                                    ins = dve.tensor_scalar(y_chan[:, m, a:b], slot(*key)[:, a:b], gate, None, ALU.mult)
                                else:
                                    ins = dve.scalar_tensor_tensor(
                                        out=y_chan[:, m, a:b], in0=slot(*key)[:, a:b], scalar=gate,
                                        in1=y_chan[:, m, a:b], op0=ALU.mult, op1=ALU.add)
                                if b == parts[-1][1]:
                                    last = release(ins, *key)
                                else:
                                    also(ins)
                return last

            for l in range(DEPTH):
                for r in range(3):
                    end_phase(dve, phase_a(l, r), "A", l, r)
                end_phase(dve, phase_b(l), "B", l)
                end_phase(dve, phase_c(l), "C", l)
                end_phase(dve, phase_o(l), "O", l)
                end_phase(dve, phase_post(l, 0), "post", l, 0)
                end_phase(dve, phase_f(l), "F", l)
                end_phase(dve, phase_post(l, 1), "post", l, 1)

        @block.scalar
        def _(act):
            own = Signal(s["act_step"])

            def step(ins):
                token = own.on(ins)
                act.wait_ge(*token)
                return token

            def release(ins, *key):
                ins.then_inc(s[f"freed{plan.use[key] % 2}"], 1)
                return freed(*key)

            def say(name, ins):
                ins.then_inc(s[name], 1)

            def copy(dst, src, scale=1.0):
                return act.activation(dst, src, ACT.Copy, scale=scale)

            act.wait_ge(s["rows_turned"], 1)
            say("cond_ready", act.activation(cond[:], psum[:, 6, 456:472].rearrange("p (a k) -> p k a", a=2), ACT.Silu))
            act.preload_act_table_set(LN_EXP_SET)
            act.wait_ge(s["lb_shifted"], 2)
            say("lb_exps", act.activation(lb[:, 0], lb[:, 0], ACT.Exp))
            act.wait_ge(s["lb_args"], 1)
            step(act.activation(lb[:, 1], lb[:, 1], ACT.Ln, scale=float(2 ** LN_SHIFT)))
            say("lb_logs", act.activation(lb[:, 2], lb[:, 2], ACT.Ln))
            end_phase(act, (s["lb_logs"], 1), "setup")

            def rstd_of(key):
                n = nth("stat", *key)
                w, i = (n - 1) // NT % 2, (n - 1) % NT
                act.wait_ge(s["mean_ready"], n)
                r = rstd[:, w, i:i + 1]
                step(act.activation(r, mv[:, w, i, 1:2], ACT.Ln, bias=EPS))
                say("rstd_ready", act.activation(r, r, ACT.Exp, scale=-0.5))

            def modulated(key):
                n = nth("xh", *key)
                i = key[-1]
                l, first = (key[1], 3 * KT) if key[0] == "h2" else (key[1], 0)
                who = 0 if i < NTL else 1
                act.wait_ge(*full(*key))
                if n > 2:
                    act.wait_ge(s["h_ready"], n - 2)
                for k in range(KT):
                    ins = act.activation(n_t[:, n % 2, k], slot(*key)[:, P * k:P * k + P], ACT.Identity,
                                         bias=mods[:, l, first + k, who:who + 1],
                                         scale=mods[:, l, first + KT + k, who:who + 1])
                    if k < KT - 1:
                        own.on(ins)
                    else:
                        last = release(ins, *key)
                return last

            for i in range(NT + 2):
                if i < NT:
                    rstd_of(("h", 0, i))
                if i >= 2:
                    last = modulated(("h", 0, i - 2))
            end_phase(act, last, "h0")

            def attend(units, key_of, probs, turned):
                for u in range(len(units) + 1):
                    if u < len(units):
                        probs(u)
                    if u >= 1:
                        n = nth("unit", *key_of(u - 1))
                        act.wait_ge(*full(*key_of(u - 1)))
                        if n > 2:
                            act.wait_ge(s["out_ready"], n - 2)
                        last = turned(u - 1)
                return last

            def phase_a(l, r):
                for name, dst, scale in (("q", a_q, QSCALE), ("k", a_k, 1.0), ("v", a_vt, 1.0)):
                    key = ("A", l, r, name)
                    w = T if name != "q" or q_tiles(l) == NT else LAT
                    act.wait_ge(*full(*key))
                    release(copy(dst[:, 0:w], slot(*key)[:, 0:w], scale), *key)
                key = ("A", l, r, "vt")
                act.wait_ge(*full(*key))
                release(copy(a_v[:].rearrange("p c v -> p (c v)"), slot(*key)[:, 0:T]), *key)
                units = [(hh, p) for hh in range(2) for p in range(q_tiles(l))]

                def key_of(u):
                    return ("A", l, r, u)

                def probs(u):
                    hh, p = units[u]
                    n = nth("unit", *key_of(u))
                    c_ = n % 64
                    act.wait_ge(s["negmax_ready"], n)
                    if u >= 2:
                        act.wait_ge(*full(*key_of(u - 2)))
                    neg = stats[:, 1, c_:c_ + 1]
                    if p < NTL:
                        w = 64 * ROW_PAIRS[p][1]
                        own.on(act.activation(a_p[:, n % 2, 0:w], a_p[:, n % 2, 0:w], ACT.Exp, bias=neg,
                                              accum_out=stats[:, 2, c_:c_ + 1]))
                    else:
                        own.on(act.activation(stats[:, 2, c_:c_ + 1], neg, ACT.Copy, scale=0.0))
                    say("probs_ready", act.activation(a_p[:, n % 2, 576:832], slot(*key_of(u))[:, 576:832], ACT.Exp,
                                                      bias=neg, accum_out=stats[:, 3, c_:c_ + 1]))

                def turned(u):
                    hh, p = units[u]
                    key = key_of(u)
                    n = nth("unit", *key)
                    dst = a_pt[:, n % 2].rearrange("p b t -> p (b t)")
                    acc = slot(*key)
                    if p >= NTL:
                        return release(copy(dst[:, 512:768], acc[:, 512:768]), *key)
                    if ROW_PAIRS[p][1] > WIN_R:
                        own.on(copy(dst[0:64, 768:896], acc[0:64, 768:896]))
                    return release(copy(dst[:, 0:768], acc[:, 0:768]), *key)
                return attend(units, key_of, probs, turned)

            def phase_b(l):
                def part(name):
                    return {"k": b_k[:], "v": b_vt[:]}.get(name) if name in "kv" else b_q[:, int(name[1])]

                for name, _ in B_PARTS:
                    key = ("B", l, name)
                    w = T if name in "kv" or q_tiles(l) == NT else LAT
                    act.wait_ge(*full(*key))
                    release(copy(part(name)[:, 0:w], slot(*key)[:, 0:w]), *key)
                key = ("B", l, "vt")
                act.wait_ge(*full(*key))
                release(copy(b_v[:].rearrange("p c v -> p (c v)"), slot(*key)[:, 0:T]), *key)
                for name in B_NORMED:
                    n = nth("bn", l, name)
                    w = T if name == "k" or q_tiles(l) == NT else LAT
                    act.wait_ge(*freed("B", l, name))
                    if name != "k":
                        act.wait_ge(s["rope_ready"], n - 1)
                    say("sq_ready", act.activation(b_tmp[:, 0:w], part(name)[:, 0:w], ACT.Square))
                    key = ("B", l, name, "ms")
                    act.wait_ge(*full(*key))
                    act.wait_ge(*release(act.activation(b_tmp[:, 0:w], slot(*key)[:, 0:w], ACT.Ln, bias=EPS), *key))
                    say("act_headrstd", act.activation(b_tmp[:, 0:w], b_tmp[:, 0:w], ACT.Exp, scale=-0.5))
                key = ("B", l, "ks")
                act.wait_ge(*full(*key))
                release(copy(b_ks[:], slot(*key)[:, 0:T]), *key)
                units = [(h, i) for h in range(6) for i in range(q_tiles(l))]

                def key_of(u):
                    return ("B", l, u)

                def cols(u):
                    return slice(0, T) if units[u][1] < NTL else slice(LAT, T)

                def probs(u):
                    n = nth("unit", *key_of(u))
                    c_ = n % 64
                    act.wait_ge(s["negmax_ready"], n)
                    if u >= 2:
                        act.wait_ge(*full(*key_of(u - 2)))
                    own.on(act.activation(stats[:, 3, c_:c_ + 1], stats[:, 1, c_:c_ + 1], ACT.Copy, scale=0.0))
                    say("probs_ready", act.activation(b_p[:, n % 2, cols(u)], slot(*key_of(u))[:, cols(u)], ACT.Exp,
                                                      bias=stats[:, 1, c_:c_ + 1], accum_out=stats[:, 2, c_:c_ + 1]))

                def turned(u):
                    key = key_of(u)
                    dst = b_pt[:, nth("unit", *key) % 2].rearrange("p b t -> p (b t)")
                    return release(copy(dst[:, cols(u)], slot(*key)[:, cols(u)]), *key)
                return attend(units, key_of, probs, turned)

            def phase_c(l):
                for name, _ in C_PARTS:
                    j = int(name[1])
                    key = ("C", l, name)
                    dst = {"i": lambda: c_z[:, 2 + j], "g": lambda: c_z[:, 2 + j], "f": lambda: c_z[:, j],
                           "b": lambda: c_z[:, 2 + j], "q": lambda: c_q[:, j]}[name[0]]()
                    act.wait_ge(*full(*key))
                    release(copy(dst, slot(*key)[:, 0:T], QSCALE if name[0] == "q" else 1.0), *key)
                    if name in C_TURNED:
                        key = ("C", l, name, "t")
                        act.wait_ge(*full(*key))
                        to = (c_v if name[0] == "i" else c_g)[:, :, P * j:P * j + P]
                        src = slot(*key)[:, 0:T].rearrange("p (c v) -> p c v", v=P)
                        release(copy(to, src) if name[0] == "i" else act.activation(to, src, ACT.Silu), *key)
                act.preload_act_table_set(LN_EXP_SET)
                for name in ("q0", "q1"):
                    act.wait_ge(*freed("C", l, name))

                def gates_1(j):
                    w = c_w[:, j % 2]
                    if j >= 2:
                        act.wait_ge(s["b_ready"], nth("hg", l, j - 2))
                    step(act.activation(w[:, 0], c_z[:, j], ACT.Abs))
                    step(act.activation(w[:, 0], w[:, 0], ACT.Exp, scale=-1.0))
                    say("gate_l", act.activation(w[:, 0], w[:, 0], ACT.Ln, bias=1.0))

                def gates_2(j):
                    w = c_w[:, j % 2]
                    c_ = slice(4 * l + j, 4 * l + j + 1)
                    act.wait_ge(s["gate_m"], nth("hg", l, j))
                    own.on(act.activation(c_k[:, j], w[:, 2], ACT.Exp, scale=-1.0, bias=lb[:, 2, c_]))
                    step(act.activation(w[:, 3], w[:, 1], ACT.Abs, bias=lb[:, 3, c_]))
                    step(act.activation(w[:, 3], w[:, 3], ACT.Exp, scale=-1.0))
                    say("gate_k", act.activation(w[:, 3], w[:, 3], ACT.Ln, bias=1.0))

                gates_1(0)
                for j in range(4):
                    if j < 3:
                        gates_1(j + 1)
                    gates_2(j)

                def decays(j):
                    act.wait_ge(s["el_args"], nth("hg", l, j))
                    b = c_b[:, j].rearrange("p (c t) -> p c t", t=P)
                    own.on(act.activation(c_el[:, j, :], b[:, :, P - 1] if j < 2 else b[:, :, 0], ACT.Exp))
                    say("el_ready", act.activation(c_w[:, j % 2, 0], c_w[:, j % 2, 0], ACT.Exp))

                def turned(j):
                    act.wait_ge(*full("C", l, "kd", j))
                    if j >= 2:
                        act.wait_ge(*full("C", l, "D", j - 2))
                    release(copy(c_w[:, j % 2, 1], slot("C", l, "kd", j)[:, 0:T]), "C", l, "kd", j)

                for j in range(5):
                    if j < 4:
                        decays(j)
                    if j >= 1:
                        turned(j - 1)
                for lev in range(len(LEVELS)):
                    for tile in range(2):
                        act.wait_ge(s["lev_args"], nth("levx", l, lev, tile))
                        own.on(act.activation(c_lk[:, tile], c_lk[:, tile], ACT.Exp))
                        say("lev_exps", act.activation(c_lq[:, tile], c_lq[:, tile], ACT.Exp))
                for j in range(4):
                    say("inter_exps", act.activation(c_b[:, j], c_b[:, j], ACT.Exp))
                for i in range(q_tiles(l)):
                    n = nth("chunk", l, i)
                    act.wait_ge(s["ms_ready"], n)
                    step(act.activation(c_ms[:, 1, i, :], c_ms[:, 0, i, :], ACT.Ln, scale=1.0 / HD, bias=EPS))
                    say("hg_rstd", act.activation(c_ms[:, 1, i, :], c_ms[:, 1, i, :], ACT.Exp, scale=-0.5))
                return s["hg_rstd"], nth("chunk", l, q_tiles(l) - 1)

            def phase_o(l):
                for i in range(q_tiles(l)):
                    act.wait_ge(*full("O", l, i))
                    say("o_hi_ready", copy(h_hi[:, :, P * i:P * i + P],
                                           slot("O", l, i)[:, 0:D].rearrange("p (k n) -> p k n", n=P)))
                for m in range(KT):
                    key = ("W", l, m)
                    act.wait_ge(*full(*key))
                    if q_tiles(l) == NT:
                        own.on(act.activation(y_chan[:, m, LAT:T], slot(*key)[:, LAT:T], ACT.Copy,
                                              scale=mods[:, l, 2 * KT + m, 1:2]))
                    last = release(act.activation(y_chan[:, m, 0:LAT], slot(*key)[:, 0:LAT], ACT.Copy,
                                                  scale=mods[:, l, 2 * KT + m, 0:1]), *key)
                return last

            def phase_post(l, which):
                after = next_h(l, which)
                last = None
                nq = q_tiles(l)
                for i in range(nq + 4):
                    if i < nq:
                        rstd_of(("y", l, which, i))
                    if after and 1 <= i <= nq:
                        rstd_of((*after, i - 1))
                    if after and i >= 3 and i - 3 < nq:
                        last = modulated((*after, i - 3))
                return last or (s["rstd_ready"], nth("stat", "y", l, which, nq - 1))

            def phase_f(l):
                w = T if q_tiles(l) == NT else LAT
                for f in range(FT):
                    for half in range(2):
                        key = ("F", l, f, half)
                        act.wait_ge(*full(*key))
                        if f:
                            act.wait_ge(s["a_ready"], nth("ff", l, f - 1))
                        mid, shift = [224 * l + MODS + 2 * FT * j + FT * half + f for j in (1, 3)]
                        say("conv_start", act.activation(f_t[:, half, 0:w], slot(*key)[:, 0:w], ACT.Identity,
                                                         scale=vec[:, mid:mid + 1], bias=vec[:, shift:shift + 1]))
                        if half == 0:
                            act.wait_ge(*freed(*key))
                            say("silu_done", act.activation(f_t[:, 0, 0:w], f_t[:, 0, 0:w], ACT.Silu))
                act.preload_act_table_set(LN_EXP_SET)
                return s["silu_done"], nth("ff", l, FT - 1)

            for l in range(DEPTH):
                for r in range(3):
                    end_phase(act, phase_a(l, r), "A", l, r)
                end_phase(act, phase_b(l), "B", l)
                end_phase(act, phase_c(l), "C", l)
                end_phase(act, phase_o(l), "O", l)
                end_phase(act, phase_post(l, 0), "post", l, 0)
                end_phase(act, phase_f(l), "F", l)
                end_phase(act, phase_post(l, 1), "post", l, 1)


_INS = ["x", "c", "ctx", "c_ctx", "w_ada", "b_ada", "w_in", "w_out", "na_rpb", "q_norm", "k_norm", "hg_lower_bound",
        "hg_norm", "ln1_g", "ln1_b", "w_up", "conv_w", "conv_b", "w_down", "ln2_g", "ln2_b"]


def shape_constants():
    import numpy as np

    lane = np.arange(P)
    eye = np.eye(P, dtype=np.float32)
    rotate = eye[lane ^ 16]
    swap = eye[lane ^ 64]
    flip = eye[lane ^ 63]
    means = ((lane[:, None] // HD == lane[None] // HD) / HD).astype(np.float32)
    masks = np.zeros((P, len(LEVELS) + 1, P), np.float32)
    for n, h in enumerate(LEVELS):
        same = lane[:, None] // (2 * h) == lane[None] // (2 * h)
        masks[:, n] = same & (lane[:, None] // h != lane[None] // h)
    masks[:, len(LEVELS)] = np.eye(P)
    n_freq = HD // 4
    inv_freq = np.float32(10000.0) ** (-np.arange(n_freq, dtype=np.float32) / np.float32(n_freq))
    t = np.arange(LAT)
    pos = np.stack([t // GRID_W, t % GRID_W]).astype(np.float32)
    axis, half, freq = lane % HD // 32, lane % 32 // 16, lane % 16
    angle = (pos[axis] * inv_freq[freq][:, None]).astype(np.float32)
    sign = np.where(half == 0, -1.0, 1.0).astype(np.float32)[:, None]
    window = np.full((P, BIAS_BLOCKS, 64), -1e30, np.float32)
    for w in range(64):
        first = min(max(w - WIN_C // 2, 0), GRID_W - WIN_C)
        window[[w, 64 + w], :, first:first + WIN_C] = 0.0
    window[0:64, BIAS_BLOCKS - 1] = -1e30
    window[64:P, BIAS_BLOCKS - 9] = -1e30
    return dict(identity=eye, reverse_columns=flip, rotate_halves=rotate, swap_heads=swap, head_means=means, level_masks=masks,
                rope_cos=np.cos(angle), rope_sin=np.sin(angle) * sign, window_mask=window.reshape(P, -1))


def kernel(**inputs):
    import numpy as np
    import concourse.bacc as bacc
    from concourse.bass_utils import run_bass_kernel_spmd

    nc = bacc.Bacc("TRN2", target_bir_lowering=False, num_devices=1)
    arrays, args = {}, {}
    for name, value in [(n, inputs[n]) for n in _INS] + list(shape_constants().items()):
        a = np.ascontiguousarray(value)
        arrays[f"in_{name}_dram"] = a
        args[name] = nc.dram_tensor(f"in_{name}_dram", a.shape, mybir.dt.from_np(a.dtype), kind="ExternalInput").ap()
    out = nc.dram_tensor("out_0_dram", (1, LAT, D), F32, kind="ExternalOutput").ap()
    build(nc, **args, out=out)
    r = run_bass_kernel_spmd(nc, [arrays], core_ids=[0])
    return r.results[0]["out_0_dram"]
```

```python
from contextlib import ExitStack

import concourse.bass as bass
from concourse import mybir

P = 128
D = 1024
KT = D // P
LAT, CTX = 1024, 256
T = LAT + CTX
NT, NTL = T // P, LAT // P
DEPTH = 2
GRID_W, ROWS = 64, LAT // 64
WIN_R, WIN_C = 8, 16
HD = 64
HG_COLS = 256
D_FF = 2816
FT = D_FF // P
NPAIR = FT // 2
N_MOD = 6
MODS = N_MOD * KT
ALPHA = (2.0 * DEPTH) ** 0.25
EPS = 1e-6
LB_FLOOR = 1e-30
QSCALE = HD ** -0.5
LN_SHIFT = 40
NEVER = -1e30
LN2 = 0.6931471805599453
COL = dict(a_k=0, a_v=384, b_k=768, b_v=896, c_f=1024, c_b=1280, c_i=1536, a_q=1792, b_q=2176, c_q=2560, c_g=2816)
GROUPS = [(0, 512), (512, 512), (1024, 256)]
LEVELS = [1, 2, 4, 8, 16, 32, 64]
PAD_W = 128
N_RPB = 15
RPB_ROWS = 6 * N_RPB
ROW_PAIRS = []
for _p in range(ROWS // 2):
    _s = [min(max(r - WIN_R // 2, 0), ROWS - WIN_R) for r in (2 * _p, 2 * _p + 1)]
    _n = _s[1] + WIN_R - _s[0]
    ROW_PAIRS.append((_s[0], _n, 14 if _n > WIN_R else _s[0] - 2 * _p + 6))
BIAS_BLOCKS = 14 + 9
B_PARTS = dict(k=COL["b_k"], v=COL["b_v"], q0=COL["b_q"], q1=COL["b_q"] + P, q2=COL["b_q"] + 2 * P)
B_STEPS = [("gemm", "k"), ("gemm", "v"), ("gemm", "q0"), ("turn", "v"), ("ms", "k"), ("gemm", "q1"), ("rot", "k"),
           ("ms", "q0"), ("gemm", "q2"), ("rot", "q0"), ("ms", "q1"), ("rot", "q1"), ("ms", "q2"), ("swap", "k"),
           ("rot", "q2")]
B_NORMED = ["k", "q0", "q1", "q2"]
C_PARTS = [(f"{x}{j}", COL["c_" + x] + P * j) for x in "igfbq" for j in range(2)]
C_TURNED = ("i0", "i1", "g0", "g1")
N_CONSTS = 6 + DEPTH
N_ROWS = 4 * DEPTH + 7
ARENA = 206 * 1024
CHUNK_GROUPS = [(0, 4), (4, 4), (8, 2)]


ADA_FIRST = 2 * D // 512
ADA_LATE_W = 256
LATE_PER_MOD = D // ADA_LATE_W


def late_tiles(l):
    parts = [(l, 2 * D, N_MOD * D)] + [(l + 1, 0, 2 * D)] * (l < DEPTH - 1)
    return [(m, a) for m, first, end in parts for a in range(first, end, ADA_LATE_W)]


def n_late(l):
    return sum(len(late_tiles(m)) for m in range(l + 1))


def q_tiles(l):
    return NT if l < DEPTH - 1 else NTL


def next_h(l, which):
    if which == 0:
        return ("h2", l)
    return ("h", l + 1) if l < DEPTH - 1 else None

F32 = mybir.dt.float32
F32R = mybir.dt.float32r
U8 = mybir.dt.uint8
ALU = mybir.AluOpType
ACT = mybir.ActivationFunctionType
AX = mybir.AxisListType.X
LN_EXP_SET = "natural_log_exp_and_others"


class Signal:

    def __init__(self, sem):
        self.sem, self.n = sem, 0

    def on(self, instruction, by=1):
        instruction.then_inc(self.sem, by)
        self.n += by
        return self.sem, self.n


class Plan:

    def __init__(self):
        self.use, self.tile, self.tiles, self.tile_last = {}, {}, [], []
        for i in range(NT):
            self.slot("h", 0, i)
        for l in range(DEPTH):
            nq = q_tiles(l)
            for r in range(3):
                for name in "qkv":
                    self.gemm(("in", l, COL["a_" + name] + P * r), ("A", l, r, name))
                self.slot("A", l, r, "vt")
                for hh in range(2):
                    self.slot("A", l, r, "bias", hh)
                self.units(2 * nq, "A", l, r)
            for what, name in B_STEPS:
                if what == "gemm":
                    self.gemm(("in", l, B_PARTS[name]), ("B", l, name))
                else:
                    self.slot("B", l, name, what)
            self.units(6 * nq, "B", l)
            for name, col in C_PARTS:
                self.gemm(("in", l, col), ("C", l, name))
                if name in C_TURNED:
                    self.slot("C", l, name, "t")
            for j in range(4):
                self.slot("C", l, "kd", j)
                self.slot("C", l, "D", j)
            for lev in range(len(LEVELS) + 1):
                for tile in range(2):
                    for q in range(len(CHUNK_GROUPS)):
                        self.slot("C", l, "att", lev, tile, q)
            for i in range(nq):
                self.slot("O", l, i)
            for m in range(KT):
                self.gemm(("out", l, m), ("W", l, m))
            self.post(l, 0, nq)
            for i in range(NPAIR + 1):
                if i < NPAIR:
                    for f in (2 * i, 2 * i + 1):
                        for half in range(2):
                            self.gemm(("up", l, f, half), ("F", l, f, half))
                if i:
                    for q in range(2):
                        self.gemm(("down", l, i - 1, q), *[("Y", l, i - 1, m) for m in range(4 * q, 4 * q + 4)])
            self.post(l, 1, nq)

    def units(self, n, *phase):
        self.slot(*phase, 0)
        for u in range(n):
            if u + 1 < n:
                self.slot(*phase, u + 1)
            self.slot(*phase, u, "turned")

    def post(self, l, which, n):
        for i in range(n + 2):
            if i < n:
                self.slot("y", l, which, i)
            if i >= 2 and next_h(l, which):
                self.slot(*next_h(l, which), i - 2)

    def slot(self, *key):
        assert key not in self.use, key
        self.use[key] = len(self.use)

    def gemm(self, tile, *uses):
        self.tile[tile] = len(self.tiles)
        self.tiles.append(tile)
        for key in uses:
            self.slot(*key)
        self.tile_last.append(uses[-1])

    def events(self):
        e = {k: [] for k in ("stat", "xh", "unit", "bn", "hg", "lev", "levx", "chunk", "osplit", "post", "conv", "ff")}
        for i in range(NT):
            e["stat"].append(("h", 0, i))
            e["xh"].append(("h", 0, i))
        for l in range(DEPTH):
            nq = q_tiles(l)
            e["unit"] += [("A", l, r, u) for r in range(3) for u in range(2 * nq)]
            e["unit"] += [("B", l, u) for u in range(6 * nq)]
            e["bn"] += [(l, name) for name in B_NORMED]
            e["hg"] += [(l, j) for j in range(4)]
            e["lev"] += [(l, lev, tile) for lev in range(len(LEVELS) + 1) for tile in range(2)]
            e["levx"] += [(l, lev, tile) for lev in range(len(LEVELS)) for tile in range(2)]
            e["chunk"] += [(l, i) for i in range(nq)]
            e["osplit"] += [(l, i) for i in range(nq)]
            e["conv"] += [(l, f, half) for f in range(FT) for half in range(2)]
            e["ff"] += [(l, f) for f in range(FT)]
            for which in range(2):
                after = next_h(l, which)
                for i in range(nq + 1):
                    if i < nq:
                        e["stat"].append(("y", l, which, i))
                        e["post"].append((l, which, i))
                    if i and after:
                        e["stat"].append((*after, i - 1))
                if after:
                    e["xh"] += [(*after, i) for i in range(nq)]
        return e


def spread(row):
    return bass.AP(tensor=row.tensor, offset=row.offset, ap=[[0, P], *row.ap])


def build(nc, x, c, ctx, c_ctx, w_ada, b_ada, w_in, w_out, na_rpb, q_norm, k_norm, hg_lower_bound, hg_norm,
          ln1_g, ln1_b, w_up, conv_w, conv_b, w_down, ln2_g, ln2_b,
          identity, reverse_columns, rotate_halves, swap_heads, head_means, level_masks, rope_cos, rope_sin, window_mask, out, dump=None):
    plan = Plan()
    events = plan.events()
    ordinal = {kind: {key: n + 1 for n, key in enumerate(keys)} for kind, keys in events.items()}
    XH = events["xh"]

    def nth(kind, *key):
        return ordinal[kind][key]

    with ExitStack() as stack:
        top_before = nc.sbuf_base
        arena = stack.enter_context(nc.sbuf_tensor("arena", [P, ARENA // 4], F32))
        ARENA_AT = nc.sbuf_base - ARENA
        psum = stack.enter_context(nc.psum_tensor("psum", [P, 8, 512], F32))
        top = [0]

        def place(name, shape, offset, dtype=F32):
            size = mybir.dt.size(dtype)
            for n in shape:
                size *= n
            assert offset + size <= ARENA, (name, offset + size)
            top[0] = max(top[0], offset + size)
            return nc.alloc_sbuf_tensor_at(name, [P, *shape], dtype, offset=ARENA_AT + offset)

        H, O, W = 0, 8 * KT * T, 12 * KT * T
        G = W + 6 * KT * P * 4
        C = G + 51200

        h_hi = place("h_hi", [KT, T], H, F32R)
        h_lo = place("h_lo", [KT, T], H + 4 * KT * T, F32R)
        o_tok = place("o_tok", [NT, D], O)
        y_chan = place("y_chan", [KT, T], O)
        w_raw = place("w_raw", [2, KT * P], W)
        w_hi = place("w_hi", [2, KT * P], W + 8 * KT * P, F32R)
        w_lo = place("w_lo", [2, KT * P], W + 16 * KT * P, F32R)

        at = [C]

        def keep(name, shape, dtype=F32):
            t = place(name, shape, at[0], dtype)
            size = mybir.dt.size(dtype)
            for n in shape:
                size *= n
            at[0] += (size + 31) // 32 * 32
            return t

        ident = keep("ident", [P])
        flip = keep("flip", [P])
        rot = keep("rot", [P])
        swap = keep("swap", [P])
        means = keep("means", [P])
        ones = keep("ones", [P])
        zeros = keep("zeros", [P])
        masks = keep("masks", [len(LEVELS) + 1, P], U8)
        vec = keep("vec", [2 * 224 + 8])
        mods = keep("mods", [DEPTH, MODS, 2])
        head_g = keep("head_g", [2, DEPTH])
        hgn = keep("hgn", [DEPTH, HD])
        cond = keep("cond", [KT, 2])
        lb = keep("lb", [4, 8])
        stats = keep("stats", [4, 64])
        bn = keep("bn", [NT, 12])
        mv = keep("mv", [2, NT, 2])
        rstd = keep("rstd", [2, NT])

        def g(name, shape, at_float, dtype=F32):
            return place(name, shape, G + 4 * at_float, dtype)

        rows = g("rows", [14, P], 0)
        pad_rows = g("pad_rows", [DEPTH, PAD_W], 14 * P)
        masks_in = g("masks_in", [len(LEVELS) + 1, P], (14 + 2) * P)
        ada = place("ada", [4, KT, 512], H)
        ada_late = place("ada_late", [3, KT, ADA_LATE_W], W)

        n_xt = g("n_xt", [2, D], 0)
        n_xh = g("n_xh", [2, D], 2 * D)
        n_t = g("n_t", [2, KT, P], 4 * D)
        n_r = g("n_r", [2, D], 6 * D)
        n_x1 = g("n_x1", [2, D], 8 * D)
        n_g = g("n_g", [D], 10 * D)
        n_b = g("n_b", [D], 11 * D)

        a_q = g("a_q", [2, T], 0)
        a_k = g("a_k", [T], 2 * T)
        a_v = g("a_v", [NT, P], 3 * T)
        a_bias = g("a_bias", [2, BIAS_BLOCKS, GRID_W], 4 * T)
        a_mask = g("a_mask", [GRID_W], 4 * T + 2 * BIAS_BLOCKS * 64)
        a_at = 4 * T + (2 * BIAS_BLOCKS + 1) * GRID_W
        a_p = g("a_p", [2, 832], a_at)
        a_pt = g("a_pt", [2, 7, P], a_at + 2 * 832)
        a_vt = g("a_vt", [T], a_at + 2 * 832)

        b_q = g("b_q", [3, T], 0)
        b_v = g("b_v", [NT, P], 3 * T)
        b_kz = g("b_kz", [2, 2, T], 4 * T)
        b_pt = g("b_pt", [2, NT, P], 8 * T)
        b_cos = g("b_cos", [LAT], 4 * T)
        b_sin = g("b_sin", [LAT], 4 * T + LAT)
        b_tmp = [g("b_tmp0", [T], 9 * T), g("b_tmp1", [T], 4 * T + 2 * LAT)]
        b_vt = g("b_vt", [T], 4 * T + 2 * LAT)
        b_k = g("b_k", [T], 8 * T)

        def b_p(n):
            return o_tok[:, :, D - P * (1 + n % 2):D - P * (n % 2)]

        c_z = g("c_z", [4, T], 0)
        c_state = g("c_state", [4, NT, HD], 0)
        c_q = g("c_q", [2, T], 4 * T)
        c_v = g("c_v", [NT, 2 * P], 6 * T)
        c_g = g("c_g", [NT, 2 * P], 8 * T)
        c_b = place("c_b", [4, T], H)
        c_k = place("c_k", [4, T], H + 16 * T)
        c_lq = place("c_lq", [2, T], H + 32 * T)
        c_lk = place("c_lk", [2, T], H + 40 * T)
        c_w = place("c_w", [2, 4, T], H + 32 * T)
        c_att = place("c_att", [NT, 4, P], H + 48 * T)
        c_el = keep("c_el", [4, NT])
        c_o = g("c_o", [2, 2 * P], 2 * T)
        c_o2 = g("c_o2", [2, 2 * P], 2 * T + 4 * P)
        c_ms = keep("c_ms", [2, NT, 4])

        f_hi = g("f_hi", [2, 2, T], 0, F32R)
        f_lo = g("f_lo", [2, 2, T], 4 * T, F32R)
        f_t = g("f_t", [2, T], 8 * T)

        pads = nc.dram_tensor("pads", (DEPTH, RPB_ROWS, PAD_W), F32, kind="Internal").ap()
        x_mid = [[nc.dram_tensor(f"x_mid{l}{w}", (T, D), F32, kind="Internal").ap() for w in range(2)]
                 for l in range(DEPTH)]

        def sem(name):
            return stack.enter_context(nc.semaphore(name))

        s = {}
        for name in (
            "const_landed", "rows_landed", "pads_stored", "cond_ready", "rows_turned", "vec_ready",
            "ada_landed0", "ada_landed1", "ada_landed2", "ada_landed3", "ada_used", "late_landed0", "late_landed1",
            "late_landed2", "late_used", "lb_shifted", "lb_exps",
            "lb_args", "lb_logs", "phase_end",
            "w_landed0", "w_landed1", "w_hi_done", "w_ready",
            "full0", "full1", "freed0", "freed1",
            "x_landed0", "x_landed1", "ln_landed", "mean_ready", "rstd_ready", "xh_ready", "h_ready",
            "mean2_ready", "rstd2_ready", "x1_ready", "x1_stored0", "x1_stored1",
            "bias_landed", "negmax_ready", "probs_ready", "out_ready", "out_freed",
            "sq_ready", "act_headrstd", "headnorm_ready", "rope_ready", "rope_landed", "a_zeroed", "kz_ready",
            "gate_l", "gate_m", "gate_k", "b_ready", "el_args", "el_ready", "kd_ready", "states_ready",
            "lev_args", "lev_exps", "lev_ready", "att_done", "inter_exps", "inter_ready",
            "ms_ready", "hg_rstd", "c_out_ready", "c_out_freed", "silu_g", "o_hi_ready", "h_split",
            "conv_start", "conv_done", "silu_done", "a_ready", "w_unused",
            "pe_step", "act_step", "dve_step", "pool_step", "sp_done",
        ):
            s[name] = sem(name)

        def full(*key):
            n = plan.use[key]
            return s[f"full{n % 2}"], n // 2 + 1

        def freed(*key):
            n = plan.use[key]
            return s[f"freed{n % 2}"], n // 2 + 1

        def slot(*key):
            n = plan.use[key] % 2
            return psum[:, 3 * n:3 * n + 3, :].rearrange("p b n -> p (b n)")

        def before(*key):
            n = plan.use[key]
            return (s[f"freed{n % 2}"], n // 2) if n >= 2 else None

        def groups(l):
            return GROUPS if q_tiles(l) == NT else GROUPS[:2]

        phases = []
        for l in range(DEPTH):
            phases += [("A", l, 0), ("A", l, 1), ("A", l, 2), ("B", l), ("C", l), ("O", l), ("post", l, 0), ("F", l),
                       ("post", l, 1)]
        phases = [("setup",), ("h0",)] + phases
        PHASE = {key: n for n, key in enumerate(phases)}

        def phase_entered(*key):
            return s["phase_end"], 3 * PHASE[key]

        def n_bias_loads(l, r):
            return 8 * (3 * l + r + 1) + l + 1

        def end_phase(eng, last, *key):
            eng.wait_ge(*last)
            eng.sem_inc(s["phase_end"], 1)
            eng.wait_ge(s["phase_end"], 3 * (PHASE[key] + 1))

        block = stack.enter_context(nc.Block())

        @block.sync
        def _(sp):
            consts = Signal(s["const_landed"])
            for dst, src in ((ident, identity), (flip, reverse_columns), (rot, rotate_halves), (swap, swap_heads), (means, head_means)):
                consts.on(sp.dma_start(dst[:], src), 16)
            consts.on(sp.dma_start(masks_in[:], level_masks), 16)
            for l in range(DEPTH):
                consts.on(sp.dma_start(hgn[:, l, :], spread(hg_norm[l])), 16)
            assert consts.n == 16 * N_CONSTS
            rows_in = Signal(s["rows_landed"])
            for l in range(DEPTH):
                rows_in.on(sp.dma_start(rows[0:MODS, 5 * l, :], b_ada[l].rearrange("(m p) -> m p", p=P)), 16)
                rows_in.on(sp.dma_start(rows[0:2 * FT, 5 * l + 1:5 * l + 4, :],
                                        conv_w[l].rearrange("j (m p) -> m j p", p=P)), 16)
                rows_in.on(sp.dma_start(rows[0:2 * FT, 5 * l + 4, :], conv_b[l].rearrange("(m p) -> m p", p=P)), 16)
            rows_in.on(sp.dma_start(rows[0:8, 10, :], hg_lower_bound.rearrange("l d (m p) -> (l d m) p", p=P)), 16)
            for a, vector in enumerate((c[0], c_ctx)):
                rows_in.on(sp.dma_start(rows[0:KT, 11 + a, :], vector.rearrange("(k p) -> k p", p=P)), 16)
            for n, gain in enumerate((q_norm, k_norm)):
                for half in range(2):
                    rows_in.on(sp.dma_start(rows[DEPTH * n:DEPTH * (n + 1), 13, HD * half:HD * (half + 1)], gain), 16)
            sp.wait_ge(s["pool_step"], 1)
            for l in range(DEPTH):
                rows_in.on(sp.dma_start(pad_rows[0:RPB_ROWS, l, 48:79], na_rpb[l].rearrange("h a b -> (h a) b")), 16)
            sp.wait_ge(s["rows_landed"], rows_in.n)
            assert rows_in.n == 16 * N_ROWS
            pads_out = Signal(s["pads_stored"])
            pads_out.on(sp.dma_start(pads.rearrange("l r n -> r l n"), pad_rows[0:RPB_ROWS]), 16)

            def load_weights(n):
                kind, l, a, *b = plan.tiles[n]
                if kind == "in":
                    src = w_in[l].rearrange("(k p) n -> p k n", p=P)[:, :, a:a + P]
                elif kind == "out":
                    src = w_out[l].rearrange("(k p) n -> p k n", p=P)[:, :, P * a:P * a + P]
                elif kind == "up":
                    at_col = P * a + D_FF * b[0]
                    src = w_up[l].rearrange("(k p) n -> p k n", p=P)[:, :, at_col:at_col + P]
                else:
                    src = w_down[l][2 * P * a:2 * P * (a + 1)].rearrange("(k p) n -> p k n", p=P)[
                        :, :, 512 * b[0]:512 * (b[0] + 1)]
                if n >= 2:
                    sp.wait_ge(s["w_ready"], n - 1)
                sp.dma_start(w_raw[:, n % 2].rearrange("p (k n) -> p k n", k=src.shape[1]), src)\
                  .then_inc(s[f"w_landed{n % 2}"], 16)

            sent = [0]

            def weights_up_to(*tile):
                end = plan.tile[tile] + 1
                for n in range(sent[0], end):
                    load_weights(n)
                sent[0] = max(sent[0], end)

            weights_up_to("in", 0, COL["a_k"])
            for n in range(ADA_FIRST):
                src = w_ada[0].rearrange("(k p) n -> p k n", p=P)[:, :, 512 * n:512 * (n + 1)]
                sp.dma_start(ada[:, n], src).then_inc(s[f"ada_landed{n}"], 16)

            x_in = [Signal(s["x_landed0"]), Signal(s["x_landed1"])]
            n_in = [0]

            def load_x(src, i):
                x_in[n_in[0] % 2].on(sp.dma_start(n_xt[:, n_in[0] % 2, :], src), 16)
                n_in[0] += 1

            def source(l, which, i):
                if (l, which) == (0, 0):
                    return x[0, P * i:P * i + P, :] if i < NTL else ctx[0, P * (i - NTL):P * (i - NTL) + P, :]
                before_ = x_mid[l][0] if which else x_mid[l - 1][1]
                return before_[P * i:P * i + P, :]

            sp.wait_ge(*phase_entered("h0"))
            for i in range(NT):
                if i >= 2:
                    sp.wait_ge(s["xh_ready"], i - 1)
                load_x(source(0, 0, i), i)

            bias_in = Signal(s["bias_landed"])
            ln_in = Signal(s["ln_landed"])
            rope_in = Signal(s["rope_landed"])
            x_out = [Signal(s["x1_stored0"]), Signal(s["x1_stored1"])]
            n_post = 0
            for l in range(DEPTH):
                for r in range(3):
                    weights_up_to("in", l, COL["a_v"] + P * r)
                    sp.wait_ge(*phase_entered("A", l, r))
                    if r == 0:
                        bias_in.on(sp.dma_start(a_mask[:], window_mask), 16)
                        if l == 0:
                            sp.wait_ge(s["pads_stored"], pads_out.n)
                    for hh in range(2):
                        row = (l * 6 + 2 * r + hh) * N_RPB
                        table = a_bias[:, hh]
                        for half, first, blocks, at_block in ((0, 1, 14, 0), (1, 0, 14, 0), (0, 3, 9, 14), (1, 2, 9, 14)):
                            src = bass.AP(tensor=pads.tensor, offset=(row + first) * PAD_W,
                                          ap=[[1, 64], [PAD_W, blocks], [1, 64]])
                            bias_in.on(sp.dma_start(table[64 * half:64 * half + 64, at_block:at_block + blocks, :],
                                                    src), 16)
                weights_up_to("in", l, B_PARTS["q2"])
                sp.wait_ge(*phase_entered("B", l))
                rope_in.on(sp.dma_start(b_cos[:], rope_cos), 16)
                rope_in.on(sp.dma_start(b_sin[:], rope_sin), 16)
                weights_up_to("in", l, C_PARTS[-1][1])
                sp.wait_ge(*full("C", l, C_PARTS[-1][0]))
                for n, (m, a) in enumerate(late_tiles(l), n_late(l) - len(late_tiles(l))):
                    if n >= 3:
                        sp.wait_ge(s["late_used"], n - 2)
                    sp.dma_start(ada_late[:, n % 3], w_ada[m].rearrange("(k p) n -> p k n", p=P)[:, :, a:a + ADA_LATE_W])\
                      .then_inc(s[f"late_landed{n % 3}"], 16)
                sp.wait_ge(s["late_used"], n_late(l))
                weights_up_to("out", l, KT - 1)
                for which in range(2):
                    if which:
                        weights_up_to("down", l, NPAIR - 1, 1)
                    sp.wait_ge(*phase_entered("post", l, which))
                    gain, shift = (ln2_g, ln2_b) if which else (ln1_g, ln1_b)
                    ln_in.on(sp.dma_start(n_g[:], spread(gain[l])), 16)
                    ln_in.on(sp.dma_start(n_b[:], spread(shift[l])), 16)
                    last = next_h(l, which) is None
                    dst = out[0] if last else x_mid[l][which]
                    nq = q_tiles(l)
                    for i in range(nq + 1):
                        if i < nq:
                            if i >= 2:
                                sp.wait_ge(*freed("y", l, which, i - 2))
                            if not (l == 0 and which == 0) and i == 0:
                                for k in range(2):
                                    sp.wait_ge(x_out[k].sem, x_out[k].n)
                            load_x(source(l, which, i), i)
                        if i >= 1:
                            sp.wait_ge(s["x1_ready"], n_post + 1)
                            x_out[n_post % 2].on(sp.dma_start(dst[P * (i - 1):P * i, :], n_x1[:, n_post % 2, :]), 16)
                            n_post += 1
            for k in range(2):
                sp.wait_ge(x_out[k].sem, x_out[k].n)

        @block.gpsimd
        def _(pool):
            pool.memset(pad_rows[:], 0.0).then_inc(s["pool_step"], 1)
            for n in range(len(plan.tiles)):
                pool.wait_ge(s[f"w_landed{n % 2}"], 16 * (n // 2 + 1))
                if n >= 2:
                    pool.wait_ge(*full(*plan.tile_last[n - 2]))
                pool.tensor_scalar(w_hi[:, n % 2], w_raw[:, n % 2], 1.0, None, ALU.mult).then_inc(s["w_hi_done"], 1)
                pool.wait_ge(s["w_hi_done"], n + 1)
                pool.tensor_tensor(w_lo[:, n % 2], w_raw[:, n % 2], w_hi[:, n % 2].bitcast(F32), ALU.subtract)\
                    .then_inc(s["w_ready"], 1)

        @block.tensor
        def _(pe):
            def wait(token):
                if token is not None and token[1] > 0:
                    pe.wait_ge(*token)

            def fill(ins, *key):
                ins.then_inc(s[f"full{plan.use[key] % 2}"], 1)
                return full(*key)

            def turn(out_ap, in_ap, rows_=P):
                return pe.transpose(out_ap, in_ap, ident[0:rows_, 0:rows_])

            def gemm(tile, key, parts, kt=KT, col=0, x_hi=h_hi, x_lo=h_lo):
                n = plan.tile[tile]
                wait((s["w_ready"], n + 1))
                wait(before(*key))
                acc = slot(*key)
                halves = ((w_hi, x_hi), (w_hi, x_lo), (w_lo, x_hi))
                for k in range(kt):
                    for j, (w, a) in enumerate(halves):
                        weight = w[:, n % 2].rearrange("p (k n) -> p k n", k=kt)[:, k, col:col + P]
                        for t0, tn in parts:
                            last = pe.matmul(acc[:, t0:t0 + tn], weight, a[:, k, t0:t0 + tn],
                                             start=(k == 0 and j == 0), stop=(k == kt - 1 and j == 2))
                return fill(last, *key)

            wait((s["const_landed"], 16 * N_CONSTS))
            wait((s["rows_landed"], 16 * N_ROWS))
            for l in range(DEPTH):
                turn(psum[:, 6, 224 * l:224 * l + MODS], rows[0:MODS, 5 * l, :], MODS)
                for j in range(4):
                    at_col = 224 * l + MODS + 2 * FT * j
                    turn(psum[:, 6, at_col:at_col + 2 * FT], rows[0:2 * FT, 5 * l + 1 + j, :], 2 * FT)
            turn(psum[:, 6, 448:456], rows[0:8, 10, :], 8)
            for a in range(2):
                turn(psum[:, 6, 456 + KT * a:456 + KT * (a + 1)], rows[0:KT, 11 + a, :], KT)
            turn(psum[:, 6, 472:476], rows[0:2 * DEPTH, 13, :], 2 * DEPTH).then_inc(s["rows_turned"], 1)
            wait((s["cond_ready"], 1))

            def modulation(at_col, weight):
                for k in range(KT):
                    last = pe.matmul(psum[:, 7, at_col:at_col + 96].rearrange("p (r a) -> p r a", a=2), weight(k),
                                     cond[:, k, :].unsqueeze(1).broadcast_to([P, 48, 2]), start=(k == 0),
                                     stop=(k == KT - 1))
                return last

            for n in range(ADA_FIRST):
                wait((s[f"ada_landed{n}"], 16))
                for m in range(4):
                    last = modulation(8 * n + 2 * m, lambda k: ada[:, n, k, P * m:P * m + P])
                last.then_inc(s["ada_used"], 1)
            end_phase(pe, (s["ada_used"], ADA_FIRST), "setup")

            def turn_normed(key):
                wait((s["xh_ready"], nth("xh", *key)))
                wait(before(*key))
                acc = slot(*key)
                for k in range(KT):
                    last = turn(acc[:, P * k:P * k + P], n_xh[:, nth("xh", *key) % 2, P * k:P * k + P])
                return fill(last, *key)

            for i in range(NT):
                last = turn_normed(("h", 0, i))
            end_phase(pe, last, "h0")

            def attend_pv(unit_key, blocks):
                u = nth("unit", *unit_key)
                wait(freed(*unit_key, "turned"))
                if u > 2:
                    wait((s["out_freed"], u - 2))
                for n, (probs, values) in enumerate(blocks):
                    last = pe.matmul(psum[:, 6 + u % 2, 0:P], probs, values, start=(n == 0),
                                     stop=(n == len(blocks) - 1))
                last.then_inc(s["out_ready"], 1)

            def phase_a(l, r):
                wait((s["h_ready"], nth("xh", "h", l, NT - 1)))
                for name in "qkv":
                    gemm(("in", l, COL["a_" + name] + P * r), ("A", l, r, name),
                         groups(l) if name == "q" else GROUPS)
                key = ("A", l, r, "vt")
                wait(freed("A", l, r, "v"))
                wait(before(*key))
                for i in range(NT):
                    last = turn(slot(*key)[:, P * i:P * i + P], a_vt[:, P * i:P * i + P])
                fill(last, *key)
                wait((s["bias_landed"], 16 * n_bias_loads(l, r)))
                for hh in range(2):
                    table = a_bias[:, hh].rearrange("p b n -> p (b n)")
                    key = ("A", l, r, "bias", hh)
                    wait(before(*key))
                    for t0 in range(0, BIAS_BLOCKS * 64, 512):
                        t1 = min(t0 + 512, BIAS_BLOCKS * 64)
                        last = pe.matmul(slot(*key)[:, t0:t1], flip[:], table[:, t0:t1], start=True, stop=True)
                    fill(last, *key)
                nq = q_tiles(l)
                units = [(hh, p) for hh in range(2) for p in range(nq)]

                def scores(u):
                    hh, p = units[u]
                    key = ("A", l, r, u)
                    if u == 0:
                        wait((s["a_zeroed"], 2 * (3 * l + r + 1)))
                        for name in "qk":
                            wait(freed("A", l, r, name))
                    wait(before(*key))
                    acc = slot(*key)
                    q = a_q[:, hh, P * p:P * p + P]
                    if p < NTL:
                        start, n, _ = ROW_PAIRS[p]
                        pe.matmul(acc[:, 0:512], q, a_k[:, 64 * start:64 * start + 512], start=True, stop=True)
                        if n > WIN_R:
                            pe.matmul(acc[:, 512:576], q, a_k[:, 64 * (start + 8):64 * (start + 9)],
                                      start=True, stop=True)
                    last = pe.matmul(acc[:, 576:832], q, a_k[:, LAT:T], start=True, stop=True)
                    fill(last, *key)

                def turn_probs(u):
                    hh, p = units[u]
                    key = ("A", l, r, u)
                    n_unit = nth("unit", *key)
                    key = (*key, "turned")
                    wait((s["probs_ready"], n_unit))
                    wait(before(*key))
                    acc = slot(*key)
                    src = a_p[:, n_unit % 2]
                    last = None
                    w = GRID_W * ROW_PAIRS[p][1] if p < NTL else 0
                    if p < NTL:
                        for b in range(4):
                            turn(acc[:, P * b:P * b + P], src[:, P * b:P * b + P])
                    for b in range(2):
                        last = turn(acc[:, P * (4 + b):P * (5 + b)], src[:, w + P * b:w + P * b + P])
                    if p < NTL and ROW_PAIRS[p][1] > WIN_R:
                        last = pe.transpose(acc[0:64, P * 6:P * 7], src[:, 512:576], ident[:])
                    fill(last, *key)

                def values(u):
                    hh, p = units[u]
                    key = ("A", l, r, u)
                    if u == 0:
                        wait(freed("A", l, r, "vt"))
                    pt = a_pt[:, nth("unit", *key) % 2]
                    blocks = [(pt[:, 4 + b, :], a_v[:, NTL + b, :]) for b in range(2)]
                    if p < NTL:
                        start, n, _ = ROW_PAIRS[p]
                        blocks += [(pt[:, b, :], a_v[:, start // 2 + b, :]) for b in range(4)]
                        if n > WIN_R:
                            blocks.append((pt[0:64, 6, :], a_v[0:64, start // 2 + 4, :]))
                    attend_pv(key, blocks)

                scores(0)
                for u in range(len(units) + 1):
                    if u + 1 < len(units):
                        scores(u + 1)
                    if u < len(units):
                        turn_probs(u)
                    if u >= 1:
                        values(u - 1)
                return s["out_ready"], nth("unit", "A", l, r, len(units) - 1)

            def phase_b(l):
                for what, name in B_STEPS:
                    parts = groups(l) if name[0] == "q" else GROUPS
                    if what == "gemm":
                        gemm(("in", l, B_PARTS[name]), ("B", l, name), parts)
                        continue
                    key = ("B", l, name, what)
                    src = b_k[:] if name == "k" else b_q[:, int(name[1])] if name[0] == "q" else b_vt[:]
                    weight = {"ms": means, "rot": rot, "swap": swap, "turn": None}[what]
                    if what == "turn":
                        wait(freed("B", l, name))
                    elif what == "ms":
                        wait((s["sq_ready"], nth("bn", l, name)))
                        src = b_tmp[B_NORMED.index(name) % 2]
                    elif what == "rot":
                        wait((s["headnorm_ready"], nth("bn", l, name)))
                        parts = GROUPS[:2]
                    else:
                        wait((s["rope_ready"], nth("bn", l, name)))
                    wait(before(*key))
                    if what == "turn":
                        for i in range(NT):
                            last = turn(slot(*key)[:, P * i:P * i + P], src[:, P * i:P * i + P])
                    else:
                        for t0, tn in parts:
                            last = pe.matmul(slot(*key)[:, t0:t0 + tn], weight[:], src[:, t0:t0 + tn],
                                             start=True, stop=True)
                    fill(last, *key)
                nq = q_tiles(l)
                units = [(h, i) for h in range(6) for i in range(nq)]

                def scores(u):
                    h, i = units[u]
                    key = ("B", l, u)
                    if u == 0:
                        wait((s["rope_ready"], nth("bn", l, "q2")))
                        wait((s["kz_ready"], 6 * (l + 1)))
                    wait(before(*key))
                    acc = slot(*key)
                    for t0, tn in (GROUPS if i < NTL else GROUPS[2:]):
                        last = pe.matmul(acc[:, t0:t0 + tn], b_q[:, h // 2, P * i:P * i + P],
                                         b_kz[:, h // 3, h % 2, t0:t0 + tn], start=True, stop=True)
                    fill(last, *key)

                def turn_probs(u):
                    h, i = units[u]
                    key = ("B", l, u)
                    n_unit = nth("unit", *key)
                    key = (*key, "turned")
                    wait((s["probs_ready"], n_unit))
                    wait(before(*key))
                    for b in range(0 if i < NTL else NTL, NT):
                        last = turn(slot(*key)[:, P * b:P * b + P], b_p(n_unit)[:, b, :])
                    fill(last, *key)

                def values(u):
                    h, i = units[u]
                    key = ("B", l, u)
                    pt = b_pt[:, nth("unit", *key) % 2]
                    attend_pv(key, [(pt[:, b, :], b_v[:, b, :]) for b in range(0 if i < NTL else NTL, NT)])

                scores(0)
                for u in range(len(units) + 1):
                    if u + 1 < len(units):
                        scores(u + 1)
                    if u < len(units):
                        turn_probs(u)
                    if u >= 1:
                        values(u - 1)
                return s["out_ready"], nth("unit", "B", l, len(units) - 1)

            def phase_c(l):
                def turn_part(name):
                    key = ("C", l, name, "t")
                    wait(freed("C", l, name))
                    wait(before(*key))
                    for i in range(NT):
                        last = turn(slot(*key)[:, P * i:P * i + P], c_z[:, 2 + int(name[1]), P * i:P * i + P])
                    fill(last, *key)

                for name, col in C_PARTS:
                    gemm(("in", l, col), ("C", l, name), GROUPS)
                    if name in C_TURNED:
                        turn_part(name)
                for n, _ in enumerate(late_tiles(l), n_late(l) - len(late_tiles(l))):
                    wait((s[f"late_landed{n % 3}"], 16 * (n // 3 + 1)))
                    for m in range(ADA_LATE_W // P):
                        at_col = 2 * (ADA_LATE_W // P * (n - n_late(l) + len(late_tiles(l))) + m)
                        last = modulation(at_col, lambda k: ada_late[:, n % 3, k, P * m:P * m + P])
                    last.then_inc(s["late_used"], 1)
                for j in range(4):
                    key = ("C", l, "kd", j)
                    wait((s["kd_ready"], nth("hg", l, j)))
                    wait(before(*key))
                    for i in range(NT):
                        last = turn(slot(*key)[:, P * i:P * i + P], c_w[:, j % 2, 0, P * i:P * i + P])
                    fill(last, *key)
                    wait(freed(*key))
                    key = ("C", l, "D", j)
                    wait(before(*key))
                    kd = c_w[:, j % 2, 1].rearrange("p (c k) -> p c k", k=P)
                    for i in range(NT):
                        for par in range(2):
                            at_col = P * (j % 2) + HD * par
                            last = pe.matmul(slot(*key)[HD * par:HD * par + HD, HD * i:HD * i + HD],
                                             kd[:, i, HD * par:HD * par + HD], c_v[:, i, at_col:at_col + HD],
                                             start=True, stop=True)
                    fill(last, *key)
                for lev in range(len(LEVELS) + 1):
                    diag = lev == len(LEVELS)
                    for tile in range(2):
                        wait((s["lev_ready"], nth("lev", l, lev, tile)))
                        for q, (c0, cn) in enumerate(CHUNK_GROUPS):
                            key = ("C", l, "att", lev, tile, q)
                            wait(before(*key))
                            acc = slot(*key)
                            for par in range(2):
                                rows_ = slice(HD * par, HD * par + HD)
                                for n in range(cn):
                                    t = slice(P * (c0 + n), P * (c0 + n) + P)
                                    qs = c_q[rows_, tile, t] if diag else c_lq[rows_, tile, t]
                                    last = pe.matmul(acc[:, 512 * par + P * n:512 * par + P * n + P],
                                                     c_lk[rows_, tile, t], qs, start=True, stop=True)
                            fill(last, *key)
                for n, i in enumerate(range(q_tiles(l))):
                    if n == 0:
                        wait(freed("C", l, "att", len(LEVELS), 1, len(CHUNK_GROUPS) - 1))
                        wait((s["inter_ready"], 4 * (l + 1)))
                        wait((s["states_ready"], 4 * (l + 1)))
                    done = nth("chunk", l, i)
                    if done > 1:
                        wait((s["c_out_freed"], done - 1))
                    for tile in range(2):
                        for par in range(2):
                            h = 2 * tile + par
                            dst = psum[:, 6 + par, HD * tile:HD * tile + HD]
                            rows_ = slice(HD * par, HD * par + HD)
                            pe.matmul(dst, c_att[:, i, h, :], c_v[:, i, HD * h:HD * h + HD], start=True, stop=False)
                            for way in range(2):
                                last = pe.matmul(dst, c_b[rows_, 2 * way + tile, P * i:P * i + P],
                                                 c_state[rows_, 2 * way + tile, i, :], start=False, stop=(way == 1))
                    last.then_inc(s["c_out_ready"], 1)
                return s["c_out_ready"], nth("chunk", l, q_tiles(l) - 1)

            def phase_o(l):
                for i in range(q_tiles(l)):
                    key = ("O", l, i)
                    wait(before(*key))
                    for k in range(KT):
                        last = turn(slot(*key)[:, P * k:P * k + P], o_tok[:, i, P * k:P * k + P])
                    fill(last, *key)
                for i in range(q_tiles(l) - 2, q_tiles(l)):
                    wait(freed("O", l, i))
                for m in range(KT):
                    last = gemm(("out", l, m), ("W", l, m), groups(l))
                return last

            def phase_post(l, which):
                nq = q_tiles(l)
                for i in range(nq + 2):
                    if i < nq:
                        key = ("y", l, which, i)
                        wait(before(*key))
                        for k in range(KT):
                            last = turn(slot(*key)[:, P * k:P * k + P], y_chan[:, k, P * i:P * i + P])
                        last = fill(last, *key)
                    if i >= 2 and next_h(l, which):
                        last = turn_normed((*next_h(l, which), i - 2))
                return last

            def phase_f(l):
                wait((s["h_ready"], nth("xh", "h2", l, q_tiles(l) - 1)))
                for i in range(NPAIR + 1):
                    if i < NPAIR:
                        for f in (2 * i, 2 * i + 1):
                            for half in range(2):
                                gemm(("up", l, f, half), ("F", l, f, half), groups(l))
                    if i:
                        wait((s["a_ready"], nth("ff", l, 2 * i - 1)))
                        for q in range(2):
                            for m in range(4 * q, 4 * q + 4):
                                last = gemm(("down", l, i - 1, q), ("Y", l, i - 1, m), groups(l), kt=2,
                                            col=P * (m % 4), x_hi=f_hi[:, (i - 1) % 2], x_lo=f_lo[:, (i - 1) % 2])
                return last

            for l in range(DEPTH):
                for r in range(3):
                    end_phase(pe, phase_a(l, r), "A", l, r)
                end_phase(pe, phase_b(l), "B", l)
                end_phase(pe, phase_c(l), "C", l)
                end_phase(pe, phase_o(l), "O", l)
                end_phase(pe, phase_post(l, 0), "post", l, 0)
                end_phase(pe, phase_f(l), "F", l)
                end_phase(pe, phase_post(l, 1), "post", l, 1)

        def blocks_of(ap, h):
            v = ap.rearrange("p (n a h) -> p n a h", a=2, h=h)
            return v[:, :, 0, :], v[:, :, 1, :]

        @block.vector
        def _(dve):
            own = Signal(s["dve_step"])

            def step(ins):
                token = own.on(ins)
                dve.wait_ge(*token)
                return token

            def also(ins):
                return own.on(ins)

            def release(ins, *key):
                ins.then_inc(s[f"freed{plan.use[key] % 2}"], 1)
                return freed(*key)

            def say(name, ins):
                ins.then_inc(s[name], 1)

            also(dve.memset(zeros[:], 0.0))
            step(dve.memset(ones[:], 1.0))
            dve.wait_ge(s["const_landed"], 16 * N_CONSTS)
            also(dve.tensor_copy(masks[:], masks_in[:]))
            dve.wait_ge(s["cond_ready"], 1)
            also(dve.tensor_scalar(head_g[:, 0, :], psum[:, 6, 472:474], QSCALE, None, ALU.mult))
            also(dve.tensor_copy(head_g[:, 1, :], psum[:, 6, 474:476]))
            step(dve.tensor_copy(vec[:], psum[:, 6, 0:456]))
            top_ = stats[:, 0, 0:4]
            step(dve.tensor_tensor(top_, vec[:, 448:452], vec[:, 452:456], ALU.max))
            for l in range(2):
                ins = dve.tensor_tensor(lb[:, 0, 4 * l:4 * l + 4], vec[:, 448 + 4 * l:452 + 4 * l], top_, ALU.subtract)
                say("lb_shifted", ins)
            dve.wait_ge(s["lb_exps"], 1)
            step(dve.tensor_tensor(stats[:, 0, 4:8], lb[:, 0, 0:4], lb[:, 0, 4:8], ALU.add))
            step(dve.reciprocal(stats[:, 0, 8:12], stats[:, 0, 4:8]))
            for l in range(2):
                step(dve.tensor_tensor(lb[:, 0, 4 * l:4 * l + 4], lb[:, 0, 4 * l:4 * l + 4], stats[:, 0, 8:12], ALU.mult))
            step(dve.tensor_tensor(stats[:, 0, 12:16], lb[:, 0, 0:4], lb[:, 0, 4:8], ALU.add))
            step(dve.tensor_tensor(lb[:, 0, 4:8], stats[:, 0, 12:16], lb[:, 0, 0:4], ALU.subtract))
            step(dve.tensor_tensor(lb[:, 0, 0:4], lb[:, 0, 0:4], lb[:, 0, 0:4], ALU.subtract))
            step(dve.tensor_scalar(lb[:, 1], lb[:, 0], LB_FLOOR, None, ALU.max))
            step(dve.tensor_scalar(lb[:, 2], lb[:, 0], -1.0, 1.0, ALU.mult, ALU.add))
            say("lb_args", dve.tensor_scalar(lb[:, 2], lb[:, 2], 1e-19, None, ALU.max))
            dve.wait_ge(s["lb_logs"], 1)
            step(dve.tensor_scalar(lb[:, 1], lb[:, 1], -LN_SHIFT * LN2, None, ALU.add))
            step(dve.tensor_tensor(lb[:, 3], lb[:, 2], lb[:, 1], ALU.subtract))
            dve.wait_ge(s["ada_used"], ADA_FIRST)

            def modulation(l, m0, m1, at_col):
                step(dve.tensor_tensor(
                    mods[:, l, m0:m1], psum[:, 7, at_col:at_col + 2 * (m1 - m0)].rearrange("p (m a) -> p m a", a=2),
                    vec[:, 224 * l + m0:224 * l + m1].unsqueeze(2).broadcast_to([P, m1 - m0, 2]), ALU.add))
                for i in (1, 4):
                    if m0 <= KT * i < m1:
                        last = step(dve.tensor_scalar(mods[:, l, KT * i:KT * i + KT], mods[:, l, KT * i:KT * i + KT],
                                                      1.0, None, ALU.add))
                return last

            last = modulation(0, 0, 2 * KT, 0)
            end_phase(dve, last, "setup")

            def moments(x_ap, key):
                n = nth("stat", *key)
                i = (n - 1) % NT
                w = (n - 1) // NT % 2
                for half in range(2):
                    tok = also(dve.bn_stats(bn[:, i, 6 * half:6 * half + 6], x_ap[:, 512 * half:512 * half + 512]))
                dve.wait_ge(*tok)
                say("mean_ready", dve.bn_aggr(mv[:, w, i, :], bn[:, i, :]))

            def mean_of(key):
                n = nth("stat", *key)
                return mv[:, (n - 1) // NT % 2, (n - 1) % NT, 0:1], rstd[:, (n - 1) // NT % 2, (n - 1) % NT:(n - 1) % NT + 1]

            def normed(dst, src, key):
                mean, r = mean_of(key)
                dve.wait_ge(s["mean_ready"], nth("stat", *key))
                dve.wait_ge(s["rstd_ready"], nth("stat", *key))
                return dve.tensor_scalar(dst, src, mean, r, ALU.subtract, ALU.mult)

            def normed_for_pe(src, key):
                n = nth("xh", *key)
                if n > 2:
                    dve.wait_ge(*full(*XH[n - 3]))
                    dve.wait_ge(s["xh_ready"], n - 2)
                say("xh_ready", normed(n_xh[:, n % 2], src, key))

            def split(key):
                n = nth("xh", *key)
                i = key[-1]
                dve.wait_ge(*freed(*key))
                t = slice(P * i, P * i + P)
                step(dve.tensor_copy(h_hi[:, :, t], n_t[:, n % 2]))
                say("h_ready", dve.tensor_tensor(h_lo[:, :, t], n_t[:, n % 2], h_hi[:, :, t].bitcast(F32), ALU.subtract))

            for i in range(NT + 2):
                if i < NT:
                    dve.wait_ge(s[f"x_landed{i % 2}"], 16 * (i // 2 + 1))
                    moments(n_xt[:, i % 2], ("h", 0, i))
                if 1 <= i <= NT:
                    normed_for_pe(n_xt[:, (i - 1) % 2], ("h", 0, i - 1))
                if i >= 2:
                    split(("h", 0, i - 2))
            end_phase(dve, (s["h_ready"], nth("xh", "h", 0, NT - 1)), "h0")

            def copied_max(dst, src, top_):
                return dve.tensor_tensor_reduce(
                    out=dst, in0=src, in1=zeros[:].unsqueeze(1).broadcast_to(list(src.shape)), scale=1.0,
                    scalar=-3e38, op0=ALU.add, op1=ALU.max, accum_out=top_)

            def attend(l, units, key_of, negmax, out_of, value_of):
                def reciprocal_of_sum(u):
                    n = nth("unit", *key_of(u))
                    dve.wait_ge(s["probs_ready"], n)
                    c_ = n % 64
                    return also(dve.reciprocal(stats[:, 2, c_:c_ + 1], stats[:, 2, c_:c_ + 1]))

                def output(u):
                    n = nth("unit", *key_of(u))
                    c_ = n % 64
                    dve.wait_ge(s["out_ready"], n)
                    dve.wait_ge(*sums[u])
                    say("out_freed", dve.tensor_scalar(out_of(u), value_of(u, 6 + n % 2), stats[:, 2, c_:c_ + 1],
                                                       None, ALU.mult))
                sums = {}
                for u in range(len(units) + 2):
                    if u < len(units):
                        negmax(u)
                    if 1 <= u <= len(units):
                        sums[u - 1] = reciprocal_of_sum(u - 1)
                    if u >= 2:
                        output(u - 2)
                return s["out_freed"], nth("unit", *key_of(len(units) - 1))

            def phase_a(l, r):
                say("a_zeroed", dve.memset(a_q[HD:P, 0], 0.0))
                say("a_zeroed", dve.memset(a_q[0:HD, 1], 0.0))
                for hh in range(2):
                    key = ("A", l, r, "bias", hh)
                    dve.wait_ge(*full(*key))
                    dve.wait_ge(*release(dve.tensor_tensor(
                        a_bias[:, hh], slot(*key)[:, 0:BIAS_BLOCKS * GRID_W].rearrange("p (b n) -> p b n", n=GRID_W),
                        a_mask[:].unsqueeze(1).broadcast_to([P, BIAS_BLOCKS, GRID_W]), ALU.add), *key))
                    also(dve.memset(a_bias[0:GRID_W, hh, BIAS_BLOCKS - 1], NEVER))
                    step(dve.memset(a_bias[GRID_W:P, hh, BIAS_BLOCKS - 9], NEVER))
                units = [(hh, p) for hh in range(2) for p in range(q_tiles(l))]

                def key_of(u):
                    return ("A", l, r, u)

                def negmax(u):
                    hh, p = units[u]
                    n = nth("unit", *key_of(u))
                    c_ = n % 64
                    acc = slot(*key_of(u))
                    dve.wait_ge(*full(*key_of(u)))
                    if u >= 2:
                        dve.wait_ge(*full(*key_of(u - 2), "turned"))
                    w = 0
                    if p < NTL:
                        _, rows_, block_ = ROW_PAIRS[p]
                        w = 64 * rows_
                        bias_of = a_bias[:, hh].rearrange("p b n -> p (b n)")
                        also(dve.tensor_tensor_reduce(
                            out=a_p[:, n % 2, 0:w], in0=acc[:, 0:w], in1=bias_of[:, 64 * block_:64 * block_ + w],
                            scale=1.0, scalar=-3e38, op0=ALU.add, op1=ALU.max, accum_out=stats[:, 0, c_:c_ + 1]))
                    dve.wait_ge(*release(copied_max(
                        a_p[:, n % 2, w:w + CTX].rearrange("p (b n) -> p b n", n=P),
                        acc[:, 576:832].rearrange("p (b n) -> p b n", n=P), stats[:, 1, c_:c_ + 1]),
                                         *key_of(u)))
                    top_ = stats[:, 0, c_:c_ + 1] if p < NTL else stats[:, 1, c_:c_ + 1]
                    say("negmax_ready", dve.tensor_scalar(stats[:, 1, c_:c_ + 1], stats[:, 1, c_:c_ + 1],
                                                          top_, -1.0, ALU.max, ALU.mult))

                def out_of(u):
                    hh, p = units[u]
                    return o_tok[:, p, HD * (2 * r + hh):HD * (2 * r + hh) + HD]

                def value_of(u, bank):
                    return psum[:, bank, HD * units[u][0]:HD * units[u][0] + HD]
                return attend(l, units, key_of, negmax, out_of, value_of)

            def phase_b(l):
                for k, name in enumerate(B_NORMED):
                    tmp = b_tmp[k % 2]
                    src = b_k[:] if name == "k" else b_q[:, int(name[1])]
                    w = T if name == "k" or q_tiles(l) == NT else LAT
                    n = nth("bn", l, name)
                    dve.wait_ge(*freed("B", l, name))
                    dve.wait_ge(s["act_headrstd"], n)
                    gain = head_g[:, int(name == "k"), l:l + 1]
                    say("headnorm_ready", dve.scalar_tensor_tensor(out=src[:, 0:w], in0=src[:, 0:w], scalar=gain,
                                                                   in1=tmp[:, 0:w], op0=ALU.mult, op1=ALU.mult))
                    dve.wait_ge(s["headnorm_ready"], n)
                    if name == "k":
                        dve.wait_ge(s["rope_landed"], 32 * (l + 1))
                    step(dve.tensor_tensor(tmp[:, 0:LAT], src[:, 0:LAT], b_cos[:], ALU.mult))
                    dve.wait_ge(*full("B", l, name, "rot"))
                    dve.wait_ge(*release(dve.tensor_tensor(src[:, 0:LAT], slot("B", l, name, "rot")[:, 0:LAT], b_sin[:],
                                                           ALU.mult), "B", l, name, "rot"))
                    say("rope_ready", dve.tensor_tensor(src[:, 0:LAT], src[:, 0:LAT], tmp[:, 0:LAT], ALU.add))
                dve.wait_ge(s["rope_ready"], nth("bn", l, B_NORMED[-1]))
                for kv in range(2):
                    other = slice(HD * (1 - kv), HD * (1 - kv) + HD)
                    own_ = slice(HD * kv, HD * kv + HD)
                    also(dve.memset(b_kz[other, kv, kv], 0.0))
                    also(dve.memset(b_kz[own_, kv, 1 - kv], 0.0))
                    tok = step(dve.tensor_copy(b_kz[own_, kv, kv], b_k[own_]))
                    dve.sem_inc(s["kz_ready"], 2)
                units = [(h, i) for h in range(6) for i in range(q_tiles(l))]

                def key_of(u):
                    return ("B", l, u)

                def negmax(u):
                    h, i = units[u]
                    n = nth("unit", *key_of(u))
                    c_ = n % 64
                    dve.wait_ge(*full(*key_of(u)))
                    if u >= 2:
                        dve.wait_ge(*full(*key_of(u - 2), "turned"))
                    blocks = slice(0 if i < NTL else NTL, NT)
                    acc = slot(*key_of(u))[:, 0:T].rearrange("p (b n) -> p b n", n=P)[:, blocks, :]
                    dve.wait_ge(*release(copied_max(b_p(n)[:, blocks, :], acc, stats[:, 0, c_:c_ + 1]), *key_of(u)))
                    say("negmax_ready", dve.tensor_scalar(stats[:, 1, c_:c_ + 1], stats[:, 0, c_:c_ + 1], -1.0, None,
                                                          ALU.mult))

                def out_of(u):
                    h, i = units[u]
                    return o_tok[:, i, HD * (6 + h):HD * (7 + h)]

                def value_of(u, bank):
                    return psum[:, bank, HD * (units[u][0] // 3):HD * (units[u][0] // 3) + HD]
                return attend(l, units, key_of, negmax, out_of, value_of)

            def phase_c(l):
                dve.wait_ge(*freed("C", l, "q1"))
                dve.wait_ge(*freed("C", l, "q0"))

                def gates_1(j):
                    dve.wait_ge(s["gate_l"], nth("hg", l, j))
                    w = c_w[:, j % 2]
                    also(dve.scalar_tensor_tensor(out=w[:, 1], in0=c_z[:, j], scalar=0.0, in1=w[:, 0], op0=ALU.min,
                                                  op1=ALU.subtract))
                    say("gate_m", dve.scalar_tensor_tensor(out=w[:, 2], in0=c_z[:, j], scalar=0.0, in1=w[:, 0],
                                                           op0=ALU.max, op1=ALU.add))

                def gates_2(j):
                    w = c_w[:, j % 2]
                    way = j // 2
                    dve.wait_ge(s["gate_k"], nth("hg", l, j))
                    step(dve.tensor_scalar(w[:, 1], w[:, 1], lb[:, 2, 4 * l + j:4 * l + j + 1],
                                           lb[:, 1, 4 * l + j:4 * l + j + 1], ALU.add, ALU.max))
                    step(dve.tensor_tensor(c_z[:, j], w[:, 1], w[:, 3], ALU.add))
                    for i in range(NT):
                        src, dst = c_z[:, j, P * i:P * i + P], c_b[:, j, P * i:P * i + P]
                        if way:
                            src, dst = src[:, ::-1], dst[:, ::-1]
                        ins = dve.tensor_tensor_scan(dst, ones[:], src, 0.0, ALU.mult, ALU.add)
                        also(ins) if i < NT - 1 else say("b_ready", ins)

                gates_1(0)
                for j in range(4):
                    if j < 3:
                        gates_1(j + 1)
                    gates_2(j)

                def chunks(ap):
                    return ap.rearrange("p (c t) -> p c t", t=P)

                def end_of(j):
                    return chunks(c_b[:, j])[:, :, P - 1:P] if j < 2 else chunks(c_b[:, j])[:, :, 0:1]

                def to_end(j):
                    dve.wait_ge(s["b_ready"], nth("hg", l, 3))
                    if j >= 2:
                        dve.wait_ge(*full("C", l, "kd", j - 2))
                    w = chunks(c_w[:, j % 2, 0])
                    say("el_args", dve.tensor_tensor(w, end_of(j).broadcast_to([P, NT, P]), chunks(c_b[:, j]),
                                                     ALU.subtract))
                    dve.wait_ge(s["el_ready"], nth("hg", l, j))
                    say("kd_ready", dve.tensor_tensor(c_w[:, j % 2, 0], c_w[:, j % 2, 0], c_k[:, j], ALU.mult))

                def states(j):
                    order = [8, 9] + list(range(8)) if j < 2 else list(range(9, -1, -1))
                    step(dve.memset(c_state[:, j, order[0], :], 0.0))
                    dve.wait_ge(*full("C", l, "D", j))
                    for now, then in zip(order[:-1], order[1:]):
                        ins = dve.scalar_tensor_tensor(
                            out=c_state[:, j, then, :], in0=c_state[:, j, now, :], scalar=c_el[:, j, now:now + 1],
                            in1=slot("C", l, "D", j)[:, HD * now:HD * now + HD], op0=ALU.mult, op1=ALU.add)
                        if then != order[-1]:
                            step(ins)
                        else:
                            token = release(ins, "C", l, "D", j)
                    dve.wait_ge(*token)
                    dve.sem_inc(s["states_ready"], 1)

                for j in range(5):
                    if j < 4:
                        to_end(j)
                    if j >= 1:
                        states(j - 1)

                dve.wait_ge(s["late_used"], n_late(l))
                modulation(l, 2 * KT, MODS, 0)
                if l < DEPTH - 1:
                    modulation(l + 1, 0, 2 * KT, 2 * (MODS - 2 * KT))
                levels = [(lev, tile) for lev in range(len(LEVELS) + 1) for tile in range(2)]

                def level_args(n):
                    lev, tile = levels[n]
                    if n >= 2:
                        dve.wait_ge(*full("C", l, "att", lev - 1, tile, len(CHUNK_GROUPS) - 1))
                    else:
                        for j in (2, 3):
                            dve.wait_ge(*full("C", l, "D", j))
                    if lev == len(LEVELS):
                        return
                    h = LEVELS[lev]
                    bf1, bf2 = blocks_of(c_b[:, tile], h)
                    bb1, bb2 = blocks_of(c_b[:, 2 + tile], h)
                    q1, q2 = blocks_of(c_lq[:, tile], h)
                    k1, k2 = blocks_of(c_lk[:, tile], h)
                    shape = [P, T // (2 * h), h]
                    mid_f = bf1[:, :, h - 1:h].broadcast_to(shape)
                    mid_b = bb2[:, :, 0:1].broadcast_to(shape)
                    also(dve.tensor_tensor(q2, bf2, mid_f, ALU.subtract))
                    also(dve.tensor_tensor(q1, bb1, mid_b, ALU.subtract))
                    also(dve.tensor_tensor(k1, mid_f, bf1, ALU.subtract))
                    say("lev_args", dve.tensor_tensor(k2, mid_b, bb2, ALU.subtract))

                def level_operands(n):
                    lev, tile = levels[n]
                    if lev == len(LEVELS):
                        say("lev_ready", dve.tensor_tensor(c_lk[:, tile], c_k[:, tile], c_k[:, 2 + tile], ALU.add))
                        return
                    h = LEVELS[lev]
                    dve.wait_ge(s["lev_exps"], nth("levx", l, lev, tile))
                    k1, k2 = blocks_of(c_lk[:, tile], h)
                    kf1, _ = blocks_of(c_k[:, tile], h)
                    _, kb2 = blocks_of(c_k[:, 2 + tile], h)
                    also(dve.tensor_tensor(k1, k1, kf1, ALU.mult))
                    also(dve.tensor_tensor(k2, k2, kb2, ALU.mult))
                    say("lev_ready", dve.tensor_tensor(c_lq[:, tile], c_lq[:, tile], c_q[:, tile], ALU.mult))

                def level_masked(n):
                    lev, tile = levels[n]
                    for q, (c0, cn) in enumerate(CHUNK_GROUPS):
                        key = ("C", l, "att", lev, tile, q)
                        dve.wait_ge(*full(*key))
                        if lev:
                            dve.wait_ge(*freed("C", l, "att", lev - 1, tile, q))
                        src = slot(*key)[:, 0:1024].rearrange("p (h c t) -> p h c t", h=2, t=P)[:, :, 0:cn, :]
                        dst = c_att[:, c0:c0 + cn, 2 * tile:2 * tile + 2, :].rearrange("p c h t -> p h c t")
                        mask = masks[:, lev, :].unsqueeze(1).unsqueeze(1).broadcast_to([P, 2, cn, P])
                        release(dve.copy_predicated(out=dst, mask=mask, data=src), *key)

                for n in range(len(levels) + 1):
                    if n < len(levels):
                        level_args(n)
                    if n >= 1:
                        level_masked(n - 1)
                    if n < len(levels):
                        level_operands(n)
                for j in range(4):
                    dve.wait_ge(s["inter_exps"], nth("hg", l, j))
                    say("inter_ready", dve.tensor_tensor(c_b[:, j], c_b[:, j], c_q[:, j % 2], ALU.mult))
                gated = step(dve.tensor_tensor(
                    c_g[:].rearrange("p c (h v) -> p (c h) v", v=HD), c_g[:].rearrange("p c (h v) -> p (c h) v", v=HD),
                    hgn[:, l, :].unsqueeze(1).broadcast_to([P, 4 * NT, HD]), ALU.mult))

                def read_out(i):
                    n = nth("chunk", l, i)
                    dve.wait_ge(s["c_out_ready"], n)
                    say("c_out_freed", dve.tensor_copy(
                        c_o[:, n % 2].rearrange("p (t a v) -> p a t v", a=2, v=HD),
                        psum[:, 6:8, 0:P].rearrange("p a (t v) -> p a t v", v=HD)))
                    dve.wait_ge(s["c_out_freed"], n)
                    step(dve.tensor_tensor(c_o2[:, n % 2], c_o[:, n % 2], c_o[:, n % 2], ALU.mult))
                    say("ms_ready", dve.tensor_reduce(c_ms[:, 0, i, :], c_o2[:, n % 2].rearrange(
                        "p (h v) -> p h v", v=HD), AX, ALU.add))
                    dve.wait_ge(s["ms_ready"], n)

                def gate_out(i):
                    n = nth("chunk", l, i)
                    dve.wait_ge(s["hg_rstd"], n)
                    step(dve.tensor_tensor(
                        c_o2[:, n % 2].rearrange("p (h v) -> p h v", v=HD), c_o[:, n % 2].rearrange(
                            "p (h v) -> p h v", v=HD),
                        c_ms[:, 1, i, :].unsqueeze(2).broadcast_to([P, 4, HD]), ALU.mult))
                    return also(dve.tensor_tensor(o_tok[:, i, D - 2 * P:D], c_o2[:, n % 2], c_g[:, i, :], ALU.mult))

                nq = q_tiles(l)
                for i in range(nq + 1):
                    if i < nq:
                        read_out(i)
                    if i >= 1:
                        last = gate_out(i - 1)
                        dve.wait_ge(*last)
                return last

            def phase_o(l):
                for i in range(q_tiles(l)):
                    dve.wait_ge(s["o_hi_ready"], nth("osplit", l, i))
                    t = slice(P * i, P * i + P)
                    last = release(dve.tensor_tensor(
                        h_lo[:, :, t], slot("O", l, i)[:, 0:D].rearrange("p (k n) -> p k n", n=P),
                        h_hi[:, :, t].bitcast(F32), ALU.subtract), "O", l, i)
                return last

            def phase_post(l, which):
                nq = q_tiles(l)
                after = next_h(l, which)
                last = None
                dve.wait_ge(s["ln_landed"], 32 * (2 * l + which + 1))

                def post(i):
                    return nth("post", l, which, i)

                for i in range(nq + 4):
                    if i < nq:
                        n = post(i)
                        key = ("y", l, which, i)
                        k = NT + n - 1
                        dve.wait_ge(s[f"x_landed{k % 2}"], 16 * (k // 2 + 1))
                        dve.wait_ge(*full(*key))
                        if i >= 2:
                            dve.wait_ge(s["x1_ready"], n - 2)
                        dve.wait_ge(*release(dve.scalar_tensor_tensor(
                            out=n_r[:, n % 2], in0=n_xt[:, k % 2], scalar=ALPHA, in1=slot(*key)[:, 0:D],
                            op0=ALU.mult, op1=ALU.add), *key))
                        moments(n_r[:, n % 2], key)
                    if 1 <= i <= nq:
                        n = post(i - 1)
                        r = n_r[:, n % 2]
                        step(normed(r, r, ("y", l, which, i - 1)))
                        step(dve.tensor_tensor(r, r, n_g[:], ALU.mult))
                        if n > 2:
                            dve.wait_ge(s[f"x1_stored{(n - 1) % 2}"], 16 * ((n - 1) // 2))
                        if after and i >= 3:
                            dve.wait_ge(s["xh_ready"], nth("xh", *after, i - 3))
                        say("x1_ready", dve.tensor_tensor(n_x1[:, (n - 1) % 2], r, n_b[:], ALU.add))
                        dve.wait_ge(s["x1_ready"], n)
                        if after:
                            moments(n_x1[:, (n - 1) % 2], (*after, i - 1))
                    if after and 2 <= i <= nq + 1:
                        n = post(i - 2)
                        normed_for_pe(n_x1[:, (n - 1) % 2], (*after, i - 2))
                    if after and i >= 4:
                        split((*after, i - 4))
                for k in range(2):
                    n = sum(1 for m in range(post(nq - 1)) if m % 2 == k)
                    dve.wait_ge(s[f"x1_stored{k}"], 16 * n)
                if after:
                    return s["h_ready"], nth("xh", *after, nq - 1)
                return s["x1_ready"], post(nq - 1)

            def phase_f(l):
                ctx_too = q_tiles(l) == NT

                def conv(f, half):
                    key = ("F", l, f, half)
                    w = f_t[:, half]
                    acc = slot(*key)
                    dve.wait_ge(s["conv_start"], nth("conv", l, f, half))
                    parts = [(0, LAT)] + [(LAT, T)] * ctx_too
                    for j in (0, 2):
                        at_col = 224 * l + MODS + 2 * FT * j + FT * half + f
                        for a, b in parts:
                            dst, src = (w[:, a + 1:b], acc[:, a:b - 1]) if j == 0 else (w[:, a:b - 1], acc[:, a + 1:b])
                            ins = dve.scalar_tensor_tensor(out=dst, in0=src, scalar=vec[:, at_col:at_col + 1], in1=dst,
                                                           op0=ALU.mult, op1=ALU.add)
                            if (j, b) == (2, parts[-1][1]):
                                dve.wait_ge(*release(ins, *key))
                            elif b == parts[-1][1]:
                                step(ins)
                            else:
                                also(ins)

                w = T if ctx_too else LAT
                for i in range(NPAIR + 1):
                    if i < NPAIR:
                        for f in (2 * i, 2 * i + 1):
                            conv(f, 0)
                            conv(f, 1)
                            dve.wait_ge(s["silu_done"], nth("ff", l, f))
                            step(dve.tensor_tensor(f_t[:, 0, 0:w], f_t[:, 0, 0:w], f_t[:, 1, 0:w], ALU.mult))
                            hi, lo = f_hi[:, i % 2, f % 2, 0:w], f_lo[:, i % 2, f % 2, 0:w]
                            if i >= 2:
                                dve.wait_ge(*full("Y", l, i - 2, KT - 1))
                            step(dve.tensor_copy(hi, f_t[:, 0, 0:w]))
                            say("a_ready", dve.tensor_tensor(lo, f_t[:, 0, 0:w], hi.bitcast(F32), ALU.subtract))
                    if i:
                        for m in range(KT):
                            key = ("Y", l, i - 1, m)
                            dve.wait_ge(*full(*key))
                            parts = [(0, LAT, 0)] + [(LAT, T, 1)] * ctx_too
                            if i > 1:
                                dve.wait_ge(*freed("Y", l, i - 2, m))
                            for a, b, who in parts:
                                gate = mods[:, l, KT * 5 + m, who:who + 1]
                                if i == 1:
                                    ins = dve.tensor_scalar(y_chan[:, m, a:b], slot(*key)[:, a:b], gate, None, ALU.mult)
                                else:
                                    ins = dve.scalar_tensor_tensor(
                                        out=y_chan[:, m, a:b], in0=slot(*key)[:, a:b], scalar=gate,
                                        in1=y_chan[:, m, a:b], op0=ALU.mult, op1=ALU.add)
                                if b == parts[-1][1]:
                                    last = release(ins, *key)
                                else:
                                    also(ins)
                return last

            for l in range(DEPTH):
                for r in range(3):
                    end_phase(dve, phase_a(l, r), "A", l, r)
                end_phase(dve, phase_b(l), "B", l)
                end_phase(dve, phase_c(l), "C", l)
                end_phase(dve, phase_o(l), "O", l)
                end_phase(dve, phase_post(l, 0), "post", l, 0)
                end_phase(dve, phase_f(l), "F", l)
                end_phase(dve, phase_post(l, 1), "post", l, 1)

        @block.scalar
        def _(act):
            own = Signal(s["act_step"])

            def step(ins):
                token = own.on(ins)
                act.wait_ge(*token)
                return token

            def release(ins, *key):
                ins.then_inc(s[f"freed{plan.use[key] % 2}"], 1)
                return freed(*key)

            def say(name, ins):
                ins.then_inc(s[name], 1)

            def copy(dst, src, scale=1.0):
                return act.activation(dst, src, ACT.Copy, scale=scale)

            act.wait_ge(s["rows_turned"], 1)
            say("cond_ready", act.activation(cond[:], psum[:, 6, 456:472].rearrange("p (a k) -> p k a", a=2), ACT.Silu))
            act.preload_act_table_set(LN_EXP_SET)
            act.wait_ge(s["lb_shifted"], 2)
            say("lb_exps", act.activation(lb[:, 0], lb[:, 0], ACT.Exp))
            act.wait_ge(s["lb_args"], 1)
            step(act.activation(lb[:, 1], lb[:, 1], ACT.Ln, scale=float(2 ** LN_SHIFT)))
            say("lb_logs", act.activation(lb[:, 2], lb[:, 2], ACT.Ln))
            end_phase(act, (s["lb_logs"], 1), "setup")

            def rstd_of(key):
                n = nth("stat", *key)
                w, i = (n - 1) // NT % 2, (n - 1) % NT
                act.wait_ge(s["mean_ready"], n)
                r = rstd[:, w, i:i + 1]
                step(act.activation(r, mv[:, w, i, 1:2], ACT.Ln, bias=EPS))
                say("rstd_ready", act.activation(r, r, ACT.Exp, scale=-0.5))

            def modulated(key):
                n = nth("xh", *key)
                i = key[-1]
                l, first = (key[1], 3 * KT) if key[0] == "h2" else (key[1], 0)
                who = 0 if i < NTL else 1
                act.wait_ge(*full(*key))
                if n > 2:
                    act.wait_ge(s["h_ready"], n - 2)
                for k in range(KT):
                    ins = act.activation(n_t[:, n % 2, k], slot(*key)[:, P * k:P * k + P], ACT.Identity,
                                         bias=mods[:, l, first + k, who:who + 1],
                                         scale=mods[:, l, first + KT + k, who:who + 1])
                    if k < KT - 1:
                        own.on(ins)
                    else:
                        last = release(ins, *key)
                return last

            for i in range(NT + 2):
                if i < NT:
                    rstd_of(("h", 0, i))
                if i >= 2:
                    last = modulated(("h", 0, i - 2))
            end_phase(act, last, "h0")

            def attend(units, key_of, probs, turned):
                for u in range(len(units) + 1):
                    if u < len(units):
                        probs(u)
                    if u >= 1:
                        n = nth("unit", *key_of(u - 1))
                        act.wait_ge(*full(*key_of(u - 1), "turned"))
                        if n > 2:
                            act.wait_ge(s["out_ready"], n - 2)
                        last = turned(u - 1)
                return last

            def phase_a(l, r):
                key = ("A", l, r, "q")
                w = P * q_tiles(l)
                act.wait_ge(*full(*key))
                own.on(copy(a_q[0:HD, 0, 0:w], slot(*key)[0:HD, 0:w], QSCALE))
                release(copy(a_q[HD:P, 1, 0:w], slot(*key)[HD:P, 0:w], QSCALE), *key)
                for name, dst in (("k", a_k), ("v", a_vt)):
                    key = ("A", l, r, name)
                    act.wait_ge(*full(*key))
                    release(copy(dst[:], slot(*key)[:, 0:T]), *key)
                key = ("A", l, r, "vt")
                act.wait_ge(*full(*key))
                release(copy(a_v[:].rearrange("p c v -> p (c v)"), slot(*key)[:, 0:T]), *key)
                units = [(hh, p) for hh in range(2) for p in range(q_tiles(l))]

                def key_of(u):
                    return ("A", l, r, u)

                def probs(u):
                    hh, p = units[u]
                    n = nth("unit", *key_of(u))
                    c_ = n % 64
                    act.wait_ge(s["negmax_ready"], n)
                    w = CTX + (GRID_W * ROW_PAIRS[p][1] if p < NTL else 0)
                    say("probs_ready", act.activation(a_p[:, n % 2, 0:w], a_p[:, n % 2, 0:w], ACT.Exp,
                                                      bias=stats[:, 1, c_:c_ + 1], accum_out=stats[:, 2, c_:c_ + 1]))

                def turned(u):
                    hh, p = units[u]
                    key = key_of(u)
                    n = nth("unit", *key)
                    dst = a_pt[:, n % 2].rearrange("p b t -> p (b t)")
                    key = (*key, "turned")
                    acc = slot(*key)
                    if p >= NTL:
                        return release(copy(dst[:, 512:768], acc[:, 512:768]), *key)
                    if ROW_PAIRS[p][1] > WIN_R:
                        own.on(copy(dst[0:64, 768:896], acc[0:64, 768:896]))
                    return release(copy(dst[:, 0:768], acc[:, 0:768]), *key)
                return attend(units, key_of, probs, turned)

            def phase_b(l):
                def part(name):
                    return {"k": b_k[:], "v": b_vt[:]}.get(name) if name in "kv" else b_q[:, int(name[1])]

                def width(name):
                    return T if name in "kv" else P * q_tiles(l)

                def take(name):
                    key = ("B", l, name)
                    w = width(name)
                    act.wait_ge(*full(*key))
                    release(copy(part(name)[:, 0:w], slot(*key)[:, 0:w]), *key)
                    if name != "v":
                        act.wait_ge(*freed(*key))

                def square(name):
                    k = B_NORMED.index(name)
                    w = width(name)
                    if k >= 2:
                        act.wait_ge(s["rope_ready"], nth("bn", l, B_NORMED[k - 2]))
                    say("sq_ready", act.activation(b_tmp[k % 2][:, 0:w], part(name)[:, 0:w], ACT.Square))

                def head_rstd(name):
                    w = width(name)
                    tmp = b_tmp[B_NORMED.index(name) % 2]
                    key = ("B", l, name, "ms")
                    act.wait_ge(*full(*key))
                    act.wait_ge(*release(act.activation(tmp[:, 0:w], slot(*key)[:, 0:w], ACT.Ln, bias=EPS), *key))
                    say("act_headrstd", act.activation(tmp[:, 0:w], tmp[:, 0:w], ACT.Exp, scale=-0.5))

                take("k")
                square("k")
                take("v")
                take("q0")
                key = ("B", l, "v", "turn")
                act.wait_ge(*full(*key))
                release(copy(b_v[:].rearrange("p c v -> p (c v)"), slot(*key)[:, 0:T]), *key)
                square("q0")
                head_rstd("k")
                take("q1")
                square("q1")
                head_rstd("q0")
                take("q2")
                square("q2")
                head_rstd("q1")
                head_rstd("q2")
                key = ("B", l, "k", "swap")
                act.wait_ge(*full(*key))
                act.wait_ge(s["rope_ready"], nth("bn", l, B_NORMED[-1]))
                own.on(copy(b_kz[HD:P, 0, 1], slot(*key)[HD:P, 0:T]))
                act.wait_ge(*release(copy(b_kz[0:HD, 1, 0], slot(*key)[0:HD, 0:T]), *key))
                act.sem_inc(s["kz_ready"], 2)
                units = [(h, i) for h in range(6) for i in range(q_tiles(l))]

                def key_of(u):
                    return ("B", l, u)

                def blocks(u):
                    return slice(0 if units[u][1] < NTL else NTL, NT)

                def probs(u):
                    n = nth("unit", *key_of(u))
                    c_ = n % 64
                    act.wait_ge(s["negmax_ready"], n)
                    p = b_p(n)[:, blocks(u), :]
                    say("probs_ready", act.activation(p, p, ACT.Exp, bias=stats[:, 1, c_:c_ + 1], accum_out=stats[:, 2, c_:c_ + 1]))

                def turned(u):
                    n = nth("unit", *key_of(u))
                    key = (*key_of(u), "turned")
                    src = slot(*key)[:, 0:T].rearrange("p (b n) -> p b n", n=P)
                    return release(copy(b_pt[:, n % 2, blocks(u), :], src[:, blocks(u), :]), *key)
                return attend(units, key_of, probs, turned)

            def phase_c(l):
                for name, _ in C_PARTS:
                    j = int(name[1])
                    key = ("C", l, name)
                    dst = {"i": lambda: c_z[:, 2 + j], "g": lambda: c_z[:, 2 + j], "f": lambda: c_z[:, j],
                           "b": lambda: c_z[:, 2 + j], "q": lambda: c_q[:, j]}[name[0]]()
                    act.wait_ge(*full(*key))
                    release(copy(dst, slot(*key)[:, 0:T], QSCALE if name[0] == "q" else 1.0), *key)
                    if name in C_TURNED:
                        key = ("C", l, name, "t")
                        act.wait_ge(*full(*key))
                        to = (c_v if name[0] == "i" else c_g)[:, :, P * j:P * j + P]
                        src = slot(*key)[:, 0:T].rearrange("p (c v) -> p c v", v=P)
                        release(copy(to, src) if name[0] == "i" else act.activation(to, src, ACT.Silu), *key)
                act.preload_act_table_set(LN_EXP_SET)
                for name in ("q0", "q1"):
                    act.wait_ge(*freed("C", l, name))

                def gates_1(j):
                    w = c_w[:, j % 2]
                    if j >= 2:
                        act.wait_ge(s["b_ready"], nth("hg", l, j - 2))
                    step(act.activation(w[:, 0], c_z[:, j], ACT.Abs))
                    step(act.activation(w[:, 0], w[:, 0], ACT.Exp, scale=-1.0))
                    say("gate_l", act.activation(w[:, 0], w[:, 0], ACT.Ln, bias=1.0))

                def gates_2(j):
                    w = c_w[:, j % 2]
                    c_ = slice(4 * l + j, 4 * l + j + 1)
                    act.wait_ge(s["gate_m"], nth("hg", l, j))
                    own.on(act.activation(c_k[:, j], w[:, 2], ACT.Exp, scale=-1.0, bias=lb[:, 2, c_]))
                    step(act.activation(w[:, 3], w[:, 1], ACT.Abs, bias=lb[:, 3, c_]))
                    step(act.activation(w[:, 3], w[:, 3], ACT.Exp, scale=-1.0))
                    say("gate_k", act.activation(w[:, 3], w[:, 3], ACT.Ln, bias=1.0))

                gates_1(0)
                for j in range(4):
                    if j < 3:
                        gates_1(j + 1)
                    gates_2(j)

                def decays(j):
                    act.wait_ge(s["el_args"], nth("hg", l, j))
                    b = c_b[:, j].rearrange("p (c t) -> p c t", t=P)
                    own.on(act.activation(c_el[:, j, :], b[:, :, P - 1] if j < 2 else b[:, :, 0], ACT.Exp))
                    say("el_ready", act.activation(c_w[:, j % 2, 0], c_w[:, j % 2, 0], ACT.Exp))

                def turned(j):
                    act.wait_ge(*full("C", l, "kd", j))
                    if j >= 2:
                        act.wait_ge(*full("C", l, "D", j - 2))
                    release(copy(c_w[:, j % 2, 1], slot("C", l, "kd", j)[:, 0:T]), "C", l, "kd", j)

                for j in range(5):
                    if j < 4:
                        decays(j)
                    if j >= 1:
                        turned(j - 1)
                for lev in range(len(LEVELS)):
                    for tile in range(2):
                        act.wait_ge(s["lev_args"], nth("levx", l, lev, tile))
                        own.on(act.activation(c_lk[:, tile], c_lk[:, tile], ACT.Exp))
                        say("lev_exps", act.activation(c_lq[:, tile], c_lq[:, tile], ACT.Exp))
                for j in range(4):
                    say("inter_exps", act.activation(c_b[:, j], c_b[:, j], ACT.Exp))
                for i in range(q_tiles(l)):
                    n = nth("chunk", l, i)
                    act.wait_ge(s["ms_ready"], n)
                    step(act.activation(c_ms[:, 1, i, :], c_ms[:, 0, i, :], ACT.Ln, scale=1.0 / HD, bias=EPS))
                    say("hg_rstd", act.activation(c_ms[:, 1, i, :], c_ms[:, 1, i, :], ACT.Exp, scale=-0.5))
                return s["hg_rstd"], nth("chunk", l, q_tiles(l) - 1)

            def phase_o(l):
                for i in range(q_tiles(l)):
                    act.wait_ge(*full("O", l, i))
                    say("o_hi_ready", copy(h_hi[:, :, P * i:P * i + P],
                                           slot("O", l, i)[:, 0:D].rearrange("p (k n) -> p k n", n=P)))
                for m in range(KT):
                    key = ("W", l, m)
                    act.wait_ge(*full(*key))
                    if q_tiles(l) == NT:
                        own.on(act.activation(y_chan[:, m, LAT:T], slot(*key)[:, LAT:T], ACT.Copy,
                                              scale=mods[:, l, 2 * KT + m, 1:2]))
                    last = release(act.activation(y_chan[:, m, 0:LAT], slot(*key)[:, 0:LAT], ACT.Copy,
                                                  scale=mods[:, l, 2 * KT + m, 0:1]), *key)
                return last

            def phase_post(l, which):
                after = next_h(l, which)
                last = None
                nq = q_tiles(l)
                for i in range(nq + 4):
                    if i < nq:
                        rstd_of(("y", l, which, i))
                    if after and 1 <= i <= nq:
                        rstd_of((*after, i - 1))
                    if after and i >= 3 and i - 3 < nq:
                        last = modulated((*after, i - 3))
                return last or (s["rstd_ready"], nth("stat", "y", l, which, nq - 1))

            def phase_f(l):
                w = T if q_tiles(l) == NT else LAT
                for f in range(FT):
                    for half in range(2):
                        key = ("F", l, f, half)
                        act.wait_ge(*full(*key))
                        if f:
                            act.wait_ge(s["a_ready"], nth("ff", l, f - 1))
                        mid, shift = [224 * l + MODS + 2 * FT * j + FT * half + f for j in (1, 3)]
                        say("conv_start", act.activation(f_t[:, half, 0:w], slot(*key)[:, 0:w], ACT.Identity,
                                                         scale=vec[:, mid:mid + 1], bias=vec[:, shift:shift + 1]))
                        if half == 0:
                            act.wait_ge(*freed(*key))
                            say("silu_done", act.activation(f_t[:, 0, 0:w], f_t[:, 0, 0:w], ACT.Silu))
                act.preload_act_table_set(LN_EXP_SET)
                return s["silu_done"], nth("ff", l, FT - 1)

            for l in range(DEPTH):
                for r in range(3):
                    end_phase(act, phase_a(l, r), "A", l, r)
                end_phase(act, phase_b(l), "B", l)
                end_phase(act, phase_c(l), "C", l)
                end_phase(act, phase_o(l), "O", l)
                end_phase(act, phase_post(l, 0), "post", l, 0)
                end_phase(act, phase_f(l), "F", l)
                end_phase(act, phase_post(l, 1), "post", l, 1)


_INS = ["x", "c", "ctx", "c_ctx", "w_ada", "b_ada", "w_in", "w_out", "na_rpb", "q_norm", "k_norm", "hg_lower_bound",
        "hg_norm", "ln1_g", "ln1_b", "w_up", "conv_w", "conv_b", "w_down", "ln2_g", "ln2_b"]


def shape_constants():
    import numpy as np

    lane = np.arange(P)
    eye = np.eye(P, dtype=np.float32)
    rotate = eye[lane ^ 16]
    swap = eye[lane ^ 64]
    flip = eye[lane ^ 63]
    means = ((lane[:, None] // HD == lane[None] // HD) / HD).astype(np.float32)
    masks = np.zeros((P, len(LEVELS) + 1, P), np.float32)
    for n, h in enumerate(LEVELS):
        same = lane[:, None] // (2 * h) == lane[None] // (2 * h)
        masks[:, n] = same & (lane[:, None] // h != lane[None] // h)
    masks[:, len(LEVELS)] = np.eye(P)
    n_freq = HD // 4
    inv_freq = np.float32(10000.0) ** (-np.arange(n_freq, dtype=np.float32) / np.float32(n_freq))
    t = np.arange(LAT)
    pos = np.stack([t // GRID_W, t % GRID_W]).astype(np.float32)
    axis, half, freq = lane % HD // 32, lane % 32 // 16, lane % 16
    angle = (pos[axis] * inv_freq[freq][:, None]).astype(np.float32)
    sign = np.where(half == 0, -1.0, 1.0).astype(np.float32)[:, None]
    window = np.full((P, GRID_W), NEVER, np.float32)
    for w in range(64):
        first = min(max(w - WIN_C // 2, 0), GRID_W - WIN_C)
        window[[w, GRID_W + w], first:first + WIN_C] = 0.0
    return dict(identity=eye, reverse_columns=flip, rotate_halves=rotate, swap_heads=swap, head_means=means, level_masks=masks,
                rope_cos=np.cos(angle), rope_sin=np.sin(angle) * sign, window_mask=window)


def kernel(**inputs):
    import numpy as np
    import concourse.bacc as bacc
    from concourse.bass_utils import run_bass_kernel_spmd

    nc = bacc.Bacc("TRN2", target_bir_lowering=False, num_devices=1)
    arrays, args = {}, {}
    for name, value in [(n, inputs[n]) for n in _INS] + list(shape_constants().items()):
        a = np.ascontiguousarray(value)
        arrays[f"in_{name}_dram"] = a
        args[name] = nc.dram_tensor(f"in_{name}_dram", a.shape, mybir.dt.from_np(a.dtype), kind="ExternalInput").ap()
    out = nc.dram_tensor("out_0_dram", (1, LAT, D), F32, kind="ExternalOutput").ap()
    build(nc, **args, out=out)
    r = run_bass_kernel_spmd(nc, [arrays], core_ids=[0])
    return r.results[0]["out_0_dram"]
```

```python
from contextlib import ExitStack

import concourse.bass as bass
from concourse import mybir

P = 128
D = 1024
KT = D // P
LAT, CTX = 1024, 256
T = LAT + CTX
NT, NTL = T // P, LAT // P
DEPTH = 2
GRID_W, ROWS = 64, LAT // 64
WIN_R, WIN_C = 8, 16
HD = 64
D_FF = 2816
FT = D_FF // P
NPAIR = FT // 2
N_MOD = 6
MODS = N_MOD * KT
ALPHA = (2.0 * DEPTH) ** 0.25
EPS = 1e-6
LB_FLOOR = 1e-30
QSCALE = HD ** -0.5
LN_SHIFT = 40
NEVER = -1e30
LN2 = 0.6931471805599453
COL = dict(a_k=0, a_v=384, b_k=768, b_v=896, c_f=1024, c_b=1280, c_i=1536, a_q=1792, b_q=2176, c_q=2560, c_g=2816)
GROUPS = [(0, 512), (512, 512), (1024, 256)]
LEVELS = [1, 2, 4, 8, 16, 32, 64]
PAD_W = 128
N_RPB = 15
RPB_ROWS = 6 * N_RPB
ROW_PAIRS = []
for _p in range(ROWS // 2):
    _s = [min(max(r - WIN_R // 2, 0), ROWS - WIN_R) for r in (2 * _p, 2 * _p + 1)]
    _n = _s[1] + WIN_R - _s[0]
    ROW_PAIRS.append((_s[0], _n, 14 if _n > WIN_R else _s[0] - 2 * _p + 6))
BIAS_BLOCKS = 14 + 9
B_PARTS = dict(k=COL["b_k"], v=COL["b_v"], q0=COL["b_q"], q1=COL["b_q"] + P, q2=COL["b_q"] + 2 * P)
B_STEPS = [("gemm", "k"), ("gemm", "q0"), ("ms", "k"), ("gemm", "q1"), ("rot", "k"), ("ms", "q0"), ("gemm", "q2"),
           ("rot", "q0"), ("ms", "q1"), ("gemm", "v"), ("rot", "q1"), ("ms", "q2"), ("turn", "v"), ("rot", "q2"),
           ("swap", "k")]
B_NORMED = ["k", "q0", "q1", "q2"]
C_PARTS = [(f"{x}{j}", COL["c_" + x] + P * j) for x in "igfbq" for j in range(2)]
C_TURNED = ("i0", "i1", "g0", "g1")
N_CONSTS = 6 + DEPTH
N_ROWS = 4 * DEPTH + 7
ARENA = 206 * 1024
CHUNK_GROUPS = [(0, 4), (4, 4), (8, 2)]


ADA_FIRST = 2 * D // 512
ADA_LATE_W = 256
LATE_PER_MOD = D // ADA_LATE_W


def late_tiles(l):
    parts = [(l, 2 * D, N_MOD * D)] + [(l + 1, 0, 2 * D)] * (l < DEPTH - 1)
    return [(m, a) for m, first, end in parts for a in range(first, end, ADA_LATE_W)]


def ada_before_keys(l, j):
    return min(13 + 3 * j, len(late_tiles(l)))


def n_late(l):
    return sum(len(late_tiles(m)) for m in range(l + 1))


def q_tiles(l):
    return NT if l < DEPTH - 1 else NTL


def next_h(l, which):
    if which == 0:
        return ("h2", l)
    return ("h", l + 1) if l < DEPTH - 1 else None

F32 = mybir.dt.float32
F32R = mybir.dt.float32r
U8 = mybir.dt.uint8
ALU = mybir.AluOpType
ACT = mybir.ActivationFunctionType
AX = mybir.AxisListType.X
LN_EXP_SET = "natural_log_exp_and_others"


class Signal:

    def __init__(self, sem):
        self.sem, self.n = sem, 0

    def on(self, instruction, by=1):
        instruction.then_inc(self.sem, by)
        self.n += by
        return self.sem, self.n


class Plan:

    def __init__(self):
        self.use, self.tile, self.tiles, self.tile_last = {}, {}, [], []
        for i in range(NT):
            self.slot("h", 0, i)
        for l in range(DEPTH):
            nq = q_tiles(l)
            for r in range(3):
                for name in "qkv":
                    self.gemm(("in", l, COL["a_" + name] + P * r), ("A", l, r, name))
                self.slot("A", l, r, "vt")
                for hh in range(2):
                    self.slot("A", l, r, "bias", hh)
                self.units(2 * nq, "A", l, r)
            for what, name in B_STEPS:
                if what == "gemm":
                    self.gemm(("in", l, B_PARTS[name]), ("B", l, name))
                else:
                    self.slot("B", l, name, what)
            self.units(6 * nq, "B", l)
            for name, col in C_PARTS:
                self.gemm(("in", l, col), ("C", l, name))
                if name in C_TURNED:
                    self.slot("C", l, name, "t")
            for j in range(4):
                self.slot("C", l, "kd", j)
                self.slot("C", l, "D", j)
            for lev in range(len(LEVELS) + 1):
                for tile in range(2):
                    for q in range(len(CHUNK_GROUPS)):
                        self.slot("C", l, "att", lev, tile, q)
            for i in range(nq):
                self.slot("C", l, "out", i)
            for i in range(nq):
                self.slot("O", l, i)
            for m in range(KT):
                self.gemm(("out", l, m), ("W", l, m))
            self.post(l, 0, nq)
            for i in range(NPAIR + 1):
                if i < NPAIR:
                    for f in (2 * i, 2 * i + 1):
                        for half in range(2):
                            self.gemm(("up", l, f, half), ("F", l, f, half))
                if i:
                    for q in range(2):
                        self.gemm(("down", l, i - 1, q), *[("Y", l, i - 1, m) for m in range(4 * q, 4 * q + 4)])
            self.post(l, 1, nq)

    def units(self, n, *phase):
        self.slot(*phase, 0)
        for u in range(n):
            if u + 1 < n:
                self.slot(*phase, u + 1)
            self.slot(*phase, u, "turned")

    def post(self, l, which, n):
        for i in range(n + 3):
            if i < n:
                self.slot("y", l, which, i)
            if i >= 3 and next_h(l, which):
                self.slot(*next_h(l, which), i - 3)

    def slot(self, *key):
        assert key not in self.use, key
        self.use[key] = len(self.use)

    def gemm(self, tile, *uses):
        self.tile[tile] = len(self.tiles)
        self.tiles.append(tile)
        for key in uses:
            self.slot(*key)
        self.tile_last.append(uses[-1])

    def events(self):
        e = {k: [] for k in ("stat", "xh", "unit", "bn", "hg", "lev", "levx", "chunk", "osplit", "post", "conv", "ff")}
        for i in range(NT):
            e["stat"].append(("h", 0, i))
            e["xh"].append(("h", 0, i))
        for l in range(DEPTH):
            nq = q_tiles(l)
            e["unit"] += [("A", l, r, u) for r in range(3) for u in range(2 * nq)]
            e["unit"] += [("B", l, u) for u in range(6 * nq)]
            e["bn"] += [(l, name) for name in B_NORMED]
            e["hg"] += [(l, j) for j in range(4)]
            e["lev"] += [(l, lev, tile) for lev in range(len(LEVELS) + 1) for tile in range(2)]
            e["levx"] += [(l, lev, tile) for lev in range(len(LEVELS)) for tile in range(2)]
            e["chunk"] += [(l, i) for i in range(nq)]
            e["osplit"] += [(l, i) for i in range(nq)]
            e["conv"] += [(l, f, half) for f in range(FT) for half in range(2)]
            e["ff"] += [(l, f) for f in range(FT)]
            for which in range(2):
                after = next_h(l, which)
                for i in range(nq + 2):
                    if i < nq:
                        e["stat"].append(("y", l, which, i))
                        e["post"].append((l, which, i))
                    if i >= 2 and after:
                        e["stat"].append((*after, i - 2))
                if after:
                    e["xh"] += [(*after, i) for i in range(nq)]
        return e


def spread(row):
    return bass.AP(tensor=row.tensor, offset=row.offset, ap=[[0, P], *row.ap])


def build(nc, x, c, ctx, c_ctx, w_ada, b_ada, w_in, w_out, na_rpb, q_norm, k_norm, hg_lower_bound, hg_norm,
          ln1_g, ln1_b, w_up, conv_w, conv_b, w_down, ln2_g, ln2_b,
          identity, reverse_columns, rotate_halves, swap_heads, head_means, level_masks, rope_cos, rope_sin,
          window_mask, out):
    plan = Plan()
    events = plan.events()
    ordinal = {kind: {key: n + 1 for n, key in enumerate(keys)} for kind, keys in events.items()}
    XH = events["xh"]

    def nth(kind, *key):
        return ordinal[kind][key]

    with ExitStack() as stack:
        arena = stack.enter_context(nc.sbuf_tensor("arena", [P, ARENA // 4], F32))
        ARENA_AT = nc.sbuf_base - ARENA
        psum = stack.enter_context(nc.psum_tensor("psum", [P, 8, 512], F32))

        def place(name, shape, offset, dtype=F32):
            size = mybir.dt.size(dtype)
            for n in shape:
                size *= n
            assert offset + size <= ARENA, (name, offset + size)
            return nc.alloc_sbuf_tensor_at(name, [P, *shape], dtype, offset=ARENA_AT + offset)

        H, O, W = 0, 8 * KT * T, 12 * KT * T
        G = W + 6 * KT * P * 4
        C = G + 51200

        h_hi = place("h_hi", [KT, T], H, F32R)
        h_lo = place("h_lo", [KT, T], H + 4 * KT * T, F32R)
        o_tok = place("o_tok", [NT, D], O)
        y_chan = place("y_chan", [KT, T], O)
        w_raw = place("w_raw", [2, KT * P], W)
        w_hi = place("w_hi", [2, KT * P], W + 8 * KT * P, F32R)
        w_lo = place("w_lo", [2, KT * P], W + 16 * KT * P, F32R)

        at = [C]

        def keep(name, shape, dtype=F32):
            t = place(name, shape, at[0], dtype)
            size = mybir.dt.size(dtype)
            for n in shape:
                size *= n
            at[0] += (size + 31) // 32 * 32
            return t

        ident = keep("ident", [P])
        flip = keep("flip", [P])
        rot = keep("rot", [P])
        swap = keep("swap", [P])
        means = keep("means", [P])
        ones = keep("ones", [P])
        zeros = keep("zeros", [P])
        masks = keep("masks", [len(LEVELS) + 1, P], U8)
        vec = keep("vec", [2 * 224 + 8])
        mods = keep("mods", [DEPTH, MODS, 2])
        head_g = keep("head_g", [2, DEPTH])
        hgn = keep("hgn", [DEPTH, HD])
        cond = keep("cond", [KT, 2])
        lb = keep("lb", [4, 8])
        stats = keep("stats", [4, 64])
        bn = keep("bn", [NT, 12])
        mv = keep("mv", [2, NT, 2])
        rstd = keep("rstd", [2, NT])

        def g(name, shape, at_float, dtype=F32):
            return place(name, shape, G + 4 * at_float, dtype)

        rows = g("rows", [14, P], 0)
        pad_rows = g("pad_rows", [DEPTH, PAD_W], 11 * D)
        masks_in = g("masks_in", [len(LEVELS) + 1, P], 10 * D)
        ada = [place(f"ada{n}", [KT, 512], at_) for n, at_ in enumerate((O, O + 2048 * KT, W))]
        ada_late = place("ada_late", [3, KT, ADA_LATE_W], W)

        n_xt = g("n_xt", [2, D], 0)
        n_xh = g("n_xh", [2, D], 2 * D)
        n_t = g("n_t", [2, KT, P], 4 * D)
        n_r = g("n_r", [2, D], 6 * D)
        n_x1 = g("n_x1", [2, D], 8 * D)
        x_first = [n_r[:, 0], n_r[:, 1], n_x1[:, 0], n_x1[:, 1]]
        n_g = g("n_g", [D], 10 * D)
        n_b = g("n_b", [D], 11 * D)

        a_q = g("a_q", [2, T], 0)
        a_k = g("a_k", [T], 2 * T)
        a_v = g("a_v", [NT, P], 3 * T)
        a_bias = g("a_bias", [2, BIAS_BLOCKS, GRID_W], 4 * T)
        a_mask = g("a_mask", [GRID_W], 4 * T + 2 * BIAS_BLOCKS * 64)
        a_at = 4 * T + (2 * BIAS_BLOCKS + 1) * GRID_W
        a_p = g("a_p", [2, 832], a_at)
        a_pt = g("a_pt", [2, 7, P], a_at + 2 * 832)
        a_vt = g("a_vt", [T], a_at + 2 * 832)

        b_q = g("b_q", [3, T], 0)
        b_v = g("b_v", [NT, P], 3 * T)
        b_kz = g("b_kz", [2, 2, T], 4 * T)
        b_pt = g("b_pt", [2, NT, P], 8 * T)
        b_cos = g("b_cos", [LAT], 4 * T)
        b_sin = g("b_sin", [LAT], 4 * T + LAT)
        b_tmp = [g("b_tmp0", [T], 9 * T), g("b_tmp1", [T], 4 * T + 2 * LAT)]
        b_vt = g("b_vt", [T], 5 * T + 2 * LAT)
        b_k = g("b_k", [T], 8 * T)

        def b_p(n):
            return o_tok[:, :, D - P * (1 + n % 2):D - P * (n % 2)]

        c_z = g("c_z", [4, T], 0)
        c_state = g("c_state", [4, NT, P], 0)
        c_q = g("c_q", [2, T], 4 * T)
        c_v = g("c_v", [NT, 2 * P], 6 * T)
        c_g = g("c_g", [NT, 2 * P], 8 * T)
        c_b = place("c_b", [4, T], H)
        c_k = place("c_k", [4, T], H + 16 * T)
        c_lev = [place("c_lev_h", [2, 2, T], H + 32 * T), place("c_lev_w", [2, 2, T], W)]

        def c_lq(n):
            return c_lev[n // 2 % 2][:, n % 2, 0]

        def c_lk(n):
            return c_lev[n // 2 % 2][:, n % 2, 1]

        c_w = place("c_w", [2, 4, T], H + 32 * T)
        c_att = place("c_att", [NT, 4, P], H + 48 * T)
        c_el = keep("c_el", [4, NT])
        c_o = place("c_o", [2, 2 * P], H + 32 * T)
        c_o2 = place("c_o2", [2, 2 * P], H + 32 * T + 16 * P)
        c_ms = keep("c_ms", [2, NT, 4])

        f_hi = g("f_hi", [2, 2, T], 0, F32R)
        f_lo = g("f_lo", [2, 2, T], 4 * T, F32R)
        f_t = g("f_t", [2, T], 8 * T)

        pads = nc.dram_tensor("pads", (DEPTH, RPB_ROWS, PAD_W), F32, kind="Internal").ap()
        x_mid = [[nc.dram_tensor(f"x_mid{l}{w}", (T, D), F32, kind="Internal").ap() for w in range(2)]
                 for l in range(DEPTH)]

        def sem(name):
            return stack.enter_context(nc.semaphore(name))

        s = {}
        for name in (
            "const_landed", "rows_landed", "pads_stored", "cond_ready", "rows_turned", "ada_landed0", "ada_landed1",
            "ada_landed2", "ada_used", "mods_ready", "late_landed0", "late_landed1", "late_landed2", "late_used",
            "lb_shifted", "lb_exps", "lb_args", "lb_logs", "phase_end", "w_landed0", "w_landed1", "w_hi_done",
            "w_ready", "full0", "full1", "freed0", "freed1", "x_landed0", "x_landed1", "first_landed0",
            "first_landed1", "first_landed2", "first_landed3", "h_hi_ready", "r_ready", "rg_done", "ln_landed",
            "mean_ready", "rstd_ready", "xh_ready", "h_ready", "x1_ready", "x1_stored0", "x1_stored1", "bias_landed",
            "negmax_ready", "probs_ready", "out_ready", "out_freed", "sq_ready", "act_headrstd", "headnorm_ready",
            "rope_ready",
            "rope_landed", "a_zeroed", "kz_ready", "gate_l", "gate_m", "gate_k", "b_ready", "el_args", "el_ready",
            "kd_ready", "states_ready", "lev_k_args", "lev_k_exps", "lev_k_ready", "lev_q_args", "lev_q_exps",
            "lev_q_ready", "c_g_ready", "state_zeroed", "c_o_half", "c_o_used", "inter_exps", "inter_ready",
            "ms_ready", "hg_rstd", "o_hi_ready", "conv_start", "silu_done", "a_whole", "a_hi_ready", "a_ready",
            "act_step", "dve_step", "pool_step",
        ):
            s[name] = sem(name)

        def full(*key):
            n = plan.use[key]
            return s[f"full{n % 2}"], n // 2 + 1

        def freed(*key):
            n = plan.use[key]
            return s[f"freed{n % 2}"], n // 2 + 1

        def slot(*key):
            n = plan.use[key] % 2
            return psum[:, 3 * n:3 * n + 3, :].rearrange("p b n -> p (b n)")

        def before(*key):
            n = plan.use[key]
            return (s[f"freed{n % 2}"], n // 2) if n >= 2 else None

        def groups(l):
            return GROUPS if q_tiles(l) == NT else GROUPS[:2]

        phases = []
        for l in range(DEPTH):
            phases += [("A", l, 0), ("A", l, 1), ("A", l, 2), ("B", l), ("C", l), ("O", l), ("post", l, 0), ("F", l),
                       ("post", l, 1)]
        phases = [("h0",)] + phases
        PHASE = {key: n for n, key in enumerate(phases)}

        def phase_entered(*key):
            return s["phase_end"], 3 * PHASE[key]

        def n_bias_loads(l, r):
            return 8 * (3 * l + r + 1) + l + 1

        def blocks_of(ap, h):
            v = ap.rearrange("p (n a h) -> p n a h", a=2, h=h)
            return v[:, :, 0, :], v[:, :, 1, :]

        def end_phase(eng, last, *key):
            eng.wait_ge(*last)
            eng.sem_inc(s["phase_end"], 1)
            eng.wait_ge(s["phase_end"], 3 * (PHASE[key] + 1))

        block = stack.enter_context(nc.Block())

        @block.sync
        def _(sp):
            consts = Signal(s["const_landed"])
            for dst, src in ((ident, identity), (flip, reverse_columns), (rot, rotate_halves), (swap, swap_heads),
                             (means, head_means)):
                consts.on(sp.dma_start(dst[:], src), 16)
            consts.on(sp.dma_start(masks_in[:], level_masks), 16)
            for l in range(DEPTH):
                consts.on(sp.dma_start(hgn[:, l, :], spread(hg_norm[l])), 16)
            assert consts.n == 16 * N_CONSTS
            rows_in = Signal(s["rows_landed"])
            for l in range(DEPTH):
                rows_in.on(sp.dma_start(rows[0:MODS, 5 * l, :], b_ada[l].rearrange("(m p) -> m p", p=P)), 16)
                rows_in.on(sp.dma_start(rows[0:2 * FT, 5 * l + 1:5 * l + 4, :],
                                        conv_w[l].rearrange("j (m p) -> m j p", p=P)), 16)
                rows_in.on(sp.dma_start(rows[0:2 * FT, 5 * l + 4, :], conv_b[l].rearrange("(m p) -> m p", p=P)), 16)
            rows_in.on(sp.dma_start(rows[0:8, 10, :], hg_lower_bound.rearrange("l d (m p) -> (l d m) p", p=P)), 16)
            for a, vector in enumerate((c[0], c_ctx)):
                rows_in.on(sp.dma_start(rows[0:KT, 11 + a, :], vector.rearrange("(k p) -> k p", p=P)), 16)
            for n, gain in enumerate((q_norm, k_norm)):
                for half in range(2):
                    rows_in.on(sp.dma_start(rows[DEPTH * n:DEPTH * (n + 1), 13, HD * half:HD * (half + 1)], gain), 16)
            sp.wait_ge(s["pool_step"], 1)
            for l in range(DEPTH):
                rows_in.on(sp.dma_start(pad_rows[0:RPB_ROWS, l, 48:79], na_rpb[l].rearrange("h a b -> (h a) b")), 16)
            assert rows_in.n == 16 * N_ROWS

            def load_ada(n):
                src = w_ada[0].rearrange("(k p) n -> p k n", p=P)[:, :, 512 * n:512 * (n + 1)]
                sp.dma_start(ada[n % 3][:], src).then_inc(s[f"ada_landed{n % 3}"], 16)

            for n in range(3):
                load_ada(n)

            def load_first(i):
                src = x[0, P * i:P * i + P, :] if i < NTL else ctx[0, P * (i - NTL):P * (i - NTL) + P, :]
                sp.dma_start(x_first[i % 4], src).then_inc(s[f"first_landed{i % 4}"], 16)

            for i in range(4):
                load_first(i)
            sp.wait_ge(s["rows_landed"], rows_in.n)
            pads_out = Signal(s["pads_stored"])
            pads_out.on(sp.dma_start(pads.rearrange("l r n -> r l n"), pad_rows[0:RPB_ROWS]), 16)

            def load_weights(n):
                kind, l, a, *b = plan.tiles[n]
                if kind == "in":
                    src = w_in[l].rearrange("(k p) n -> p k n", p=P)[:, :, a:a + P]
                elif kind == "out":
                    src = w_out[l].rearrange("(k p) n -> p k n", p=P)[:, :, P * a:P * a + P]
                elif kind == "up":
                    at_col = P * a + D_FF * b[0]
                    src = w_up[l].rearrange("(k p) n -> p k n", p=P)[:, :, at_col:at_col + P]
                else:
                    src = w_down[l][2 * P * a:2 * P * (a + 1)].rearrange("(k p) n -> p k n", p=P)[
                        :, :, 512 * b[0]:512 * (b[0] + 1)]
                if n >= 2:
                    sp.wait_ge(s["w_ready"], n - 1)
                sp.dma_start(w_raw[:, n % 2].rearrange("p (k n) -> p k n", k=src.shape[1]), src)\
                  .then_inc(s[f"w_landed{n % 2}"], 16)

            sent = [0]

            def weights_up_to(*tile):
                end = plan.tile[tile] + 1
                for n in range(sent[0], end):
                    load_weights(n)
                sent[0] = max(sent[0], end)

            for n in range(3, ADA_FIRST):
                sp.wait_ge(s["ada_used"], n - 2)
                load_ada(n)
            sp.wait_ge(s["ada_used"], 3)
            weights_up_to("in", 0, COL["a_k"])

            x_in = [Signal(s["x_landed0"]), Signal(s["x_landed1"])]
            n_in = [0]

            def load_x(src, i):
                x_in[n_in[0] % 2].on(sp.dma_start(n_xt[:, n_in[0] % 2, :], src), 16)
                n_in[0] += 1

            def source(l, which, i):
                if (l, which) == (0, 0):
                    return x[0, P * i:P * i + P, :] if i < NTL else ctx[0, P * (i - NTL):P * (i - NTL) + P, :]
                before_ = x_mid[l][0] if which else x_mid[l - 1][1]
                return before_[P * i:P * i + P, :]

            for i in range(4, NT):
                sp.wait_ge(s["xh_ready"], i - 3)
                load_first(i)

            bias_in = Signal(s["bias_landed"])
            ln_in = Signal(s["ln_landed"])
            rope_in = Signal(s["rope_landed"])
            x_out = [Signal(s["x1_stored0"]), Signal(s["x1_stored1"])]
            n_post = 0
            for l in range(DEPTH):
                for r in range(3):
                    weights_up_to("in", l, COL["a_v"] + P * r)
                    sp.wait_ge(*phase_entered("A", l, r))
                    if r == 0:
                        bias_in.on(sp.dma_start(a_mask[:], window_mask), 16)
                        if l == 0:
                            sp.wait_ge(s["pads_stored"], pads_out.n)
                    for hh in range(2):
                        row = (l * 6 + 2 * r + hh) * N_RPB
                        table = a_bias[:, hh]
                        for half, first, blocks, at_block in ((0, 1, 14, 0), (1, 0, 14, 0), (0, 3, 9, 14),
                                                              (1, 2, 9, 14)):
                            src = bass.AP(tensor=pads.tensor, offset=(row + first) * PAD_W,
                                          ap=[[1, 64], [PAD_W, blocks], [1, 64]])
                            bias_in.on(sp.dma_start(table[64 * half:64 * half + 64, at_block:at_block + blocks, :],
                                                    src), 16)
                weights_up_to("in", l, B_PARTS["v"])
                sp.wait_ge(*phase_entered("B", l))
                rope_in.on(sp.dma_start(b_cos[:], rope_cos), 16)
                rope_in.on(sp.dma_start(b_sin[:], rope_sin), 16)
                weights_up_to("in", l, C_PARTS[-1][1])
                sp.wait_ge(*full("C", l, C_PARTS[-1][0]))
                for n, (m, a) in enumerate(late_tiles(l), n_late(l) - len(late_tiles(l))):
                    if n >= 3:
                        sp.wait_ge(s["late_used"], n - 2)
                    src = w_ada[m].rearrange("(k p) n -> p k n", p=P)[:, :, a:a + ADA_LATE_W]
                    sp.dma_start(ada_late[:, n % 3], src)\
                      .then_inc(s[f"late_landed{n % 3}"], 16)
                sp.wait_ge(s["late_used"], n_late(l))
                sp.wait_ge(*full("C", l, "att", len(LEVELS), 1, len(CHUNK_GROUPS) - 1))
                weights_up_to("out", l, KT - 1)
                for which in range(2):
                    if which:
                        weights_up_to("down", l, NPAIR - 1, 1)
                    sp.wait_ge(*phase_entered("post", l, which))
                    gain, shift = (ln2_g, ln2_b) if which else (ln1_g, ln1_b)
                    ln_in.on(sp.dma_start(n_g[:], spread(gain[l])), 16)
                    ln_in.on(sp.dma_start(n_b[:], spread(shift[l])), 16)
                    last = next_h(l, which) is None
                    dst = out[0] if last else x_mid[l][which]
                    nq = q_tiles(l)
                    for i in range(nq + 3):
                        if i < nq:
                            if i >= 2:
                                sp.wait_ge(*freed("y", l, which, i - 2))
                            if not (l == 0 and which == 0) and i == 0:
                                for k in range(2):
                                    sp.wait_ge(x_out[k].sem, x_out[k].n)
                            load_x(source(l, which, i), i)
                        if i >= 3:
                            sp.wait_ge(s["x1_ready"], n_post + 1)
                            store = sp.dma_start(dst[P * (i - 3):P * (i - 2), :], n_x1[:, n_post % 2, :])
                            x_out[n_post % 2].on(store, 16)
                            n_post += 1
            for k in range(2):
                sp.wait_ge(x_out[k].sem, x_out[k].n)

        @block.gpsimd
        def _(pool):
            pool.memset(pad_rows[:], 0.0).then_inc(s["pool_step"], 1)
            def split_tile(n):
                pool.wait_ge(s[f"w_landed{n % 2}"], 16 * (n // 2 + 1))
                if n >= 2:
                    pool.wait_ge(*full(*plan.tile_last[n - 2]))
                pool.tensor_scalar(w_hi[:, n % 2], w_raw[:, n % 2], 1.0, None, ALU.mult).then_inc(s["w_hi_done"], 1)
                pool.wait_ge(s["w_hi_done"], n + 1)
                pool.tensor_tensor(w_lo[:, n % 2], w_raw[:, n % 2], w_hi[:, n % 2].bitcast(F32), ALU.subtract)\
                    .then_inc(s["w_ready"], 1)

            def norm_gains(l, which):
                pool.wait_ge(s["ln_landed"], 32 * (2 * l + which + 1))
                for i in range(q_tiles(l)):
                    n = nth("post", l, which, i)
                    x1 = n_x1[:, (n - 1) % 2]
                    pool.wait_ge(s["r_ready"], n)
                    pool.tensor_tensor(x1, x1, n_g[:], ALU.mult).then_inc(s["rg_done"], 1)
                    pool.wait_ge(s["rg_done"], n)
                    pool.tensor_tensor(x1, x1, n_b[:], ALU.add).then_inc(s["x1_ready"], 1)

            def recurrence(l):
                pool.wait_ge(*freed("C", l, "g1", "t"))
                gates = c_g[:].rearrange("p c (h v) -> p (c h) v", v=HD)
                pool.tensor_tensor(gates, gates, hgn[:, l, :].unsqueeze(1).broadcast_to([P, 4 * NT, HD]), ALU.mult)\
                    .then_inc(s["c_g_ready"], 1)
                pool.wait_ge(s["b_ready"], nth("hg", l, 3))
                pool.memset(c_state[:], 0.0).then_inc(s["state_zeroed"], 1)
                levels = [(lev, tile) for lev in range(len(LEVELS) + 1) for tile in range(2)]

                def args(n):
                    lev, tile = levels[n]
                    if n >= 4:
                        pool.wait_ge(*full("C", l, "att", lev - 2, tile, len(CHUNK_GROUPS) - 1))
                    elif n >= 2:
                        pool.wait_ge(s["late_used"], n_late(l))
                    else:
                        for j in (2, 3):
                            pool.wait_ge(*full("C", l, "D", j))
                    if lev == len(LEVELS):
                        return
                    h = LEVELS[lev]
                    k1, k2 = blocks_of(c_lk(n), h)
                    bf1, _ = blocks_of(c_b[:, tile], h)
                    _, bb2 = blocks_of(c_b[:, 2 + tile], h)
                    shape = [P, T // (2 * h), h]
                    pool.tensor_tensor(k1, bf1[:, :, h - 1:h].broadcast_to(shape), bf1, ALU.subtract)\
                        .then_inc(s["pool_step"], 1)
                    pool.tensor_tensor(k2, bb2[:, :, 0:1].broadcast_to(shape), bb2, ALU.subtract)\
                        .then_inc(s["lev_k_args"], 1)

                def operands(n):
                    lev, tile = levels[n]
                    if lev == len(LEVELS):
                        pool.tensor_tensor(c_lk(n), c_k[:, tile], c_k[:, 2 + tile], ALU.add)\
                            .then_inc(s["lev_k_ready"], 1)
                        return
                    h = LEVELS[lev]
                    pool.wait_ge(s["lev_k_exps"], nth("levx", l, lev, tile))
                    k1, k2 = blocks_of(c_lk(n), h)
                    kf1, _ = blocks_of(c_k[:, tile], h)
                    _, kb2 = blocks_of(c_k[:, 2 + tile], h)
                    pool.tensor_tensor(k1, k1, kf1, ALU.mult).then_inc(s["pool_step"], 1)
                    pool.tensor_tensor(k2, k2, kb2, ALU.mult).then_inc(s["lev_k_ready"], 1)

                for n in range(len(levels) + 1):
                    if n < len(levels):
                        args(n)
                    if n >= 1:
                        operands(n - 1)
                for j in (1, 3):
                    pool.wait_ge(s["inter_exps"], nth("hg", l, j))
                    pool.tensor_tensor(c_b[:, j], c_b[:, j], c_q[:, j % 2], ALU.mult).then_inc(s["inter_ready"], 1)

            done = 0
            for l in range(DEPTH):
                for after_tiles, end in ((lambda: recurrence(l), plan.tile["out", l, 0]),
                                         (lambda: norm_gains(l, 0), plan.tile["up", l, 0, 0]),
                                         (lambda: norm_gains(l, 1), plan.tile["down", l, NPAIR - 1, 1] + 1)):
                    for n in range(done, end):
                        split_tile(n)
                    after_tiles()
                    done = end

        @block.tensor
        def _(pe):
            def wait(token):
                if token is not None and token[1] > 0:
                    pe.wait_ge(*token)

            def fill(ins, *key):
                ins.then_inc(s[f"full{plan.use[key] % 2}"], 1)
                return full(*key)

            def turn(out_ap, in_ap, rows_=P):
                return pe.transpose(out_ap, in_ap, ident[0:rows_, 0:rows_])

            def gemm(tile, key, parts, kt=KT, col=0, x_hi=h_hi, x_lo=h_lo):
                n = plan.tile[tile]
                wait((s["w_ready"], n + 1))
                wait(before(*key))
                acc = slot(*key)
                halves = ((w_hi, x_hi), (w_hi, x_lo), (w_lo, x_hi))
                for k in range(kt):
                    for j, (w, a) in enumerate(halves):
                        weight = w[:, n % 2].rearrange("p (k n) -> p k n", k=kt)[:, k, col:col + P]
                        for t0, tn in parts:
                            last = pe.matmul(acc[:, t0:t0 + tn], weight, a[:, k, t0:t0 + tn],
                                             start=(k == 0 and j == 0), stop=(k == kt - 1 and j == 2))
                return fill(last, *key)

            wait((s["const_landed"], 16 * N_CONSTS))
            wait((s["rows_landed"], 16 * N_ROWS))
            for l in range(DEPTH):
                turn(psum[:, 6, 224 * l:224 * l + MODS], rows[0:MODS, 5 * l, :], MODS)
                for j in range(4):
                    at_col = 224 * l + MODS + 2 * FT * j
                    turn(psum[:, 6, at_col:at_col + 2 * FT], rows[0:2 * FT, 5 * l + 1 + j, :], 2 * FT)
            turn(psum[:, 6, 448:456], rows[0:8, 10, :], 8)
            for a in range(2):
                turn(psum[:, 6, 456 + KT * a:456 + KT * (a + 1)], rows[0:KT, 11 + a, :], KT)
            turn(psum[:, 6, 472:476], rows[0:2 * DEPTH, 13, :], 2 * DEPTH).then_inc(s["rows_turned"], 1)
            wait((s["cond_ready"], 1))

            def modulation(at_col, weight):
                for k in range(KT):
                    last = pe.matmul(psum[:, 7, at_col:at_col + 96].rearrange("p (r a) -> p r a", a=2), weight(k),
                                     cond[:, k, :].unsqueeze(1).broadcast_to([P, 48, 2]), start=(k == 0),
                                     stop=(k == KT - 1))
                return last

            for n in range(ADA_FIRST):
                wait((s[f"ada_landed{n % 3}"], 16 * (n // 3 + 1)))
                for m in range(4):
                    last = modulation(8 * n + 2 * m, lambda k: ada[n % 3][:, k, P * m:P * m + P])
                last.then_inc(s["ada_used"], 1)

            def turn_normed(key):
                wait((s["xh_ready"], nth("xh", *key)))
                wait(before(*key))
                acc = slot(*key)
                for k in range(KT):
                    last = turn(acc[:, P * k:P * k + P], n_xh[:, nth("xh", *key) % 2, P * k:P * k + P])
                return fill(last, *key)

            for i in range(NT):
                last = turn_normed(("h", 0, i))
            end_phase(pe, last, "h0")

            def attend_pv(unit_key, blocks, cols):
                u = nth("unit", *unit_key)
                wait(freed(*unit_key, "turned"))
                if u > 2:
                    wait((s["out_freed"], u - 2))
                for n, (probs, values) in enumerate(blocks):
                    last = pe.matmul(psum[:, 6 + u % 2, cols], probs, values[:, cols], start=(n == 0),
                                     stop=(n == len(blocks) - 1))
                last.then_inc(s["out_ready"], 1)

            def phase_a(l, r):
                wait((s["h_ready"], nth("xh", "h", l, NT - 1)))
                for name in "qkv":
                    gemm(("in", l, COL["a_" + name] + P * r), ("A", l, r, name),
                         groups(l) if name == "q" else GROUPS)
                key = ("A", l, r, "vt")
                wait(freed("A", l, r, "v"))
                wait(before(*key))
                for i in range(NT):
                    last = turn(slot(*key)[:, P * i:P * i + P], a_vt[:, P * i:P * i + P])
                fill(last, *key)
                wait((s["bias_landed"], 16 * n_bias_loads(l, r)))
                for hh in range(2):
                    table = a_bias[:, hh].rearrange("p b n -> p (b n)")
                    key = ("A", l, r, "bias", hh)
                    wait(before(*key))
                    for t0 in range(0, BIAS_BLOCKS * 64, 512):
                        t1 = min(t0 + 512, BIAS_BLOCKS * 64)
                        last = pe.matmul(slot(*key)[:, t0:t1], flip[:], table[:, t0:t1], start=True, stop=True)
                    fill(last, *key)
                nq = q_tiles(l)
                units = [(hh, p) for hh in range(2) for p in range(nq)]

                def scores(u):
                    hh, p = units[u]
                    key = ("A", l, r, u)
                    if u == 0:
                        wait((s["a_zeroed"], 2 * (3 * l + r + 1)))
                        for name in "qk":
                            wait(freed("A", l, r, name))
                    wait(before(*key))
                    acc = slot(*key)
                    q = a_q[:, hh, P * p:P * p + P]
                    if p < NTL:
                        start, n, _ = ROW_PAIRS[p]
                        pe.matmul(acc[:, 0:512], q, a_k[:, 64 * start:64 * start + 512], start=True, stop=True)
                        if n > WIN_R:
                            pe.matmul(acc[:, 512:576], q, a_k[:, 64 * (start + 8):64 * (start + 9)],
                                      start=True, stop=True)
                    last = pe.matmul(acc[:, 576:832], q, a_k[:, LAT:T], start=True, stop=True)
                    fill(last, *key)

                def turn_probs(u):
                    hh, p = units[u]
                    key = ("A", l, r, u)
                    n_unit = nth("unit", *key)
                    key = (*key, "turned")
                    wait((s["probs_ready"], n_unit))
                    wait(before(*key))
                    acc = slot(*key)
                    src = a_p[:, n_unit % 2]
                    w = GRID_W * ROW_PAIRS[p][1] if p < NTL else 0
                    if p < NTL:
                        for b in range(4):
                            turn(acc[:, P * b:P * b + P], src[:, P * b:P * b + P])
                    for b in range(2):
                        last = turn(acc[:, P * (4 + b):P * (5 + b)], src[:, w + P * b:w + P * b + P])
                    if p < NTL and ROW_PAIRS[p][1] > WIN_R:
                        last = pe.transpose(acc[0:64, P * 6:P * 7], src[:, 512:576], ident[:])
                    fill(last, *key)

                def values(u):
                    hh, p = units[u]
                    key = ("A", l, r, u)
                    if u == 0:
                        wait(freed("A", l, r, "vt"))
                    pt = a_pt[:, nth("unit", *key) % 2]
                    blocks = [(pt[:, 4 + b, :], a_v[:, NTL + b, :]) for b in range(2)]
                    if p < NTL:
                        start, n, _ = ROW_PAIRS[p]
                        blocks += [(pt[:, b, :], a_v[:, start // 2 + b, :]) for b in range(4)]
                        if n > WIN_R:
                            blocks.append((pt[0:64, 6, :], a_v[0:64, start // 2 + 4, :]))
                    attend_pv(key, blocks, slice(HD * hh, HD * hh + HD))

                scores(0)
                for u in range(len(units) + 1):
                    if u + 1 < len(units):
                        scores(u + 1)
                    if u < len(units):
                        turn_probs(u)
                    if u >= 1:
                        values(u - 1)
                return s["out_ready"], nth("unit", "A", l, r, len(units) - 1)

            def phase_b(l):
                for what, name in B_STEPS:
                    parts = groups(l) if name[0] == "q" else GROUPS
                    if what == "gemm":
                        gemm(("in", l, B_PARTS[name]), ("B", l, name), parts)
                        continue
                    key = ("B", l, name, what)
                    src = b_k[:] if name == "k" else b_q[:, int(name[1])] if name[0] == "q" else b_vt[:]
                    weight = {"ms": means, "rot": rot, "swap": swap, "turn": None}[what]
                    if what == "turn":
                        wait(freed("B", l, name))
                    elif what == "ms":
                        wait((s["sq_ready"], nth("bn", l, name)))
                        src = b_tmp[B_NORMED.index(name) % 2]
                    elif what == "rot":
                        wait((s["headnorm_ready"], nth("bn", l, name)))
                        parts = GROUPS[:2]
                    else:
                        wait((s["rope_ready"], nth("bn", l, name)))
                    wait(before(*key))
                    if what == "turn":
                        for i in range(NT):
                            last = turn(slot(*key)[:, P * i:P * i + P], src[:, P * i:P * i + P])
                    else:
                        for t0, tn in parts:
                            last = pe.matmul(slot(*key)[:, t0:t0 + tn], weight[:], src[:, t0:t0 + tn],
                                             start=True, stop=True)
                    fill(last, *key)
                nq = q_tiles(l)
                units = [(h, i) for h in range(6) for i in range(nq)]

                def scores(u):
                    h, i = units[u]
                    key = ("B", l, u)
                    if u == 0:
                        wait((s["rope_ready"], nth("bn", l, "q2")))
                        wait((s["kz_ready"], 6 * (l + 1)))
                    wait(before(*key))
                    acc = slot(*key)
                    for t0, tn in (GROUPS if i < NTL else GROUPS[2:]):
                        last = pe.matmul(acc[:, t0:t0 + tn], b_q[:, h // 2, P * i:P * i + P],
                                         b_kz[:, h // 3, h % 2, t0:t0 + tn], start=True, stop=True)
                    fill(last, *key)

                def turn_probs(u):
                    h, i = units[u]
                    key = ("B", l, u)
                    n_unit = nth("unit", *key)
                    key = (*key, "turned")
                    wait((s["probs_ready"], n_unit))
                    wait(before(*key))
                    for b in range(0 if i < NTL else NTL, NT):
                        last = turn(slot(*key)[:, P * b:P * b + P], b_p(n_unit)[:, b, :])
                    fill(last, *key)

                def values(u):
                    h, i = units[u]
                    key = ("B", l, u)
                    pt = b_pt[:, nth("unit", *key) % 2]
                    attend_pv(key, [(pt[:, b, :], b_v[:, b, :]) for b in range(0 if i < NTL else NTL, NT)],
                              slice(HD * (h // 3), HD * (h // 3) + HD))

                scores(0)
                for u in range(len(units) + 1):
                    if u + 1 < len(units):
                        scores(u + 1)
                    if u < len(units):
                        turn_probs(u)
                    if u >= 1:
                        values(u - 1)
                return s["out_ready"], nth("unit", "B", l, len(units) - 1)

            def phase_c(l):
                def turn_part(name):
                    key = ("C", l, name, "t")
                    wait(freed("C", l, name))
                    wait(before(*key))
                    for i in range(NT):
                        last = turn(slot(*key)[:, P * i:P * i + P], c_z[:, 2 + int(name[1]), P * i:P * i + P])
                    fill(last, *key)

                for name, col in C_PARTS:
                    gemm(("in", l, col), ("C", l, name), GROUPS)
                    if name in C_TURNED:
                        turn_part(name)
                first_late = n_late(l) - len(late_tiles(l))

                def late(n):
                    wait((s[f"late_landed{n % 3}"], 16 * (n // 3 + 1)))
                    for m in range(ADA_LATE_W // P):
                        at_col = 2 * (ADA_LATE_W // P * (n - first_late) + m)
                        last = modulation(at_col, lambda k: ada_late[:, n % 3, k, P * m:P * m + P])
                    last.then_inc(s["late_used"], 1)
                done_late = 0
                for j in range(5):
                    upto = ada_before_keys(l, j) if j < 4 else len(late_tiles(l))
                    for n in range(done_late, upto):
                        late(first_late + n)
                    done_late = max(upto, done_late)
                    if j == 4:
                        break
                    key = ("C", l, "kd", j)
                    wait((s["kd_ready"], nth("hg", l, j)))
                    wait(before(*key))
                    for i in range(NT):
                        last = turn(slot(*key)[:, P * i:P * i + P], c_w[:, j % 2, 0, P * i:P * i + P])
                    fill(last, *key)
                    wait(freed(*key))
                    key = ("C", l, "D", j)
                    wait(before(*key))
                    kd = c_w[:, j % 2, 1].rearrange("p (c k) -> p c k", k=P)
                    for i in range(NT):
                        last = pe.matmul(slot(*key)[:, P * i:P * i + P], kd[:, i, :],
                                         c_v[:, i, P * (j % 2):P * (j % 2) + P], start=True, stop=True)
                    fill(last, *key)
                for lev in range(len(LEVELS) + 1):
                    diag = lev == len(LEVELS)
                    for tile in range(2):
                        wait((s["lev_k_ready"], nth("lev", l, lev, tile)))
                        if not diag:
                            wait((s["lev_q_ready"], nth("levx", l, lev, tile)))
                        for q, (c0, cn) in enumerate(CHUNK_GROUPS):
                            key = ("C", l, "att", lev, tile, q)
                            wait(before(*key))
                            acc = slot(*key)
                            for par in range(2):
                                rows_ = slice(HD * par, HD * par + HD)
                                for n in range(cn):
                                    t = slice(P * (c0 + n), P * (c0 + n) + P)
                                    qs = c_q[rows_, tile, t] if diag else c_lq(2 * lev + tile)[rows_, t]
                                    last = pe.matmul(acc[:, 512 * par + P * n:512 * par + P * n + P],
                                                     c_lk(2 * lev + tile)[rows_, t], qs, start=True, stop=True)
                            fill(last, *key)
                for i in range(q_tiles(l)):
                    if i == 0:
                        wait(freed("C", l, "att", len(LEVELS), 1, len(CHUNK_GROUPS) - 1))
                        wait((s["inter_ready"], 4 * (l + 1)))
                        wait((s["states_ready"], 4 * (l + 1)))
                    key = ("C", l, "out", i)
                    wait(before(*key))
                    acc = slot(*key)
                    for tile in range(2):
                        t = slice(P * tile, P * tile + P)
                        for h in (2 * tile, 2 * tile + 1):
                            pe.matmul(acc[:, P * h:P * h + P], c_att[:, i, h, :], c_v[:, i, t], start=True, stop=True)
                        for way in range(2):
                            last = pe.matmul(acc[:, 512 + P * tile:512 + P * tile + P],
                                             c_b[:, 2 * way + tile, P * i:P * i + P],
                                             c_state[:, 2 * way + tile, i, :], start=(way == 0), stop=(way == 1))
                    last = fill(last, *key)
                return last

            def phase_o(l):
                for i in range(q_tiles(l)):
                    key = ("O", l, i)
                    wait(before(*key))
                    for k in range(KT):
                        last = turn(slot(*key)[:, P * k:P * k + P], o_tok[:, i, P * k:P * k + P])
                    fill(last, *key)
                for i in range(q_tiles(l) - 2, q_tiles(l)):
                    wait(freed("O", l, i))
                for m in range(KT):
                    last = gemm(("out", l, m), ("W", l, m), groups(l))
                return last

            def phase_post(l, which):
                nq = q_tiles(l)
                for i in range(nq + 3):
                    if i < nq:
                        key = ("y", l, which, i)
                        wait(before(*key))
                        for k in range(KT):
                            last = turn(slot(*key)[:, P * k:P * k + P], y_chan[:, k, P * i:P * i + P])
                        last = fill(last, *key)
                    if i >= 3 and next_h(l, which):
                        last = turn_normed((*next_h(l, which), i - 3))
                return last

            def phase_f(l):
                wait((s["h_ready"], nth("xh", "h2", l, q_tiles(l) - 1)))
                for i in range(NPAIR + 1):
                    if i < NPAIR:
                        for f in (2 * i, 2 * i + 1):
                            for half in range(2):
                                gemm(("up", l, f, half), ("F", l, f, half), groups(l))
                    if i:
                        wait((s["a_ready"], nth("ff", l, 2 * i - 1)))
                        for q in range(2):
                            for m in range(4 * q, 4 * q + 4):
                                last = gemm(("down", l, i - 1, q), ("Y", l, i - 1, m), groups(l), kt=2,
                                            col=P * (m % 4), x_hi=f_hi[:, (i - 1) % 2], x_lo=f_lo[:, (i - 1) % 2])
                return last

            for l in range(DEPTH):
                for r in range(3):
                    end_phase(pe, phase_a(l, r), "A", l, r)
                end_phase(pe, phase_b(l), "B", l)
                end_phase(pe, phase_c(l), "C", l)
                end_phase(pe, phase_o(l), "O", l)
                end_phase(pe, phase_post(l, 0), "post", l, 0)
                end_phase(pe, phase_f(l), "F", l)
                end_phase(pe, phase_post(l, 1), "post", l, 1)

        @block.vector
        def _(dve):
            own = Signal(s["dve_step"])

            def step(ins):
                token = own.on(ins)
                dve.wait_ge(*token)
                return token

            def also(ins):
                return own.on(ins)

            def release(ins, *key):
                ins.then_inc(s[f"freed{plan.use[key] % 2}"], 1)
                return freed(*key)

            def say(name, ins):
                ins.then_inc(s[name], 1)

            also(dve.memset(zeros[:], 0.0))
            step(dve.memset(ones[:], 1.0))
            dve.wait_ge(s["const_landed"], 16 * N_CONSTS)
            also(dve.tensor_copy(masks[:], masks_in[:]))
            dve.wait_ge(s["cond_ready"], 1)
            also(dve.tensor_scalar(head_g[:, 0, :], psum[:, 6, 472:474], QSCALE, None, ALU.mult))
            also(dve.tensor_copy(head_g[:, 1, :], psum[:, 6, 474:476]))
            step(dve.tensor_copy(vec[:], psum[:, 6, 0:456]))
            top_ = stats[:, 0, 0:4]
            step(dve.tensor_tensor(top_, vec[:, 448:452], vec[:, 452:456], ALU.max))
            for l in range(2):
                ins = dve.tensor_tensor(lb[:, 0, 4 * l:4 * l + 4], vec[:, 448 + 4 * l:452 + 4 * l], top_, ALU.subtract)
                say("lb_shifted", ins)
            dve.wait_ge(s["lb_exps"], 1)
            step(dve.tensor_tensor(stats[:, 0, 4:8], lb[:, 0, 0:4], lb[:, 0, 4:8], ALU.add))
            step(dve.reciprocal(stats[:, 0, 8:12], stats[:, 0, 4:8]))
            for l in range(2):
                share = lb[:, 0, 4 * l:4 * l + 4]
                step(dve.tensor_tensor(share, share, stats[:, 0, 8:12], ALU.mult))
            step(dve.tensor_tensor(stats[:, 0, 12:16], lb[:, 0, 0:4], lb[:, 0, 4:8], ALU.add))
            step(dve.tensor_tensor(lb[:, 0, 4:8], stats[:, 0, 12:16], lb[:, 0, 0:4], ALU.subtract))
            step(dve.tensor_tensor(lb[:, 0, 0:4], lb[:, 0, 0:4], lb[:, 0, 0:4], ALU.subtract))
            step(dve.tensor_scalar(lb[:, 1], lb[:, 0], LB_FLOOR, None, ALU.max))
            step(dve.tensor_scalar(lb[:, 2], lb[:, 0], -1.0, 1.0, ALU.mult, ALU.add))
            say("lb_args", dve.tensor_scalar(lb[:, 2], lb[:, 2], 1e-19, None, ALU.max))
            dve.wait_ge(s["lb_logs"], 1)
            step(dve.tensor_scalar(lb[:, 1], lb[:, 1], -LN_SHIFT * LN2, None, ALU.add))
            step(dve.tensor_tensor(lb[:, 3], lb[:, 2], lb[:, 1], ALU.subtract))
            def modulation(l, m0, m1, at_col):
                step(dve.tensor_tensor(
                    mods[:, l, m0:m1], psum[:, 7, at_col:at_col + 2 * (m1 - m0)].rearrange("p (m a) -> p m a", a=2),
                    vec[:, 224 * l + m0:224 * l + m1].unsqueeze(2).broadcast_to([P, m1 - m0, 2]), ALU.add))
                for i in (1, 4):
                    if m0 <= KT * i < m1:
                        last = step(dve.tensor_scalar(mods[:, l, KT * i:KT * i + KT], mods[:, l, KT * i:KT * i + KT],
                                                      1.0, None, ALU.add))
                return last


            def moments(x_ap, key):
                n = nth("stat", *key)
                i = (n - 1) % NT
                w = (n - 1) // NT % 2
                for half in range(2):
                    tok = also(dve.bn_stats(bn[:, i, 6 * half:6 * half + 6], x_ap[:, 512 * half:512 * half + 512]))
                dve.wait_ge(*tok)
                say("mean_ready", dve.bn_aggr(mv[:, w, i, :], bn[:, i, :]))

            def mean_of(key):
                n = nth("stat", *key)
                w, i = (n - 1) // NT % 2, (n - 1) % NT
                return mv[:, w, i, 0:1], rstd[:, w, i:i + 1]

            def normed(dst, src, key):
                mean, r = mean_of(key)
                dve.wait_ge(s["mean_ready"], nth("stat", *key))
                dve.wait_ge(s["rstd_ready"], nth("stat", *key))
                return dve.tensor_scalar(dst, src, mean, r, ALU.subtract, ALU.mult)

            def normed_for_pe(src, key):
                n = nth("xh", *key)
                if n > 2:
                    dve.wait_ge(*full(*XH[n - 3]))
                    dve.wait_ge(s["xh_ready"], n - 2)
                say("xh_ready", normed(n_xh[:, n % 2], src, key))

            def split(key):
                n = nth("xh", *key)
                i = key[-1]
                dve.wait_ge(s["h_hi_ready"], n)
                t = slice(P * i, P * i + P)
                say("h_ready", dve.tensor_tensor(h_lo[:, :, t], n_t[:, n % 2], h_hi[:, :, t].bitcast(F32),
                                                 ALU.subtract))

            for i in range(NT + 3):
                if i == 2:
                    dve.wait_ge(s["ada_used"], ADA_FIRST)
                    modulation(0, 0, 2 * KT, 0)
                    dve.sem_inc(s["mods_ready"], 1)
                if i < NT:
                    dve.wait_ge(s[f"first_landed{i % 4}"], 16 * (i // 4 + 1))
                    moments(x_first[i % 4], ("h", 0, i))
                if 1 <= i <= NT:
                    normed_for_pe(x_first[(i - 1) % 4], ("h", 0, i - 1))
                if i >= 3:
                    split(("h", 0, i - 3))
            end_phase(dve, (s["h_ready"], nth("xh", "h", 0, NT - 1)), "h0")

            def copied_max(dst, src, top_):
                return dve.tensor_tensor_reduce(
                    out=dst, in0=src, in1=zeros[:].unsqueeze(1).broadcast_to(list(src.shape)), scale=1.0,
                    scalar=-3e38, op0=ALU.add, op1=ALU.max, accum_out=top_)

            def attend(l, units, key_of, negmax, out_of, value_of):
                def reciprocal_of_sum(u):
                    n = nth("unit", *key_of(u))
                    dve.wait_ge(s["probs_ready"], n)
                    c_ = n % 64
                    return also(dve.reciprocal(stats[:, 2, c_:c_ + 1], stats[:, 2, c_:c_ + 1]))

                def output(u):
                    n = nth("unit", *key_of(u))
                    c_ = n % 64
                    dve.wait_ge(s["out_ready"], n)
                    dve.wait_ge(*sums[u])
                    say("out_freed", dve.tensor_scalar(out_of(u), value_of(u, 6 + n % 2), stats[:, 2, c_:c_ + 1],
                                                       None, ALU.mult))
                sums = {}
                for u in range(len(units) + 2):
                    if u < len(units):
                        negmax(u)
                    if 1 <= u <= len(units):
                        sums[u - 1] = reciprocal_of_sum(u - 1)
                    if u >= 2:
                        output(u - 2)
                return s["out_freed"], nth("unit", *key_of(len(units) - 1))

            def phase_a(l, r):
                say("a_zeroed", dve.memset(a_q[HD:P, 0], 0.0))
                say("a_zeroed", dve.memset(a_q[0:HD, 1], 0.0))
                for hh in range(2):
                    key = ("A", l, r, "bias", hh)
                    dve.wait_ge(*full(*key))
                    dve.wait_ge(*release(dve.tensor_tensor(
                        a_bias[:, hh], slot(*key)[:, 0:BIAS_BLOCKS * GRID_W].rearrange("p (b n) -> p b n", n=GRID_W),
                        a_mask[:].unsqueeze(1).broadcast_to([P, BIAS_BLOCKS, GRID_W]), ALU.add), *key))
                    also(dve.memset(a_bias[0:GRID_W, hh, BIAS_BLOCKS - 1], NEVER))
                    step(dve.memset(a_bias[GRID_W:P, hh, BIAS_BLOCKS - 9], NEVER))
                units = [(hh, p) for hh in range(2) for p in range(q_tiles(l))]

                def key_of(u):
                    return ("A", l, r, u)

                def negmax(u):
                    hh, p = units[u]
                    n = nth("unit", *key_of(u))
                    c_ = n % 64
                    acc = slot(*key_of(u))
                    dve.wait_ge(*full(*key_of(u)))
                    if u >= 2:
                        dve.wait_ge(*full(*key_of(u - 2), "turned"))
                    w = 0
                    if p < NTL:
                        _, rows_, block_ = ROW_PAIRS[p]
                        w = 64 * rows_
                        bias_of = a_bias[:, hh].rearrange("p b n -> p (b n)")
                        also(dve.tensor_tensor_reduce(
                            out=a_p[:, n % 2, 0:w], in0=acc[:, 0:w], in1=bias_of[:, 64 * block_:64 * block_ + w],
                            scale=1.0, scalar=-3e38, op0=ALU.add, op1=ALU.max, accum_out=stats[:, 0, c_:c_ + 1]))
                    dve.wait_ge(*release(copied_max(
                        a_p[:, n % 2, w:w + CTX].rearrange("p (b n) -> p b n", n=P),
                        acc[:, 576:832].rearrange("p (b n) -> p b n", n=P), stats[:, 1, c_:c_ + 1]),
                                         *key_of(u)))
                    top_ = stats[:, 0, c_:c_ + 1] if p < NTL else stats[:, 1, c_:c_ + 1]
                    say("negmax_ready", dve.tensor_scalar(stats[:, 1, c_:c_ + 1], stats[:, 1, c_:c_ + 1],
                                                          top_, -1.0, ALU.max, ALU.mult))

                def out_of(u):
                    hh, p = units[u]
                    return o_tok[:, p, HD * (2 * r + hh):HD * (2 * r + hh) + HD]

                def value_of(u, bank):
                    return psum[:, bank, HD * units[u][0]:HD * units[u][0] + HD]
                return attend(l, units, key_of, negmax, out_of, value_of)

            def phase_b(l):
                for k, name in enumerate(B_NORMED):
                    tmp = b_tmp[k % 2]
                    src = b_k[:] if name == "k" else b_q[:, int(name[1])]
                    w = T if name == "k" or q_tiles(l) == NT else LAT
                    n = nth("bn", l, name)
                    dve.wait_ge(*freed("B", l, name))
                    dve.wait_ge(s["act_headrstd"], n)
                    gain = head_g[:, int(name == "k"), l:l + 1]
                    say("headnorm_ready", dve.scalar_tensor_tensor(out=src[:, 0:w], in0=src[:, 0:w], scalar=gain,
                                                                   in1=tmp[:, 0:w], op0=ALU.mult, op1=ALU.mult))
                    dve.wait_ge(s["headnorm_ready"], n)
                    if name == "k":
                        dve.wait_ge(s["rope_landed"], 32 * (l + 1))
                    step(dve.tensor_tensor(tmp[:, 0:LAT], src[:, 0:LAT], b_cos[:], ALU.mult))
                    dve.wait_ge(*full("B", l, name, "rot"))
                    dve.wait_ge(*release(dve.tensor_tensor(src[:, 0:LAT], slot("B", l, name, "rot")[:, 0:LAT], b_sin[:],
                                                           ALU.mult), "B", l, name, "rot"))
                    say("rope_ready", dve.tensor_tensor(src[:, 0:LAT], src[:, 0:LAT], tmp[:, 0:LAT], ALU.add))
                dve.wait_ge(s["rope_ready"], nth("bn", l, B_NORMED[-1]))
                for kv in range(2):
                    other = slice(HD * (1 - kv), HD * (1 - kv) + HD)
                    own_ = slice(HD * kv, HD * kv + HD)
                    also(dve.memset(b_kz[other, kv, kv], 0.0))
                    also(dve.memset(b_kz[own_, kv, 1 - kv], 0.0))
                    step(dve.tensor_copy(b_kz[own_, kv, kv], b_k[own_]))
                    dve.sem_inc(s["kz_ready"], 2)
                units = [(h, i) for h in range(6) for i in range(q_tiles(l))]

                def key_of(u):
                    return ("B", l, u)

                def negmax(u):
                    h, i = units[u]
                    n = nth("unit", *key_of(u))
                    c_ = n % 64
                    dve.wait_ge(*full(*key_of(u)))
                    if u >= 2:
                        dve.wait_ge(*full(*key_of(u - 2), "turned"))
                    blocks = slice(0 if i < NTL else NTL, NT)
                    acc = slot(*key_of(u))[:, 0:T].rearrange("p (b n) -> p b n", n=P)[:, blocks, :]
                    dve.wait_ge(*release(copied_max(b_p(n)[:, blocks, :], acc, stats[:, 0, c_:c_ + 1]), *key_of(u)))
                    say("negmax_ready", dve.tensor_scalar(stats[:, 1, c_:c_ + 1], stats[:, 0, c_:c_ + 1], -1.0, None,
                                                          ALU.mult))

                def out_of(u):
                    h, i = units[u]
                    return o_tok[:, i, HD * (6 + h):HD * (7 + h)]

                def value_of(u, bank):
                    return psum[:, bank, HD * (units[u][0] // 3):HD * (units[u][0] // 3) + HD]
                return attend(l, units, key_of, negmax, out_of, value_of)

            def phase_c(l):
                dve.wait_ge(*freed("C", l, "q1"))
                dve.wait_ge(*freed("C", l, "q0"))

                def gates_1(j):
                    dve.wait_ge(s["gate_l"], nth("hg", l, j))
                    w = c_w[:, j % 2]
                    also(dve.scalar_tensor_tensor(out=w[:, 1], in0=c_z[:, j], scalar=0.0, in1=w[:, 0], op0=ALU.min,
                                                  op1=ALU.subtract))
                    say("gate_m", dve.scalar_tensor_tensor(out=w[:, 2], in0=c_z[:, j], scalar=0.0, in1=w[:, 0],
                                                           op0=ALU.max, op1=ALU.add))

                def gates_2(j):
                    w = c_w[:, j % 2]
                    way = j // 2
                    dve.wait_ge(s["gate_k"], nth("hg", l, j))
                    step(dve.tensor_scalar(w[:, 1], w[:, 1], lb[:, 2, 4 * l + j:4 * l + j + 1],
                                           lb[:, 1, 4 * l + j:4 * l + j + 1], ALU.add, ALU.max))
                    step(dve.tensor_tensor(c_z[:, j], w[:, 1], w[:, 3], ALU.add))
                    for i in range(NT):
                        src, dst = c_z[:, j, P * i:P * i + P], c_b[:, j, P * i:P * i + P]
                        if way:
                            src, dst = src[:, ::-1], dst[:, ::-1]
                        ins = dve.tensor_tensor_scan(dst, ones[:], src, 0.0, ALU.mult, ALU.add)
                        also(ins) if i < NT - 1 else say("b_ready", ins)

                gates_1(0)
                for j in range(4):
                    if j < 3:
                        gates_1(j + 1)
                    gates_2(j)

                def chunks(ap):
                    return ap.rearrange("p (c t) -> p c t", t=P)

                def end_of(j):
                    return chunks(c_b[:, j])[:, :, P - 1:P] if j < 2 else chunks(c_b[:, j])[:, :, 0:1]

                def to_end(j):
                    dve.wait_ge(s["b_ready"], nth("hg", l, 3))
                    if j >= 2:
                        dve.wait_ge(*full("C", l, "kd", j - 2))
                    w = chunks(c_w[:, j % 2, 0])
                    say("el_args", dve.tensor_tensor(w, end_of(j).broadcast_to([P, NT, P]), chunks(c_b[:, j]),
                                                     ALU.subtract))
                    dve.wait_ge(s["el_ready"], nth("hg", l, j))
                    say("kd_ready", dve.tensor_tensor(c_w[:, j % 2, 0], c_w[:, j % 2, 0], c_k[:, j], ALU.mult))

                def states(j):
                    order = [8, 9] + list(range(8)) if j < 2 else list(range(9, -1, -1))
                    dve.wait_ge(s["state_zeroed"], l + 1)
                    dve.wait_ge(*full("C", l, "D", j))
                    for now, then in zip(order[:-1], order[1:]):
                        for par in range(2):
                            head = slice(HD * par, HD * par + HD)
                            ins = dve.scalar_tensor_tensor(
                                out=c_state[head, j, then, head], in0=c_state[head, j, now, head],
                                scalar=c_el[head, j, now:now + 1],
                                in1=slot("C", l, "D", j)[head, P * now + HD * par:P * now + HD * par + HD],
                                op0=ALU.mult, op1=ALU.add)
                            if (then, par) == (order[-1], 1):
                                token = release(ins, "C", l, "D", j)
                            elif par:
                                step(ins)
                            else:
                                also(ins)
                    dve.wait_ge(*token)
                    dve.sem_inc(s["states_ready"], 1)

                for j in range(5):
                    if j < 4:
                        to_end(j)
                    if j >= 1:
                        states(j - 1)

                dve.wait_ge(s["late_used"], n_late(l))
                modulation(l, 2 * KT, MODS, 0)
                if l < DEPTH - 1:
                    modulation(l + 1, 0, 2 * KT, 2 * (MODS - 2 * KT))
                levels = [(lev, tile) for lev in range(len(LEVELS) + 1) for tile in range(2)]

                def level_args(n):
                    lev, tile = levels[n]
                    if n >= 4:
                        dve.wait_ge(*full("C", l, "att", lev - 2, tile, len(CHUNK_GROUPS) - 1))
                    elif n >= 2:
                        dve.wait_ge(s["late_used"], n_late(l))
                    else:
                        for j in (2, 3):
                            dve.wait_ge(*full("C", l, "D", j))
                    if lev == len(LEVELS):
                        return
                    h = LEVELS[lev]
                    bf1, bf2 = blocks_of(c_b[:, tile], h)
                    bb1, bb2 = blocks_of(c_b[:, 2 + tile], h)
                    q1, q2 = blocks_of(c_lq(n), h)
                    shape = [P, T // (2 * h), h]
                    mid_f = bf1[:, :, h - 1:h].broadcast_to(shape)
                    mid_b = bb2[:, :, 0:1].broadcast_to(shape)
                    also(dve.tensor_tensor(q2, bf2, mid_f, ALU.subtract))
                    say("lev_q_args", dve.tensor_tensor(q1, bb1, mid_b, ALU.subtract))

                def level_operands(n):
                    lev, tile = levels[n]
                    if lev == len(LEVELS):
                        return
                    dve.wait_ge(s["lev_q_exps"], nth("levx", l, lev, tile))
                    say("lev_q_ready", dve.tensor_tensor(c_lq(n), c_lq(n), c_q[:, tile], ALU.mult))

                def level_masked(n):
                    lev, tile = levels[n]
                    for q, (c0, cn) in enumerate(CHUNK_GROUPS):
                        key = ("C", l, "att", lev, tile, q)
                        dve.wait_ge(*full(*key))
                        if lev:
                            dve.wait_ge(*freed("C", l, "att", lev - 1, tile, q))
                        src = slot(*key)[:, 0:1024].rearrange("p (h c t) -> p h c t", h=2, t=P)[:, :, 0:cn, :]
                        dst = c_att[:, c0:c0 + cn, 2 * tile:2 * tile + 2, :].rearrange("p c h t -> p h c t")
                        mask = masks[:, lev, :].unsqueeze(1).unsqueeze(1).broadcast_to([P, 2, cn, P])
                        release(dve.copy_predicated(out=dst, mask=mask, data=src), *key)

                for n in range(len(levels) + 2):
                    if n < len(levels):
                        level_args(n)
                    if 1 <= n <= len(levels):
                        level_operands(n - 1)
                    if n >= 2:
                        level_masked(n - 2)
                for j in (0, 2):
                    dve.wait_ge(s["inter_exps"], nth("hg", l, j))
                    say("inter_ready", dve.tensor_tensor(c_b[:, j], c_b[:, j], c_q[:, j % 2], ALU.mult))
                dve.wait_ge(s["c_g_ready"], l + 1)

                def read_out(i):
                    n = nth("chunk", l, i)
                    key = ("C", l, "out", i)
                    dve.wait_ge(*full(*key))
                    dve.wait_ge(s["c_o_half"], n)
                    own_part = slot(*key)[:, 0:4 * P].rearrange("p (t q v) -> p t q v", q=4, v=HD)[:, :, ::3, :]
                    dst = c_o[:, n % 2].rearrange("p (t a v) -> p t a v", a=2, v=HD)
                    dve.wait_ge(*release(dve.tensor_tensor(dst, own_part, dst, ALU.add), *key))
                    step(dve.tensor_tensor(c_o2[:, n % 2], c_o[:, n % 2], c_o[:, n % 2], ALU.mult))
                    say("ms_ready", dve.tensor_reduce(c_ms[:, 0, i, :], c_o2[:, n % 2].rearrange(
                        "p (h v) -> p h v", v=HD), AX, ALU.add))
                    dve.wait_ge(s["ms_ready"], n)

                def gate_out(i):
                    n = nth("chunk", l, i)
                    dve.wait_ge(s["hg_rstd"], n)
                    say("c_o_used", dve.tensor_tensor(
                        c_o2[:, n % 2].rearrange("p (h v) -> p h v", v=HD), c_o[:, n % 2].rearrange(
                            "p (h v) -> p h v", v=HD),
                        c_ms[:, 1, i, :].unsqueeze(2).broadcast_to([P, 4, HD]), ALU.mult))
                    dve.wait_ge(s["c_o_used"], n)
                    return also(dve.tensor_tensor(o_tok[:, i, D - 2 * P:D], c_o2[:, n % 2], c_g[:, i, :], ALU.mult))

                nq = q_tiles(l)
                for i in range(nq + 1):
                    if i < nq:
                        read_out(i)
                    if i >= 1:
                        last = gate_out(i - 1)
                        dve.wait_ge(*last)
                return last

            def phase_o(l):
                for i in range(q_tiles(l)):
                    dve.wait_ge(s["o_hi_ready"], nth("osplit", l, i))
                    t = slice(P * i, P * i + P)
                    last = release(dve.tensor_tensor(
                        h_lo[:, :, t], slot("O", l, i)[:, 0:D].rearrange("p (k n) -> p k n", n=P),
                        h_hi[:, :, t].bitcast(F32), ALU.subtract), "O", l, i)
                return last

            def phase_post(l, which):
                nq = q_tiles(l)
                after = next_h(l, which)

                def post(i):
                    return nth("post", l, which, i)

                for i in range(nq + 5):
                    if after and 3 <= i <= nq + 2:
                        n = post(i - 3)
                        normed_for_pe(n_x1[:, (n - 1) % 2], (*after, i - 3))
                    if i < nq:
                        n = post(i)
                        key = ("y", l, which, i)
                        dve.wait_ge(s[f"x_landed{(n - 1) % 2}"], 16 * ((n - 1) // 2 + 1))
                        dve.wait_ge(*full(*key))
                        if n > 2:
                            dve.wait_ge(s["r_ready"], n - 2)
                        dve.wait_ge(*release(dve.scalar_tensor_tensor(
                            out=n_r[:, n % 2], in0=n_xt[:, (n - 1) % 2], scalar=ALPHA, in1=slot(*key)[:, 0:D],
                            op0=ALU.mult, op1=ALU.add), *key))
                        moments(n_r[:, n % 2], key)
                    if 1 <= i <= nq:
                        n = post(i - 1)
                        if n > 2:
                            dve.wait_ge(s[f"x1_stored{(n - 1) % 2}"], 16 * ((n - 1) // 2))
                        if after and i >= 3:
                            dve.wait_ge(s["xh_ready"], nth("xh", *after, i - 3))
                        say("r_ready", normed(n_x1[:, (n - 1) % 2], n_r[:, n % 2], ("y", l, which, i - 1)))
                    if after and 2 <= i <= nq + 1:
                        n = post(i - 2)
                        dve.wait_ge(s["x1_ready"], n)
                        moments(n_x1[:, (n - 1) % 2], (*after, i - 2))
                    if after and i >= 5:
                        split((*after, i - 5))
                for k in range(2):
                    n = sum(1 for m in range(post(nq - 1)) if m % 2 == k)
                    dve.wait_ge(s[f"x1_stored{k}"], 16 * n)
                if after:
                    return s["h_ready"], nth("xh", *after, nq - 1)
                return s["x1_ready"], post(nq - 1)

            def phase_f(l):
                ctx_too = q_tiles(l) == NT

                def conv(f, half):
                    key = ("F", l, f, half)
                    w = f_t[:, half]
                    acc = slot(*key)
                    dve.wait_ge(s["conv_start"], nth("conv", l, f, half))
                    parts = [(0, LAT)] + [(LAT, T)] * ctx_too
                    for j in (0, 2):
                        at_col = 224 * l + MODS + 2 * FT * j + FT * half + f
                        for a, b in parts:
                            dst, src = (w[:, a + 1:b], acc[:, a:b - 1]) if j == 0 else (w[:, a:b - 1], acc[:, a + 1:b])
                            ins = dve.scalar_tensor_tensor(out=dst, in0=src, scalar=vec[:, at_col:at_col + 1], in1=dst,
                                                           op0=ALU.mult, op1=ALU.add)
                            if (j, b) == (2, parts[-1][1]):
                                dve.wait_ge(*release(ins, *key))
                            elif b == parts[-1][1]:
                                step(ins)
                            else:
                                also(ins)

                w = T if ctx_too else LAT

                def gated(f):
                    dve.wait_ge(s["silu_done"], nth("ff", l, f))
                    say("a_whole", dve.tensor_tensor(f_t[:, 0, 0:w], f_t[:, 0, 0:w], f_t[:, 1, 0:w], ALU.mult))

                def low_half(f):
                    dve.wait_ge(s["a_hi_ready"], nth("ff", l, f))
                    hi, lo = f_hi[:, f // 2 % 2, f % 2, 0:w], f_lo[:, f // 2 % 2, f % 2, 0:w]
                    say("a_ready", dve.tensor_tensor(lo, f_t[:, 0, 0:w], hi.bitcast(F32), ALU.subtract))

                def add_up(i, m):
                    key = ("Y", l, i, m)
                    dve.wait_ge(*full(*key))
                    if i:
                        dve.wait_ge(*freed("Y", l, i - 1, m))
                    for a, b, who in [(0, LAT, 0)] + [(LAT, T, 1)] * ctx_too:
                        gate = mods[:, l, KT * 5 + m, who:who + 1]
                        if i == 0:
                            ins = dve.tensor_scalar(y_chan[:, m, a:b], slot(*key)[:, a:b], gate, None, ALU.mult)
                        else:
                            ins = dve.scalar_tensor_tensor(out=y_chan[:, m, a:b], in0=slot(*key)[:, a:b], scalar=gate,
                                                           in1=y_chan[:, m, a:b], op0=ALU.mult, op1=ALU.add)
                        if b == w:
                            return release(ins, *key)
                        also(ins)

                for i in range(NPAIR + 1):
                    if i < NPAIR:
                        f = 2 * i
                        conv(f, 0)
                        conv(f, 1)
                        gated(f)
                        if i >= 2:
                            dve.wait_ge(*full("Y", l, i - 2, KT - 1))
                        low_half(f)
                        conv(f + 1, 0)
                        conv(f + 1, 1)
                        gated(f + 1)
                    for m in range(KT):
                        if i:
                            last = add_up(i - 1, m)
                        if m == 0 and i < NPAIR:
                            low_half(f + 1)
                return last

            for l in range(DEPTH):
                for r in range(3):
                    end_phase(dve, phase_a(l, r), "A", l, r)
                end_phase(dve, phase_b(l), "B", l)
                end_phase(dve, phase_c(l), "C", l)
                end_phase(dve, phase_o(l), "O", l)
                end_phase(dve, phase_post(l, 0), "post", l, 0)
                end_phase(dve, phase_f(l), "F", l)
                end_phase(dve, phase_post(l, 1), "post", l, 1)

        @block.scalar
        def _(act):
            own = Signal(s["act_step"])

            def step(ins):
                token = own.on(ins)
                act.wait_ge(*token)
                return token

            def release(ins, *key):
                ins.then_inc(s[f"freed{plan.use[key] % 2}"], 1)
                return freed(*key)

            def say(name, ins):
                ins.then_inc(s[name], 1)

            def copy(dst, src, scale=1.0):
                return act.activation(dst, src, ACT.Copy, scale=scale)

            act.wait_ge(s["rows_turned"], 1)
            say("cond_ready", act.activation(cond[:], psum[:, 6, 456:472].rearrange("p (a k) -> p k a", a=2), ACT.Silu))
            act.preload_act_table_set(LN_EXP_SET)
            act.wait_ge(s["lb_shifted"], 2)
            say("lb_exps", act.activation(lb[:, 0], lb[:, 0], ACT.Exp))
            act.wait_ge(s["lb_args"], 1)
            step(act.activation(lb[:, 1], lb[:, 1], ACT.Ln, scale=float(2 ** LN_SHIFT)))
            say("lb_logs", act.activation(lb[:, 2], lb[:, 2], ACT.Ln))

            def rstd_of(key):
                n = nth("stat", *key)
                w, i = (n - 1) // NT % 2, (n - 1) % NT
                act.wait_ge(s["mean_ready"], n)
                r = rstd[:, w, i:i + 1]
                step(act.activation(r, mv[:, w, i, 1:2], ACT.Ln, bias=EPS))
                say("rstd_ready", act.activation(r, r, ACT.Exp, scale=-0.5))

            def modulated(key):
                n = nth("xh", *key)
                i = key[-1]
                l, first = (key[1], 3 * KT) if key[0] == "h2" else (key[1], 0)
                who = 0 if i < NTL else 1
                act.wait_ge(*full(*key))
                if n > 2:
                    act.wait_ge(s["h_ready"], n - 2)
                for k in range(KT):
                    ins = act.activation(n_t[:, n % 2, k], slot(*key)[:, P * k:P * k + P], ACT.Identity,
                                         bias=mods[:, l, first + k, who:who + 1],
                                         scale=mods[:, l, first + KT + k, who:who + 1])
                    if k < KT - 1:
                        own.on(ins)
                    else:
                        act.wait_ge(*release(ins, *key))
                act.wait_ge(s["act_step"], own.n)
                say("h_hi_ready", copy(h_hi[:, :, P * i:P * i + P], n_t[:, n % 2]))
                return s["h_hi_ready"], n

            for i in range(NT + 2):
                if i < NT:
                    rstd_of(("h", 0, i))
                if i == 2:
                    act.wait_ge(s["mods_ready"], 1)
                if i >= 2:
                    last = modulated(("h", 0, i - 2))
            end_phase(act, last, "h0")

            def attend(units, key_of, probs, turned):
                for u in range(len(units) + 1):
                    if u < len(units):
                        probs(u)
                    if u >= 1:
                        n = nth("unit", *key_of(u - 1))
                        act.wait_ge(*full(*key_of(u - 1), "turned"))
                        if n > 2:
                            act.wait_ge(s["out_ready"], n - 2)
                        last = turned(u - 1)
                return last

            def phase_a(l, r):
                key = ("A", l, r, "q")
                w = P * q_tiles(l)
                act.wait_ge(*full(*key))
                own.on(copy(a_q[0:HD, 0, 0:w], slot(*key)[0:HD, 0:w], QSCALE))
                release(copy(a_q[HD:P, 1, 0:w], slot(*key)[HD:P, 0:w], QSCALE), *key)
                for name, dst in (("k", a_k), ("v", a_vt)):
                    key = ("A", l, r, name)
                    act.wait_ge(*full(*key))
                    release(copy(dst[:], slot(*key)[:, 0:T]), *key)
                key = ("A", l, r, "vt")
                act.wait_ge(*full(*key))
                release(copy(a_v[:].rearrange("p c v -> p (c v)"), slot(*key)[:, 0:T]), *key)
                units = [(hh, p) for hh in range(2) for p in range(q_tiles(l))]

                def key_of(u):
                    return ("A", l, r, u)

                def probs(u):
                    hh, p = units[u]
                    n = nth("unit", *key_of(u))
                    c_ = n % 64
                    act.wait_ge(s["negmax_ready"], n)
                    w = CTX + (GRID_W * ROW_PAIRS[p][1] if p < NTL else 0)
                    say("probs_ready", act.activation(a_p[:, n % 2, 0:w], a_p[:, n % 2, 0:w], ACT.Exp,
                                                      bias=stats[:, 1, c_:c_ + 1], accum_out=stats[:, 2, c_:c_ + 1]))

                def turned(u):
                    hh, p = units[u]
                    key = key_of(u)
                    n = nth("unit", *key)
                    dst = a_pt[:, n % 2].rearrange("p b t -> p (b t)")
                    key = (*key, "turned")
                    acc = slot(*key)
                    if p >= NTL:
                        return release(copy(dst[:, 512:768], acc[:, 512:768]), *key)
                    if ROW_PAIRS[p][1] > WIN_R:
                        own.on(copy(dst[0:64, 768:896], acc[0:64, 768:896]))
                    return release(copy(dst[:, 0:768], acc[:, 0:768]), *key)
                return attend(units, key_of, probs, turned)

            def phase_b(l):
                def part(name):
                    return {"k": b_k[:], "v": b_vt[:]}.get(name) if name in "kv" else b_q[:, int(name[1])]

                def width(name):
                    return T if name in "kv" else P * q_tiles(l)

                def take(name):
                    key = ("B", l, name)
                    w = width(name)
                    act.wait_ge(*full(*key))
                    release(copy(part(name)[:, 0:w], slot(*key)[:, 0:w]), *key)
                    if name != "v":
                        act.wait_ge(*freed(*key))

                def square(name):
                    k = B_NORMED.index(name)
                    w = width(name)
                    if k >= 2:
                        act.wait_ge(s["rope_ready"], nth("bn", l, B_NORMED[k - 2]))
                    say("sq_ready", act.activation(b_tmp[k % 2][:, 0:w], part(name)[:, 0:w], ACT.Square))

                def head_rstd(name):
                    w = width(name)
                    tmp = b_tmp[B_NORMED.index(name) % 2]
                    key = ("B", l, name, "ms")
                    act.wait_ge(*full(*key))
                    act.wait_ge(*release(act.activation(tmp[:, 0:w], slot(*key)[:, 0:w], ACT.Ln, bias=EPS), *key))
                    say("act_headrstd", act.activation(tmp[:, 0:w], tmp[:, 0:w], ACT.Exp, scale=-0.5))

                take("k")
                square("k")
                take("q0")
                square("q0")
                head_rstd("k")
                take("q1")
                square("q1")
                head_rstd("q0")
                take("q2")
                square("q2")
                head_rstd("q1")
                take("v")
                head_rstd("q2")
                key = ("B", l, "v", "turn")
                act.wait_ge(*full(*key))
                release(copy(b_v[:].rearrange("p c v -> p (c v)"), slot(*key)[:, 0:T]), *key)
                key = ("B", l, "k", "swap")
                act.wait_ge(*full(*key))
                act.wait_ge(s["rope_ready"], nth("bn", l, B_NORMED[-1]))
                own.on(copy(b_kz[HD:P, 0, 1], slot(*key)[HD:P, 0:T]))
                act.wait_ge(*release(copy(b_kz[0:HD, 1, 0], slot(*key)[0:HD, 0:T]), *key))
                act.sem_inc(s["kz_ready"], 2)
                units = [(h, i) for h in range(6) for i in range(q_tiles(l))]

                def key_of(u):
                    return ("B", l, u)

                def blocks(u):
                    return slice(0 if units[u][1] < NTL else NTL, NT)

                def probs(u):
                    n = nth("unit", *key_of(u))
                    c_ = n % 64
                    act.wait_ge(s["negmax_ready"], n)
                    p = b_p(n)[:, blocks(u), :]
                    say("probs_ready", act.activation(p, p, ACT.Exp, bias=stats[:, 1, c_:c_ + 1],
                                                      accum_out=stats[:, 2, c_:c_ + 1]))

                def turned(u):
                    n = nth("unit", *key_of(u))
                    key = (*key_of(u), "turned")
                    src = slot(*key)[:, 0:T].rearrange("p (b n) -> p b n", n=P)
                    return release(copy(b_pt[:, n % 2, blocks(u), :], src[:, blocks(u), :]), *key)
                return attend(units, key_of, probs, turned)

            def phase_c(l):
                for name, _ in C_PARTS:
                    j = int(name[1])
                    key = ("C", l, name)
                    dst = {"i": lambda: c_z[:, 2 + j], "g": lambda: c_z[:, 2 + j], "f": lambda: c_z[:, j],
                           "b": lambda: c_z[:, 2 + j], "q": lambda: c_q[:, j]}[name[0]]()
                    act.wait_ge(*full(*key))
                    release(copy(dst, slot(*key)[:, 0:T], QSCALE if name[0] == "q" else 1.0), *key)
                    if name in C_TURNED:
                        key = ("C", l, name, "t")
                        act.wait_ge(*full(*key))
                        to = (c_v if name[0] == "i" else c_g)[:, :, P * j:P * j + P]
                        src = slot(*key)[:, 0:T].rearrange("p (c v) -> p c v", v=P)
                        release(copy(to, src) if name[0] == "i" else act.activation(to, src, ACT.Silu), *key)
                act.preload_act_table_set(LN_EXP_SET)
                for name in ("q0", "q1"):
                    act.wait_ge(*freed("C", l, name))

                def gates_1(j):
                    w = c_w[:, j % 2]
                    if j >= 2:
                        act.wait_ge(s["b_ready"], nth("hg", l, j - 2))
                    step(act.activation(w[:, 0], c_z[:, j], ACT.Abs))
                    step(act.activation(w[:, 0], w[:, 0], ACT.Exp, scale=-1.0))
                    say("gate_l", act.activation(w[:, 0], w[:, 0], ACT.Ln, bias=1.0))

                def gates_2(j):
                    w = c_w[:, j % 2]
                    c_ = slice(4 * l + j, 4 * l + j + 1)
                    act.wait_ge(s["gate_m"], nth("hg", l, j))
                    own.on(act.activation(c_k[:, j], w[:, 2], ACT.Exp, scale=-1.0, bias=lb[:, 2, c_]))
                    step(act.activation(w[:, 3], w[:, 1], ACT.Abs, bias=lb[:, 3, c_]))
                    step(act.activation(w[:, 3], w[:, 3], ACT.Exp, scale=-1.0))
                    say("gate_k", act.activation(w[:, 3], w[:, 3], ACT.Ln, bias=1.0))

                gates_1(0)
                for j in range(4):
                    if j < 3:
                        gates_1(j + 1)
                    gates_2(j)

                def decays(j):
                    act.wait_ge(s["el_args"], nth("hg", l, j))
                    b = c_b[:, j].rearrange("p (c t) -> p c t", t=P)
                    own.on(act.activation(c_el[:, j, :], b[:, :, P - 1] if j < 2 else b[:, :, 0], ACT.Exp))
                    say("el_ready", act.activation(c_w[:, j % 2, 0], c_w[:, j % 2, 0], ACT.Exp))

                def turned(j):
                    act.wait_ge(*full("C", l, "kd", j))
                    if j >= 2:
                        act.wait_ge(*full("C", l, "D", j - 2))
                    release(copy(c_w[:, j % 2, 1], slot("C", l, "kd", j)[:, 0:T]), "C", l, "kd", j)

                for j in range(5):
                    if j < 4:
                        decays(j)
                    if j >= 1:
                        turned(j - 1)
                for lev in range(len(LEVELS)):
                    for tile in range(2):
                        act.wait_ge(s["lev_k_args"], nth("levx", l, lev, tile))
                        say("lev_k_exps", act.activation(c_lk(2 * lev + tile), c_lk(2 * lev + tile), ACT.Exp))
                        act.wait_ge(s["lev_q_args"], nth("levx", l, lev, tile))
                        say("lev_q_exps", act.activation(c_lq(2 * lev + tile), c_lq(2 * lev + tile), ACT.Exp))
                for j in range(4):
                    say("inter_exps", act.activation(c_b[:, j], c_b[:, j], ACT.Exp))
                def take_states_part(i):
                    n = nth("chunk", l, i)
                    act.wait_ge(*full("C", l, "out", i))
                    if n > 2:
                        act.wait_ge(s["c_o_used"], n - 2)
                    say("c_o_half", copy(c_o[:, n % 2], slot("C", l, "out", i)[:, 512:512 + 2 * P]))

                take_states_part(0)
                for i in range(q_tiles(l)):
                    if i + 1 < q_tiles(l):
                        take_states_part(i + 1)
                    n = nth("chunk", l, i)
                    act.wait_ge(s["ms_ready"], n)
                    step(act.activation(c_ms[:, 1, i, :], c_ms[:, 0, i, :], ACT.Ln, scale=1.0 / HD, bias=EPS))
                    say("hg_rstd", act.activation(c_ms[:, 1, i, :], c_ms[:, 1, i, :], ACT.Exp, scale=-0.5))
                return s["hg_rstd"], nth("chunk", l, q_tiles(l) - 1)

            def phase_o(l):
                for i in range(q_tiles(l)):
                    act.wait_ge(*full("O", l, i))
                    say("o_hi_ready", copy(h_hi[:, :, P * i:P * i + P],
                                           slot("O", l, i)[:, 0:D].rearrange("p (k n) -> p k n", n=P)))
                for m in range(KT):
                    key = ("W", l, m)
                    act.wait_ge(*full(*key))
                    if q_tiles(l) == NT:
                        own.on(act.activation(y_chan[:, m, LAT:T], slot(*key)[:, LAT:T], ACT.Copy,
                                              scale=mods[:, l, 2 * KT + m, 1:2]))
                    last = release(act.activation(y_chan[:, m, 0:LAT], slot(*key)[:, 0:LAT], ACT.Copy,
                                                  scale=mods[:, l, 2 * KT + m, 0:1]), *key)
                return last

            def phase_post(l, which):
                after = next_h(l, which)
                last = None
                nq = q_tiles(l)
                for i in range(nq + 3):
                    if i < nq:
                        rstd_of(("y", l, which, i))
                    if after and 2 <= i <= nq + 1:
                        rstd_of((*after, i - 2))
                    if after and i >= 3:
                        last = modulated((*after, i - 3))
                return last or (s["rstd_ready"], nth("stat", "y", l, which, nq - 1))

            def phase_f(l):
                w = T if q_tiles(l) == NT else LAT
                for f in range(FT):
                    for half in range(2):
                        key = ("F", l, f, half)
                        act.wait_ge(*full(*key))
                        if f:
                            act.wait_ge(s["a_ready"], nth("ff", l, f - 1))
                        mid, shift = [224 * l + MODS + 2 * FT * j + FT * half + f for j in (1, 3)]
                        say("conv_start", act.activation(f_t[:, half, 0:w], slot(*key)[:, 0:w], ACT.Identity,
                                                         scale=vec[:, mid:mid + 1], bias=vec[:, shift:shift + 1]))
                        if half == 0:
                            act.wait_ge(*freed(*key))
                            say("silu_done", act.activation(f_t[:, 0, 0:w], f_t[:, 0, 0:w], ACT.Silu))
                    act.wait_ge(s["a_whole"], nth("ff", l, f))
                    if f >= 4 and f % 2 == 0:
                        act.wait_ge(*full("Y", l, f // 2 - 2, KT - 1))
                    say("a_hi_ready", copy(f_hi[:, f // 2 % 2, f % 2, 0:w], f_t[:, 0, 0:w]))
                act.preload_act_table_set(LN_EXP_SET)
                return s["silu_done"], nth("ff", l, FT - 1)

            for l in range(DEPTH):
                for r in range(3):
                    end_phase(act, phase_a(l, r), "A", l, r)
                end_phase(act, phase_b(l), "B", l)
                end_phase(act, phase_c(l), "C", l)
                end_phase(act, phase_o(l), "O", l)
                end_phase(act, phase_post(l, 0), "post", l, 0)
                end_phase(act, phase_f(l), "F", l)
                end_phase(act, phase_post(l, 1), "post", l, 1)


_INS = ["x", "c", "ctx", "c_ctx", "w_ada", "b_ada", "w_in", "w_out", "na_rpb", "q_norm", "k_norm", "hg_lower_bound",
        "hg_norm", "ln1_g", "ln1_b", "w_up", "conv_w", "conv_b", "w_down", "ln2_g", "ln2_b"]


def shape_constants():
    import numpy as np

    lane = np.arange(P)
    eye = np.eye(P, dtype=np.float32)
    rotate = eye[lane ^ 16]
    swap = eye[lane ^ 64]
    flip = eye[lane ^ 63]
    means = ((lane[:, None] // HD == lane[None] // HD) / HD).astype(np.float32)
    masks = np.zeros((P, len(LEVELS) + 1, P), np.float32)
    for n, h in enumerate(LEVELS):
        same = lane[:, None] // (2 * h) == lane[None] // (2 * h)
        masks[:, n] = same & (lane[:, None] // h != lane[None] // h)
    masks[:, len(LEVELS)] = np.eye(P)
    n_freq = HD // 4
    inv_freq = np.float32(10000.0) ** (-np.arange(n_freq, dtype=np.float32) / np.float32(n_freq))
    t = np.arange(LAT)
    pos = np.stack([t // GRID_W, t % GRID_W]).astype(np.float32)
    axis, half, freq = lane % HD // 32, lane % 32 // 16, lane % 16
    angle = (pos[axis] * inv_freq[freq][:, None]).astype(np.float32)
    sign = np.where(half == 0, -1.0, 1.0).astype(np.float32)[:, None]
    window = np.full((P, GRID_W), NEVER, np.float32)
    for w in range(64):
        first = min(max(w - WIN_C // 2, 0), GRID_W - WIN_C)
        window[[w, GRID_W + w], first:first + WIN_C] = 0.0
    return dict(identity=eye, reverse_columns=flip, rotate_halves=rotate, swap_heads=swap, head_means=means,
                level_masks=masks,
                rope_cos=np.cos(angle), rope_sin=np.sin(angle) * sign, window_mask=window)


def kernel(**inputs):
    import numpy as np
    import concourse.bacc as bacc
    from concourse.bass_utils import run_bass_kernel_spmd

    nc = bacc.Bacc("TRN2", target_bir_lowering=False, num_devices=1)
    arrays, args = {}, {}
    for name, value in [(n, inputs[n]) for n in _INS] + list(shape_constants().items()):
        a = np.ascontiguousarray(value)
        arrays[f"in_{name}_dram"] = a
        args[name] = nc.dram_tensor(f"in_{name}_dram", a.shape, mybir.dt.from_np(a.dtype), kind="ExternalInput").ap()
    out = nc.dram_tensor("out_0_dram", (1, LAT, D), F32, kind="ExternalOutput").ap()
    build(nc, **args, out=out)
    r = run_bass_kernel_spmd(nc, [arrays], core_ids=[0])
    return r.results[0]["out_0_dram"]
```
